# Optimizing a Trainium2 kernel written in Bass

```python
import math
import jax, jax.numpy as jnp
from jax import lax
import numpy as np

D_MODEL = 1024
BATCH = 1
SEQ = 2048
DEPTH = 1

GRID_W = 64
CTX_LEN = 256

D_BRANCH = D_MODEL // 2
N_BRANCH = 3
D_LRU = D_BRANCH
N_LRU_BLOCKS = 8
LRU_BLOCK = D_LRU // N_LRU_BLOCKS
LRU_CONV = 4
LRU_C = 8.0
D_NA = D_BRANCH
NA_HEAD_DIM = 64
NA_HEADS = D_NA // NA_HEAD_DIM
NA_KH = 8
NA_KW = 16
D_HY = D_BRANCH
HY_CONV = 3
HY_POS_BANDS = 16
HY_EMB = 1 + 2 * HY_POS_BANDS
HY_HID = 64
HY_DECAY_TARGET = 1e-2
HY_FAST_DECAY = 0.3
HY_SLOW_DECAY = 1.5

ALPHA = (2 * DEPTH) ** 0.25
BETA = (8 * DEPTH) ** -0.25
LN_EPS = 1e-5

IN_WIDTHS = (D_LRU, D_LRU, D_NA, D_NA, D_NA, D_NA, 3 * D_HY, D_HY, D_MODEL, D_MODEL, D_MODEL)
D_IN = sum(IN_WIDTHS)
IN_SPLITS = tuple(int(s) for s in np.cumsum(IN_WIDTHS)[:-1])

kernel_name = "hybrid_rglru_natten_hyena_diffusion_trunk"

def layer_norm(x, g=None, b=None):
    xf = x.astype(jnp.float32)
    mu = jnp.mean(xf, -1, keepdims=True)
    var = jnp.mean(jnp.square(xf - mu), -1, keepdims=True)
    y = (xf - mu) * lax.rsqrt(var + LN_EPS)
    if g is not None:
        y = y * g.astype(jnp.float32) + b.astype(jnp.float32)
    return y.astype(x.dtype)

def dwconv_centred(x, w, b):
    k_w, ch = w.shape
    left = k_w // 2
    y = lax.conv_general_dilated(
        x, w[:, None, :].astype(x.dtype), window_strides=(1,), padding=[(left, k_w - 1 - left)],
        dimension_numbers=('NWC', 'WIO', 'NWC'), feature_group_count=ch)
    return y + b

def rglru_coeffs(x, w_a, b_a, w_x, b_x, lam):
    bsz, length, _ = x.shape
    xh = x.reshape(bsz, length, N_LRU_BLOCKS, LRU_BLOCK)
    r = jax.nn.sigmoid(jnp.einsum('blgi,gij->blgj', xh, w_a).reshape(bsz, length, D_LRU) + b_a)
    i = jax.nn.sigmoid(jnp.einsum('blgi,gij->blgj', xh, w_x).reshape(bsz, length, D_LRU) + b_x)
    log_a = -LRU_C * r.astype(jnp.float32) * jax.nn.softplus(-lam.astype(jnp.float32))
    a = jnp.exp(log_a)
    b = jnp.sqrt(-jnp.expm1(2.0 * log_a)) * (i * x).astype(jnp.float32)
    return a, b

def linear_scan(a, b, h0):
    b = b.at[:, 0].add(a[:, 0] * h0)

    def combine(p, q):
        a1, b1 = p
        a2, b2 = q
        return a1 * a2, a2 * b1 + b2

    _, h = lax.associative_scan(combine, (a, b), axis=1)
    return h

def rglru_bidir(x_ctx, x_lat, w_a, b_a, w_x, b_x, lam):
    y_ctx = jnp.zeros(x_ctx.shape, jnp.float32)
    y_lat = jnp.zeros(x_lat.shape, jnp.float32)
    for d in range(2):
        xc = x_ctx if d == 0 else jnp.flip(x_ctx, 1)
        xl = x_lat if d == 0 else jnp.flip(x_lat, 1)
        ac, bc = rglru_coeffs(xc, w_a[d], b_a[d], w_x[d], b_x[d], lam[d])
        hc = linear_scan(ac, bc, jnp.zeros_like(bc[:, 0]))
        al, bl = rglru_coeffs(xl, w_a[d], b_a[d], w_x[d], b_x[d], lam[d])
        hl = linear_scan(al, bl, hc[:, -1])
        if d == 1:
            hc = jnp.flip(hc, 1)
            hl = jnp.flip(hl, 1)
        y_ctx = y_ctx + hc
        y_lat = y_lat + hl
    return y_ctx.astype(x_ctx.dtype), y_lat.astype(x_lat.dtype)

def neighbourhood_attention(q, k, v, k_ctx, v_ctx, rpb):
    bsz, length, heads, dh = q.shape
    rows = length // GRID_W
    kh = min(NA_KH, rows)
    kw = NA_KW
    kg = k.reshape(bsz, rows, GRID_W, heads, dh)
    vg = v.reshape(bsz, rows, GRID_W, heads, dh)
    qg = (q * dh ** -0.5).reshape(bsz, rows, GRID_W, heads, dh).transpose(1, 0, 2, 3, 4)
    cols = jnp.arange(GRID_W)
    col_start = jnp.clip(cols - kw // 2, 0, GRID_W - kw)
    col_ok = (cols[None, :] >= col_start[:, None]) & (cols[None, :] < col_start[:, None] + kw)
    dc_idx = jnp.clip(cols[None, :] - cols[:, None], -(kw - 1), kw - 1) + (NA_KW - 1)
    n_loc = kh * GRID_W

    def one_row(args):
        r, q_row = args
        r0 = jnp.clip(r - kh // 2, 0, rows - kh)
        k_band = lax.dynamic_slice_in_dim(kg, r0, kh, axis=1)
        v_band = lax.dynamic_slice_in_dim(vg, r0, kh, axis=1)
        dr_idx = r0 + jnp.arange(kh) - r + (NA_KH - 1)
        bias = rpb[:, dr_idx[None, :, None], dc_idx[:, None, :]].astype(jnp.float32)
        bias = jnp.where(col_ok[None, :, None, :], bias, -jnp.inf)
        s_loc = jnp.einsum('bqhd,brkhd->bhqrk', q_row, k_band).astype(jnp.float32) + bias
        s_ctx = jnp.einsum('bqhd,bchd->bhqc', q_row, k_ctx).astype(jnp.float32)
        s = jnp.concatenate([s_loc.reshape(bsz, heads, GRID_W, n_loc), s_ctx], -1)
        p = jax.nn.softmax(s, axis=-1).astype(v.dtype)
        p_loc = p[..., :n_loc].reshape(bsz, heads, GRID_W, kh, GRID_W)
        p_ctx = p[..., n_loc:]
        return (jnp.einsum('bhqrk,brkhd->bqhd', p_loc, v_band)
                + jnp.einsum('bhqc,bchd->bqhd', p_ctx, v_ctx))

    out = lax.map(one_row, (jnp.arange(rows), qg))
    return out.transpose(1, 0, 2, 3, 4).reshape(bsz, length, heads * dh)

def context_attention(q, k, v):
    s = jnp.einsum('bqhd,bkhd->bhqk', q * NA_HEAD_DIM ** -0.5, k).astype(jnp.float32)
    p = jax.nn.softmax(s, axis=-1).astype(v.dtype)
    o = jnp.einsum('bhqk,bkhd->bqhd', p, v)
    return o.reshape(o.shape[0], o.shape[1], -1)

def hyena_filters(length, w1, b1, freq1, w2, b2, freq2, w3):
    f32 = jnp.float32
    t = jnp.arange(length, dtype=f32) / length
    ang = 2.0 * math.pi * t[:, None] * jnp.arange(1, HY_POS_BANDS + 1, dtype=f32)
    z = jnp.concatenate([t[:, None], jnp.cos(ang), jnp.sin(ang)], -1)
    hid = jnp.sin(freq1.astype(f32) * (z @ w1.astype(f32) + b1.astype(f32)))
    hid = jnp.sin(freq2.astype(f32) * (hid @ w2.astype(f32) + b2.astype(f32)))
    filt = (hid @ w3.astype(f32)).reshape(length, 2, D_HY)
    deltas = jnp.abs(jnp.linspace(math.log(HY_DECAY_TARGET) / HY_FAST_DECAY,
                                  math.log(HY_DECAY_TARGET) / HY_SLOW_DECAY, D_HY, dtype=f32))
    filt = filt * jnp.exp(-t[:, None] * deltas)[:, None, :]
    return filt[:, 0], filt[:, 1]

def long_conv_bidir(u, h_fwd, h_bwd):
    length = u.shape[1]
    kern = jnp.concatenate([h_fwd, jnp.zeros_like(h_fwd[:1]), jnp.flip(h_bwd[1:], 0)], 0)
    u_f = jnp.fft.rfft(u.astype(jnp.float32), n=2 * length, axis=1)
    k_f = jnp.fft.rfft(kern, n=2 * length, axis=0)
    return jnp.fft.irfft(u_f * k_f[None], n=2 * length, axis=1)[:, :length]

def hyena_mix(z, conv_w, conv_b, h_fwd, h_bwd, d_skip):
    z = dwconv_centred(z, conv_w, conv_b)
    x0, x1, v = jnp.split(z, 3, axis=-1)
    w = x1 * v
    y = long_conv_bidir(w, h_fwd, h_bwd).astype(w.dtype) + d_skip * w
    return x0 * y

def merge_branches(ya, yb, yc, a_gate, b_gate, c_gate, g_a, g_b, g_c, w_branch_out, w_out):
    m = (jax.nn.sigmoid(g_a) * ((ya * jax.nn.silu(a_gate)) @ w_branch_out[0])
         + jax.nn.sigmoid(g_b) * ((yb * jax.nn.silu(b_gate)) @ w_branch_out[1])
         + jax.nn.sigmoid(g_c) * ((yc * jax.nn.silu(c_gate)) @ w_branch_out[2]))
    return m @ w_out

def _heads(t):
    return t.reshape(t.shape[0], t.shape[1], NA_HEADS, NA_HEAD_DIM)

def setup_inputs(seed: int = 0) -> dict:
    key = jax.random.key(seed)
    ks = iter(jax.random.split(key, 40))
    f32 = jnp.float32

    def nrm(shape, s):
        return jax.random.normal(next(ks), shape, f32) * s

    a_c = jax.random.uniform(next(ks), (DEPTH, 2, D_LRU), f32, 0.9, 0.999)
    a0 = a_c ** (1.0 / LRU_C)
    lru_lambda = jnp.log(a0) - jnp.log1p(-a0)
    return {
        "x": nrm((BATCH, SEQ, D_MODEL), 1.0),
        "c": nrm((BATCH, D_MODEL), 1.0),
        "ctx": nrm((BATCH, CTX_LEN, D_MODEL), 1.0),
        "c_ctx": nrm((D_MODEL,), 1.0),
        "w_mod": nrm((DEPTH, D_MODEL, 3 * D_MODEL), 0.5 * D_MODEL ** -0.5),
        "b_mod": nrm((DEPTH, 3 * D_MODEL), 0.02),
        "w_in": nrm((DEPTH, D_MODEL, D_IN), D_MODEL ** -0.5),
        "lru_conv_w": nrm((DEPTH, LRU_CONV, D_LRU), LRU_CONV ** -0.5),
        "lru_conv_b": nrm((DEPTH, D_LRU), 0.02),
        "lru_w_a": nrm((DEPTH, 2, N_LRU_BLOCKS, LRU_BLOCK, LRU_BLOCK), LRU_BLOCK ** -0.5),
        "lru_b_a": nrm((DEPTH, 2, D_LRU), 0.02),
        "lru_w_x": nrm((DEPTH, 2, N_LRU_BLOCKS, LRU_BLOCK, LRU_BLOCK), LRU_BLOCK ** -0.5),
        "lru_b_x": nrm((DEPTH, 2, D_LRU), 0.02),
        "lru_lambda": lru_lambda,
        "na_rpb": nrm((DEPTH, NA_HEADS, 2 * NA_KH - 1, 2 * NA_KW - 1), 0.1),
        "hy_conv_w": nrm((DEPTH, HY_CONV, 3 * D_HY), HY_CONV ** -0.5),
        "hy_conv_b": nrm((DEPTH, 3 * D_HY), 0.02),
        "hy_w1": nrm((DEPTH, HY_EMB, HY_HID), HY_EMB ** -0.5),
        "hy_b1": nrm((DEPTH, HY_HID), 0.02),
        "hy_freq1": 1.0 + nrm((DEPTH, HY_HID), 0.02),
        "hy_w2": nrm((DEPTH, HY_HID, HY_HID), HY_HID ** -0.5),
        "hy_b2": nrm((DEPTH, HY_HID), 0.02),
        "hy_freq2": 1.0 + nrm((DEPTH, HY_HID), 0.02),
        "hy_w3": nrm((DEPTH, HY_HID, 2 * D_HY), 0.05 * HY_HID ** -0.5),
        "hy_d_skip": nrm((DEPTH, D_HY), 1.0),
        "w_branch_out": nrm((DEPTH, N_BRANCH, D_BRANCH, D_MODEL), BETA * D_BRANCH ** -0.5),
        "w_out": nrm((DEPTH, D_MODEL, D_MODEL), BETA * D_MODEL ** -0.5),
        "ln_g": 1.0 + nrm((DEPTH, D_MODEL), 0.02),
        "ln_b": nrm((DEPTH, D_MODEL), 0.02),
    }

def reference(x, c, ctx, c_ctx, w_mod, b_mod, w_in, lru_conv_w, lru_conv_b, lru_w_a, lru_b_a,
              lru_w_x, lru_b_x, lru_lambda, na_rpb, hy_conv_w, hy_conv_b, hy_w1, hy_b1, hy_freq1,
              hy_w2, hy_b2, hy_freq2, hy_w3, hy_d_skip, w_branch_out, w_out, ln_g, ln_b):
    h, hc = x, ctx
    seq_len = x.shape[1]
    ctx_len = ctx.shape[1]
    for l in range(DEPTH):
        last = l == DEPTH - 1
        mod = jax.nn.silu(c) @ w_mod[l] + b_mod[l]
        mod_x = jax.nn.silu(c_ctx) @ w_mod[l] + b_mod[l]
        shift, scale, gate = jnp.split(mod[:, None, :], 3, axis=-1)
        shift_x, scale_x, gate_x = jnp.split(mod_x, 3)
        u = layer_norm(h) * (1.0 + scale) + shift
        ux = layer_norm(hc) * (1.0 + scale_x) + shift_x

        (a_in, a_gate, q, k, v, b_gate, c_in, c_gate, g_a, g_b, g_c) = jnp.split(u @ w_in[l], IN_SPLITS, axis=-1)
        (a_in_x, a_gate_x, q_x, k_x, v_x, b_gate_x, c_in_x, c_gate_x, g_a_x, g_b_x, g_c_x) = jnp.split(
            ux @ w_in[l], IN_SPLITS, axis=-1)

        xa = dwconv_centred(a_in, lru_conv_w[l], lru_conv_b[l])
        xa_x = dwconv_centred(a_in_x, lru_conv_w[l], lru_conv_b[l])
        ya_x, ya = rglru_bidir(xa_x, xa, lru_w_a[l], lru_b_a[l], lru_w_x[l], lru_b_x[l], lru_lambda[l])

        kh_x, vh_x = _heads(k_x), _heads(v_x)
        yb = neighbourhood_attention(_heads(q), _heads(k), _heads(v), kh_x, vh_x, na_rpb[l])

        hf, hb = hyena_filters(seq_len, hy_w1[l], hy_b1[l], hy_freq1[l], hy_w2[l], hy_b2[l], hy_freq2[l], hy_w3[l])
        yc = hyena_mix(c_in, hy_conv_w[l], hy_conv_b[l], hf, hb, hy_d_skip[l])

        out = merge_branches(ya, yb, yc, a_gate, b_gate, c_gate, g_a, g_b, g_c, w_branch_out[l], w_out[l])
        h_new = layer_norm(ALPHA * h + gate * out, ln_g[l], ln_b[l])

        if not last:
            yb_x = context_attention(_heads(q_x), kh_x, vh_x)
            hf_x, hb_x = hyena_filters(ctx_len, hy_w1[l], hy_b1[l], hy_freq1[l], hy_w2[l], hy_b2[l],
                                       hy_freq2[l], hy_w3[l])
            yc_x = hyena_mix(c_in_x, hy_conv_w[l], hy_conv_b[l], hf_x, hb_x, hy_d_skip[l])
            out_x = merge_branches(ya_x, yb_x, yc_x, a_gate_x, b_gate_x, c_gate_x, g_a_x, g_b_x, g_c_x,
                                   w_branch_out[l], w_out[l])
            hc = layer_norm(ALPHA * hc + gate_x * out_x, ln_g[l], ln_b[l])
        h = h_new
    return h


_drawn_inputs = setup_inputs


def setup_inputs(seed=0):
    import zlib

    import numpy as np

    out = dict(_drawn_inputs(seed))
    spreads = {}
    factors = {'ctx': 186.219,
     'c_ctx': 4.472,
     'b_mod': 4.821,
     'lru_conv_b': 6.961,
     'lru_w_a': 4.34,
     'lru_b_a': 200.0,
     'lru_b_x': 64.0,
     'na_rpb': 64.0,
     'hy_conv_b': 8.0,
     'hy_w1': 2.886,
     'hy_b1': 8.0,
     'hy_freq1': 8.0,
     'hy_w2': 2.795,
     'hy_b2': 8.0,
     'hy_freq2': 23.6,
     'hy_w3': 2.947,
     'ln_g': 30.456,
     'ln_b': 26.706}
    for name, (base, spread) in spreads.items():
        noise = np.random.default_rng([zlib.crc32(name.encode()), seed]).standard_normal(out[name].shape)
        drawn = base * np.exp(spread * noise) if base else spread * noise
        out[name] = __import__('jax').numpy.asarray(drawn.astype(out[name].dtype))
    for name, factor in factors.items():
        out[name] = (out[name] * factor).astype(out[name].dtype)
    return out
```

```python
import math
from contextlib import ExitStack

import numpy as np

import concourse.bass as bass
from concourse import mybir

F32 = mybir.dt.float32
ALU = mybir.AluOpType
ACT = mybir.ActivationFunctionType
AX_X = mybir.AxisListType.X

P = 128
D = 1024
KD = D // P
L = 2048
LC = 256
LT = LC + L
CH = 512
NB = 512 // P
GW = 64
ROWS = L // GW
NKH, NKW = 8, 16
BAND = NKH * GW
HEADS = 8
DH = 64
NDR = 2 * NKH - 1
TOE = 2 * GW - 1
NF = 2 * L
R1 = 64
NPR = R1 // 2
EMB = 33
HID = 64
ALPHA = 2.0 ** 0.25
EPS = 1e-5
MASKED = -1e30
LAT_CHUNKS = [(LC + CH * i, CH) for i in range(L // CH)]
ALL_CHUNKS = [(0, LC)] + LAT_CHUNKS
B_AIN, B_AGATE, B_Q, B_K, B_V, B_BGATE, B_X0, B_X1, B_HV, B_CGATE, B_G = 0, 4, 8, 12, 16, 20, 24, 28, 32, 36, 40


def shape_constants():
    f = {}
    n1 = np.arange(R1)
    kk = np.arange(R1)
    k1, ri = kk % 32, kk // 32
    ang = 2 * np.pi * np.outer(n1, k1) / R1
    one = np.where(ri == 0, np.cos(ang), -np.sin(ang))
    one[:, 0] = 1.0
    one[:, 32] = (-1.0) ** n1
    lat = np.kron(np.eye(2), one[:32])
    f["dft1"] = np.concatenate([lat, lat], 0)
    f["dft1_filter"] = np.kron(np.eye(2), one[np.where(n1 < 32, n1, 95 - n1)])
    inv = np.where(ri == 0, 2 * np.cos(ang), -2 * np.sin(ang))
    inv[:, 0] = 1.0
    inv[:, 32] = (-1.0) ** n1
    f["idft1"] = np.kron(np.eye(2), inv[:32].T) / NF
    n2 = 2 * (np.arange(64) % 32) + np.arange(64) // 32
    k2 = np.arange(64)
    fwd = np.zeros((32, 128, 128))
    inv2 = np.zeros((32, 128, 128))
    for k in range(1, 32):
        th = 2 * np.pi * np.outer(n2, k + 64 * k2) / NF
        c, s = np.cos(th), np.sin(th)
        fwd[k] = np.block([[c, -s], [s, c]])
        inv2[k] = np.block([[c.T, s.T], [-s.T, c.T]])
    h = np.arange(32)
    t0 = 2 * np.pi * np.outer(n2, 64 * h) / NF
    t1 = 2 * np.pi * np.outer(n2, 32 + 64 * h) / NF
    fwd[0, :64, :32], fwd[0, :64, 64:96] = np.cos(t0), -np.sin(t0)
    fwd[0, 64:, 32:64], fwd[0, 64:, 96:] = np.cos(t1), -np.sin(t1)
    fwd[0, :64, 64] = (-1.0) ** n2
    inv2[0, :32, :64], inv2[0, 64:96, :64] = 2 * np.cos(t0).T, -2 * np.sin(t0).T
    inv2[0, 32:64, 64:], inv2[0, 96:, 64:] = 2 * np.cos(t1).T, -2 * np.sin(t1).T
    inv2[0, 0, :64] = 1.0
    inv2[0, 64, :64] = (-1.0) ** n2
    f["dft2"] = fwd.transpose(1, 0, 2)
    swapped = np.concatenate([inv2[:, 64:], inv2[:, :64]], 1)
    f["idft2"] = np.concatenate([inv2, swapped], 2).transpose(1, 0, 2)
    kb = np.concatenate([fwd[:, :, :64], fwd[:, :, :64]], 2)
    kb[0, :, 64] = fwd[0, :, 64]
    kc = np.concatenate([fwd[:, :, 64:], -fwd[:, :, 64:]], 2)
    kc[0, :, 0] = 0
    kc[0, :, 64] = 0
    f["dft2_filter"] = np.concatenate([kb, kc], 2)
    t = np.arange(L) / np.float32(L)
    a = 2 * np.pi * t[:, None] * np.arange(1, 17)
    f["positions"] = np.concatenate([t[:, None], np.cos(a), np.sin(a)], 1).T
    tt = np.zeros((32, 2, 64))
    for pr in range(32):
        for j in range(2):
            tt[pr, j, :32] = 64 * np.arange(32) + 2 * pr + j
            tt[pr, j, 32:] = 64 * (np.arange(32) + 1) - (2 * pr + j)
    f["neg_time"] = -(tt / L).reshape(32, 128).T
    f["deltas"] = np.abs(np.linspace(math.log(1e-2) / 0.3, math.log(1e-2) / 1.5, 512))[None]
    cols = np.arange(GW)
    start = np.clip(cols - NKW // 2, 0, GW - NKW)
    ok = (cols[None] >= start[:, None]) & (cols[None] < start[:, None] + NKW)
    m = np.where(ok, 0.0, MASKED)
    f["col_mask"] = np.concatenate([m, m], 0)
    f["ident"] = np.eye(P)
    f["flip"] = np.kron(np.eye(2), np.eye(GW)[::-1])
    return {k: np.ascontiguousarray(v, np.float32) for k, v in f.items()}


class Steps:

    def __init__(self, eng, sem, base=0):
        self.eng, self.sem, self.base, self.n = eng, sem, base, 0

    def __call__(self, ins):
        ins.then_inc(self.sem, 1)
        self.n += 1
        self.eng.wait_ge(self.sem, self.base + self.n)


def build_trunk(nc, a, out, debug=False):
    scratch = "ExternalOutput" if debug else "Internal"

    def dram(name, shape):
        return nc.dram_tensor(name, shape, F32, kind=scratch).ap()

    bias_tab = dram("bias_tab", (NB, P, NDR * GW))
    filt_mid = dram("filt_mid", (2, NPR, R1, 512))
    filt_spec = dram("filt_spec", (NPR, 2, P, 512))
    fwd_mid = dram("fwd_mid", (NB, P, NPR, P))
    inv_mid = dram("inv_mid", (NB, P, NPR, P))
    yg_dram = dram("yg_dram", (3 * NB, P, L))
    m_dram = dram("m_dram", (L // P, P, KD, P))
    if debug:
        ut_dbg = dram("ut_dbg", (P, KD, LT))
    names = [0]

    def free_name(n):
        names[0] += 1
        return f"{n}_{names[0]}"

    top = ExitStack()

    def sb(ctx, name, shape):
        return ctx.enter_context(nc.sbuf_tensor(free_name(name), shape, F32))

    def ps(ctx, name, shape):
        return ctx.enter_context(nc.psum_tensor(free_name(name), shape, F32))

    def sem(name):
        return top.enter_context(nc.semaphore(name))

    with top:
        ident = sb(top, "ident", [P, P])
        mod = sb(top, "mod", [P, 24, 2])
        decay = sb(top, "decay", [P, 2 * NB, 2])
        gate_row = sb(top, "gate_row", [P, D])

        with ExitStack() as cx:
            cvec = sb(cx, "cvec", [P, KD, 2])
            bmod = sb(cx, "bmod", [P, 24, 2])
            wm = sb(cx, "wm", [P, 2, D])
            lam = sb(cx, "lam", [P, 2 * NB])
            sp = sb(cx, "sp", [P, 6, 2 * NB])
            toe = sb(cx, "toe", [P, NB, NDR, GW])
            mask = sb(cx, "mask", [P, GW])
            spread = sb(cx, "spread", [P, KD, P])
            ones = sb(cx, "ones", [P, P])
            pm = ps(cx, "pm", [P, 2, CH])
            pg = ps(cx, "pg", [P, 2, CH])
            flip = sb(cx, "flip", [P, P])
            pt = ps(cx, "pt", [P, 4, CH])
            TG = 6
            flip_mm = sem("flip_mm")
            small_in, wm_in, toe_in = sem("small_in"), [sem("wm_in0"), sem("wm_in1")], sem("toe_in")
            c_ready, mod_mm, mod_done = sem("c_ready"), sem("mod_mm"), sem("mod_done")
            dv, exp_lam, y_exp, toe_done, bias_out = sem("mod_dv"), sem("exp_lam"), sem("y_exp"), sem("toe_done"), sem("bias_out")
            spread_done, row_mm, abs_lam = sem("spread_done"), sem("row_mm"), sem("abs_lam")
            with nc.Block() as block:
                @block.sync
                def _(sp_):
                    sp_.dma_start(cvec[:, :, :], a["cvec"]).then_inc(small_in, 16)
                    sp_.dma_start(bmod[:, :, :], a["bmod"]).then_inc(small_in, 16)
                    sp_.dma_start(lam[:, :], a["lam"]).then_inc(small_in, 16)
                    sp_.dma_start(ident[:, :], a["ident"]).then_inc(small_in, 16)
                    sp_.dma_start(mask[:, :], a["col_mask"]).then_inc(small_in, 16)
                    sp_.dma_start(flip[:, :], a["flip"]).then_inc(small_in, 16)
                    with sp_.Fori(0, 12) as i:
                        for s in range(2):
                            sp_.wait_ge(mod_mm, 2 * i + s + 1)
                            sp_.dma_start(wm[:, s, :], a["w_mod"][2 * i + s]).then_inc(wm_in[s], 16)
                    sp_.wait_ge(toe_done, NB * NDR // TG)
                    for p in range(NB):
                        sp_.dma_start(bias_tab[p], toe[:, p, :, :]).then_inc(bias_out, 16)
                    sp_.wait_ge(bias_out, 16 * NB)

                @block.gpsimd
                def _(pool):
                    for h in range(HEADS):
                        src = bass.AP(tensor=a["rpb"].tensor, offset=h * NDR * TOE,
                                      ap=[[1, GW], [TOE, NDR], [1, GW]])
                        pool.dma_start(toe[GW * (h % 2):GW * (h % 2) + GW, h // 2, :, :], src).then_inc(toe_in, 16)
                    pool.wait_ge(toe_in, 16 * HEADS)

                @block.scalar
                def _(act):
                    act.wait_ge(small_in, 96)
                    nc.scalar.activation(cvec[:, :, :], cvec[:, :, :], ACT.Silu).then_inc(c_ready, 1)
                    act.wait_ge(abs_lam, 1)
                    nc.scalar.activation(sp[:, 1, :], sp[:, 0, :], ACT.Exp, scale=-1.0).then_inc(y_exp, 1)

                @block.tensor
                def _(pe):
                    pe.nop().then_inc(mod_mm, 2)
                    pe.wait_ge(c_ready, 1)
                    with pe.Fori(0, 12) as i:
                        for s in range(2):
                            pe.wait_ge(wm_in[s], 16 * i + 16)
                            if s == 0:
                                pe.wait_ge(mod_done, i + 1)
                            for k in range(KD):
                                mm = pe.matmul(pm[:, s, 0:2], wm[:, s, k * P:(k + 1) * P], cvec[:, k, :],
                                               start=(k == 0), stop=(k == KD - 1))
                            mm.then_inc(mod_mm, 1)
                    pe.wait_ge(spread_done, 1)
                    for k in range(KD):
                        mm = pe.matmul(pg[:, k // 4, (k % 4) * P:(k % 4 + 1) * P], spread[:, k, :], ident[:, :],
                                       start=True, stop=True)
                    mm.then_inc(row_mm, 1)
                    pe.wait_ge(toe_in, 16 * HEADS)
                    for n in range(NB * NDR // TG):
                        if n >= 4:
                            pe.wait_ge(toe_done, n - 3)
                        pe.matmul(pt[:, n % 4, 0:TG * GW], flip[:, :], toe[:, :, :, :].rearrange("p a b c -> p (a b c)")[:, n * TG * GW:(n + 1) * TG * GW],
                                  start=True, stop=True).then_inc(flip_mm, 1)

                @block.vector
                def _(dve):
                    st = Steps(dve, dv)
                    v = nc.vector
                    dve.nop().then_inc(mod_done, 1)
                    v.memset(ones[:, :], 1.0).then_inc(dv, 1)
                    st.n += 1
                    dve.wait_ge(small_in, 96)
                    st(v.tensor_scalar(sp[:, 2, :], lam[:, :], -1.0, None, ALU.mult))
                    v.tensor_tensor(sp[:, 0, :], lam[:, :], sp[:, 2, :], ALU.max).then_inc(abs_lam, 1)
                    dve.wait_ge(y_exp, 1)
                    st(v.tensor_scalar(sp[:, 3, :], sp[:, 1, :], 2.0, None, ALU.add))
                    st(v.reciprocal(sp[:, 4, :], sp[:, 3, :]))
                    st(v.tensor_tensor(sp[:, 0, :], sp[:, 4, :], sp[:, 1, :], ALU.mult))
                    st(v.tensor_tensor(sp[:, 4, :], sp[:, 0, :], sp[:, 0, :], ALU.mult))
                    st(v.tensor_scalar(sp[:, 5, :], sp[:, 4, :], 1.0 / 17, 1.0 / 15, ALU.mult, ALU.add))
                    for n in (13, 11, 9, 7, 5, 3, 1):
                        st(v.tensor_tensor(sp[:, 5, :], sp[:, 5, :], sp[:, 4, :], ALU.mult))
                        st(v.tensor_scalar(sp[:, 5, :], sp[:, 5, :], 1.0 / n, None, ALU.add))
                    st(v.tensor_tensor(sp[:, 5, :], sp[:, 5, :], sp[:, 0, :], ALU.mult))
                    st(v.tensor_scalar(sp[:, 2, :], sp[:, 2, :], 0.0, None, ALU.max))
                    st(v.scalar_tensor_tensor(sp[:, 3, :], sp[:, 5, :], 2.0, sp[:, 2, :], ALU.mult, ALU.add))
                    st(v.tensor_scalar(decay[:, :, 0], sp[:, 3, :], -8.0, None, ALU.mult))
                    st(v.tensor_scalar(decay[:, :, 1], sp[:, 3, :], 8.0, None, ALU.mult))
                    with dve.Fori(0, 12) as i:
                        for s in range(2):
                            dve.wait_ge(mod_mm, 2 * i + s + 3)
                            ins = v.tensor_tensor(mod[:, bass.ds(2 * i + s, 1), :], pm[:, s, 0:2].rearrange("p (o c) -> p o c", o=1),
                                                  bmod[:, bass.ds(2 * i + s, 1), :], ALU.add)
                        ins.then_inc(mod_done, 1)
                    dve.wait_ge(mod_done, 13)
                    st(v.tensor_scalar(mod[:, 8:16, :], mod[:, 8:16, :], 1.0, None, ALU.add))
                    for k in range(KD):
                        ins = v.tensor_scalar(spread[:, k, :], ones[:, :], mod[:, 16 + k, 0:1], None, ALU.mult)
                    ins.then_inc(spread_done, 1)
                    dve.wait_ge(row_mm, 1)
                    st(v.tensor_copy(gate_row[:, :].rearrange("p (a b) -> p a b", a=2), pg[:, :, :]))
                    rows = toe[:, :, :, :].rearrange("p a b c -> p (a b) c")
                    for n in range(NB * NDR // TG):
                        dve.wait_ge(flip_mm, n + 1)
                        v.tensor_tensor(rows[:, n * TG:(n + 1) * TG, :], pt[:, n % 4, 0:TG * GW].rearrange("p (a b) -> p a b", b=GW),
                                        mask[:, :].unsqueeze(1).to_broadcast([P, TG, GW]), ALU.add).then_inc(toe_done, 1)

        with ExitStack() as cx:
            pos = sb(cx, "pos", [EMB, L])
            w1 = sb(cx, "w1", [EMB, 2 * HID])
            w2 = sb(cx, "w2", [HID, 2 * HID])
            w3 = sb(cx, "w3", [P, 512])
            bf = sb(cx, "bf", [P, 4])
            arg = sb(cx, "arg", [P, L])
            turns = sb(cx, "turns", [P, L])
            hid1 = sb(cx, "hid1", [P, L])
            hid = sb(cx, "hid", [P, R1, R1])
            negt = sb(cx, "negt", [P, NPR])
            deltas = sb(cx, "deltas", [P, 512])
            d1f = sb(cx, "d1f", [P, P])
            window = sb(cx, "window", [P, 2, 512])
            filt = sb(cx, "filt", [P, 2, 512])
            mid = sb(cx, "mid", [P, 2, 512])
            mid2 = sb(cx, "mid2", [P, 2, 512])
            d2f = sb(cx, "d2f", [P, 2, 256])
            spec = sb(cx, "spec", [P, 2, 2, 512])
            hpair = sb(cx, "hpair", [P, 2, P])
            ph = ps(cx, "ph", [P, 4, CH])
            pq = ps(cx, "pq", [P, 4, CH])
            f_in, hid_mm, hid_dv, sin_done, hid_zero = sem("f_in"), sem("hid_mm"), sem("hid_dv"), sem("sin_done"), sem("hid_zero")
            hpair_done, win_done, gen_mm, filt_done, mid_mm, mid_done = [sem(n) for n in (
                "hpair_done", "win_done", "gen_mm", "filt_done", "mid_mm", "mid_done")]
            mid_out = [sem("mid_out0"), sem("mid_out1")]
            mid_in = [sem("mid_in0"), sem("mid_in1")]
            spec_mm, spec_b_done, spec_c_done = sem("spec_mm"), sem("spec_b_done"), sem("spec_c_done")
            spec_out = [sem("spec_out0"), sem("spec_out1")]
            MAGIC = 1.5 * 2.0 ** 23
            TWO_PI = 2 * math.pi
            c1 = 6.28125
            c2 = float(np.round((TWO_PI - c1) * 2 ** 21) / 2 ** 21)
            c3 = float(TWO_PI - c1 - c2)
            with nc.Block() as block:
                @block.sync
                def _(sp_):
                    for dst, name in ((pos, "positions"), (w1, "hy_w1"), (w2, "hy_w2"), (w3, "hy_w3"), (bf, "hy_bf"),
                                      (negt, "neg_time"), (d1f, "dft1_filter")):
                        sp_.dma_start(dst[:, :], a[name]).then_inc(f_in, 16)
                    sp_.dma_start(deltas[:, :], bass.AP(tensor=a["deltas"].tensor, offset=0,
                                                        ap=[[0, P], [1, 512]])).then_inc(f_in, 16)
                    dst = filt_mid.rearrange("r k (j q) c -> q j (r k) c", j=2)
                    with sp_.Fori(0, NPR // 2) as i:
                        for s in range(2):
                            sp_.wait_ge(mid_done, 2 * i + s + 3)
                            for j in range(2):
                                sp_.dma_start(dst[2 * i + s, j], mid[R1 * j:R1 * (j + 1), s, :]).then_inc(mid_out[s], 16)
                    for s in range(2):
                        sp_.wait_ge(mid_out[s], 32 * (NPR // 2) + 32)
                    with sp_.Fori(0, NPR // 2) as i:
                        for s in range(2):
                            sp_.wait_ge(spec_mm, 2 * i + s + 1)
                            for r in range(2):
                                sp_.dma_start(mid2[R1 * r:R1 * r + R1, s, :], filt_mid[r, 2 * i + s]).then_inc(mid_in[s], 16)
                            sp_.dma_start(d2f[:, s, :], a["dft2_filter"][2 * i + s]).then_inc(mid_in[s], 16)

                @block.scalar
                def _(act):
                    act.nop().then_inc(mid_done, 2)
                    act.nop().then_inc(spec_c_done, 2)
                    act.wait_ge(hid_dv, 28)
                    nc.scalar.activation(hid1[:, :], arg[:, :], ACT.Sin).then_inc(sin_done, 1)
                    act.wait_ge(hid_dv, 56)
                    act.wait_ge(hid_zero, 1)
                    lo = arg[0:HID, :].rearrange("p (a b) -> p b a", b=R1)
                    nc.scalar.activation(hid[0:HID, :, 0:32], lo, ACT.Sin).then_inc(sin_done, 1)
                    hi = arg[HID:P, :].rearrange("p (a b) -> p b a", b=R1)
                    nc.scalar.activation(hid[HID:P, 1:R1, 32:R1], hi[:, R1 - 1:0:-1, :], ACT.Sin).then_inc(sin_done, 1)
                    nc.scalar.activation(hid[HID:P, 0, 32:R1 - 1], hi[:, 0, 1:32], ACT.Sin).then_inc(sin_done, 1)
                    act.wait_ge(f_in, 128)
                    with act.Fori(0, NPR // 2) as i:
                        for s in range(2):
                            act.wait_ge(filt_done, 2 * i + s + 1)
                            nc.scalar.activation(window[:, s, :], deltas[:, :], ACT.Exp,
                                                 scale=negt[:, bass.ds(2 * i + s, 1)]).then_inc(win_done, 1)
                        for s in range(2):
                            act.wait_ge(mid_mm, 2 * i + s + 3)
                            act.wait_ge(mid_out[s], 32 * i + 32)
                            nc.scalar.copy(mid[:, s, :], pq[:, 2 + s, :]).then_inc(mid_done, 1)
                    with act.Fori(0, NPR // 2) as i:
                        for s in range(2):
                            act.wait_ge(spec_mm, 2 * i + s + 3)
                            act.wait_ge(spec_out[s], 16 * i + 16)
                            nc.scalar.copy(spec[:, s, 1, :], pq[:, 2 * s + 1, :]).then_inc(spec_c_done, 1)
                            act.wait_ge(spec_b_done, 2 * i + s + 3)
                            act.wait_ge(spec_c_done, 2 * i + s + 3)
                            act.dma_start(filt_spec[2 * i + s].rearrange("b p c -> p b c"), spec[:, s, :, :]).then_inc(spec_out[s], 16)
                    for s in range(2):
                        act.wait_ge(spec_out[s], 8 * NPR + 16)

                @block.gpsimd
                def _(pool):
                    for s in range(2):
                        pool.nop().then_inc(mid_out[s], 32)
                        pool.nop().then_inc(spec_out[s], 16)
                    nc.gpsimd.memset(hid[:, :, :], 0.0).then_inc(hid_zero, 1)
                    pool.wait_ge(sin_done, 4)
                    pairs = hid[:, :, :].rearrange("p (r j) s -> p r (j s)", j=2)
                    with pool.Fori(0, NPR // 2) as i:
                        for s in range(2):
                            pool.wait_ge(gen_mm, 2 * i + s + 1)
                            nc.gpsimd.tensor_copy(hpair[:, s, :].unsqueeze(1), pairs[:, bass.ds(2 * i + s, 1), :]).then_inc(hpair_done, 1)

                @block.tensor
                def _(pe):
                    pe.nop().then_inc(gen_mm, 2)
                    pe.nop().then_inc(mid_mm, 2)
                    pe.nop().then_inc(spec_mm, 2)
                    pe.wait_ge(f_in, 128)
                    for c in range(4):
                        mm = pe.matmul(ph[:, c, :], w1[:, :], pos[:, c * CH:(c + 1) * CH], start=True, stop=True)
                    mm.then_inc(hid_mm, 1)
                    pe.wait_ge(sin_done, 1)
                    for c in range(4):
                        mm = pe.matmul(pq[:, c, :], w2[:, :], hid1[0:HID, c * CH:(c + 1) * CH], start=True, stop=True)
                    mm.then_inc(hid_mm, 1)
                    pe.wait_ge(hid_dv, 56)
                    with pe.Fori(0, NPR // 2) as i:
                        for s in range(2):
                            pe.wait_ge(hpair_done, 2 * i + s + 1)
                            pe.wait_ge(filt_done, 2 * i + s + 1)
                            pe.matmul(ph[:, s, :], hpair[:, s, :], w3[:, :], start=True, stop=True).then_inc(gen_mm, 1)
                        for s in range(2):
                            pe.wait_ge(filt_done, 2 * i + s + 3)
                            pe.wait_ge(mid_done, 2 * i + s + 1)
                            pe.matmul(pq[:, 2 + s, :], d1f[:, :], filt[:, s, :], start=True, stop=True).then_inc(mid_mm, 1)
                    pe.wait_ge(mid_done, NPR + 2)
                    with pe.Fori(0, NPR // 2) as i:
                        for s in range(2):
                            pe.wait_ge(mid_in[s], 48 * i + 48)
                            pe.wait_ge(spec_b_done, 2 * i + s + 1)
                            pe.wait_ge(spec_c_done, 2 * i + s + 1)
                            pe.matmul(pq[:, 2 * s, :], d2f[:, s, 0:P], mid2[:, s, :], start=True, stop=True)
                            pe.matmul(pq[:, 2 * s + 1, :], d2f[:, s, P:2 * P], mid2[:, s, :], start=True, stop=True).then_inc(spec_mm, 1)

                @block.vector
                def _(dve):
                    v = nc.vector
                    dve.nop().then_inc(filt_done, 2)
                    dve.nop().then_inc(spec_b_done, 2)
                    st = Steps(dve, hid_dv)
                    dve.wait_ge(f_in, 128)
                    for layer in range(2):
                        dve.wait_ge(hid_mm, layer + 1)
                        src = (ph, pq)[layer]
                        if layer:
                            dve.wait_ge(sin_done, 1)
                        for c in range(4):
                            x, n = arg[:, c * CH:(c + 1) * CH], turns[:, c * CH:(c + 1) * CH]
                            st(v.tensor_scalar(x, src[:, c, :], bf[:, 2 * layer:2 * layer + 1],
                                               bf[:, 2 * layer + 1:2 * layer + 2], ALU.add, ALU.mult))
                            st(v.tensor_scalar(n, x, 1 / TWO_PI, MAGIC, ALU.mult, ALU.add))
                            st(v.tensor_scalar(n, n, -MAGIC, None, ALU.add))
                            for part in (c1, c2, c3):
                                st(v.scalar_tensor_tensor(x, n, -part, x, ALU.mult, ALU.add))
                            st(v.tensor_scalar(x, x, 3.1415925, -3.1415925, ALU.min, ALU.max))
                    with dve.Fori(0, NPR // 2) as i:
                        for s in range(2):
                            dve.wait_ge(gen_mm, 2 * i + s + 3)
                            dve.wait_ge(win_done, 2 * i + s + 1)
                            dve.wait_ge(mid_mm, 2 * i + s + 1)
                            v.tensor_tensor(filt[:, s, :], ph[:, s, :], window[:, s, :], ALU.mult).then_inc(filt_done, 1)
                    with dve.Fori(0, NPR // 2) as i:
                        for s in range(2):
                            dve.wait_ge(spec_mm, 2 * i + s + 3)
                            dve.wait_ge(spec_out[s], 16 * i + 16)
                            v.tensor_copy(spec[:, s, 0, :], pq[:, 2 * s, :]).then_inc(spec_b_done, 1)

        main = ExitStack()
        with main:
            ut = sb(main, "ut", [P, KD, LT])

            with ExitStack() as cx:
                xin = sb(cx, "xin", [P, 2, D])
                xn = sb(cx, "xn", [P, 2, D])
                stat = sb(cx, "stat", [P, 2, 18])
                pt = ps(cx, "pt", [P, 2, 2, CH])
                x_in = [sem("x_in0"), sem("x_in1")]
                norm_dv, var_done, std_done, xn_done, turn_mm, ut_act, ut_dve = [sem(n) for n in (
                    "norm_dv", "var_done", "std_done", "xn_done", "turn_mm", "ut_act", "ut_dve")]
                NV = 5
                with nc.Block() as block:
                    @block.sync
                    def _(sp_):
                        for s in range(2):
                            sp_.dma_start(xin[:, s, :], a["ctx"][s * P:(s + 1) * P]).then_inc(x_in[s], 16)
                        with sp_.Fori(0, L // P // 2) as i:
                            for s in range(2):
                                sp_.wait_ge(xn_done, 2 * i + s + 1)
                                sp_.dma_start(xin[:, s, :], a["x"].rearrange("(n p) d -> n p d", p=P)[2 * i + s]).then_inc(x_in[s], 16)

                    def normalise(dve, n, s, t16):
                        v, b = nc.vector, n * NV
                        x, q = xin[:, s, :], stat[:, s, :]
                        dve.wait_ge(x_in[s], t16)
                        v.bn_stats(q[:, 0:6], x[:, 0:512]).then_inc(norm_dv, 1)
                        v.bn_stats(q[:, 6:12], x[:, 512:1024]).then_inc(norm_dv, 1)
                        dve.wait_ge(norm_dv, b + 2)
                        dve.nop(nofuse=True)
                        v.bn_aggr(q[:, 12:14], q[:, 0:12]).then_inc(norm_dv, 1)
                        dve.wait_ge(norm_dv, b + 3)
                        v.tensor_scalar(q[:, 14:15], q[:, 13:14], EPS, None, ALU.add).then_inc(var_done, 1)
                        dve.wait_ge(std_done, n + 1)
                        v.reciprocal(q[:, 16:17], q[:, 15:16]).then_inc(norm_dv, 1)
                        dve.wait_ge(turn_mm, n + 1)
                        dve.wait_ge(norm_dv, b + 4)
                        v.tensor_scalar(xn[:, s, :], x, q[:, 12:13], q[:, 16:17], ALU.subtract, ALU.mult).then_inc(xn_done, 1)
                        dve.wait_ge(xn_done, n + 1)
                        dve.nop().then_inc(norm_dv, 1)

                    def modulate(eng, n, s, which, col, half, done):
                        eng.wait_ge(turn_mm, n + 3)
                        for k in range(4 * half, 4 * half + 4):
                            src = pt[:, s, half, (k % 4) * P:(k % 4 + 1) * P]
                            dst = ut[:, k, col]
                            scale, shift = mod[:, 8 + k, which:which + 1], mod[:, k, which:which + 1]
                            if half:
                                ins = nc.vector.tensor_scalar(dst, src, scale, shift, ALU.mult, ALU.add)
                            else:
                                ins = nc.scalar.activation(dst, src, ACT.Identity, bias=shift, scale=scale)
                        ins.then_inc(done, 1)

                    @block.vector
                    def _(dve):
                        dve.nop().then_inc(ut_dve, 2)
                        for n in range(2):
                            normalise(dve, n, n, 16)
                            modulate(dve, n, n, 1, slice(n * P, (n + 1) * P), 1, ut_dve)
                        with dve.Fori(0, L // P // 2) as i:
                            for s in range(2):
                                normalise(dve, 2 * i + s + 2, s, 16 * i + 32)
                                modulate(dve, 2 * i + s + 2, s, 0, bass.ds((2 * i + s) * P + LC, P), 1, ut_dve)

                    @block.scalar
                    def _(act):
                        act.nop().then_inc(ut_act, 2)

                        def tile(n, s, which, col):
                            act.wait_ge(var_done, n + 1)
                            nc.scalar.activation(stat[:, s, 15:16], stat[:, s, 14:15], ACT.Sqrt).then_inc(std_done, 1)
                            modulate(act, n, s, which, col, 0, ut_act)
                        for n in range(2):
                            tile(n, n, 1, slice(n * P, (n + 1) * P))
                        with act.Fori(0, L // P // 2) as i:
                            for s in range(2):
                                tile(2 * i + s + 2, s, 0, bass.ds((2 * i + s) * P + LC, P))

                    @block.tensor
                    def _(pe):
                        pe.nop().then_inc(turn_mm, 2)

                        def tile(n, s):
                            pe.wait_ge(xn_done, n + 1)
                            pe.wait_ge(ut_act, n + 1)
                            pe.wait_ge(ut_dve, n + 1)
                            for k in range(KD):
                                mm = pe.transpose(pt[:, s, k // 4, (k % 4) * P:(k % 4 + 1) * P],
                                                  xn[:, s, k * P:(k + 1) * P], ident[:, :])
                            mm.then_inc(turn_mm, 1)
                        for n in range(2):
                            tile(n, n)
                        with pe.Fori(0, L // P // 2) as i:
                            for s in range(2):
                                tile(2 * i + s + 2, s)

            if debug:
                dbg = sem("dbg")
                with nc.Block() as block:
                    @block.sync
                    def _(sp_):
                        sp_.dma_start(ut_dbg, ut[:, :, :]).then_inc(dbg, 16)
                        sp_.wait_ge(dbg, 16)

            def product(pe, bank, w, col, width):
                for k in range(KD):
                    mm = pe.matmul(bank, w[:, k * P:(k + 1) * P], ut[:, k, col:col + width],
                                   start=(k == 0), stop=(k == KD - 1))
                return mm

            with ExitStack() as cx:
                win = sb(cx, "win", [P, 2, D])
                lw = sb(cx, "lw", [P, 4, P])
                lv = sb(cx, "lv", [P, 9])
                X0, X1 = 2, LC + 5
                xin = sb(cx, "a_in", [P, LT + 6])
                xc = sb(cx, "xc", [P, LT])
                sg = sb(cx, "sg", [P, L])
                rg = [sb(cx, f"rg{d}", [P, LT]) for d in range(2)]
                ig = [sb(cx, f"ig{d}", [P, LT]) for d in range(2)]
                th = [sb(cx, f"th{d}", [P, LT]) for d in range(2)]
                h = [sb(cx, f"h{d}", [P, LT]) for d in range(2)]
                pb = ps(cx, "pb", [P, 8, CH])
                w_land = [sem("lru_w0"), sem("lru_w1")]
                lvec_land, lru_mm, bank_read, xc_done, lru_dv, a_done, sq_ready, sq_done, ya_done, ya_out = [
                    sem(n) for n in ("lvec_land", "lru_mm", "bank_read", "xc_done", "lru_dv", "a_done", "sq_ready",
                                     "sq_done", "ya_done", "ya_out")]
                NCH = 29
                NV = 17
                with nc.Block() as block:
                    @block.sync
                    def _(sp_):
                        def load_vectors(t):
                            sp_.dma_start(lw[:, :, :], a["lru_gate"][t]).then_inc(lvec_land, 16)
                            sp_.dma_start(lv[:, :], a["lru_vec"][t]).then_inc(lvec_land, 16)

                        def store(t):
                            sp_.wait_ge(ya_done, t + 2)
                            sp_.dma_start(yg_dram[t], sg[:, :]).then_inc(ya_out, 16)
                        sp_.nop().then_inc(ya_out, 16)
                        for n in range(2):
                            sp_.dma_start(win[:, n, :], a["w_in"][(B_AIN, B_AGATE)[n]]).then_inc(w_land[n], 16)
                        load_vectors(0)
                        with sp_.Fori(0, NB - 1) as t:
                            sp_.wait_ge(lru_mm, NCH * t + 5 + 1)
                            sp_.dma_start(win[:, 0, :], a["w_in"][t + B_AIN + 1]).then_inc(w_land[0], 16)
                            sp_.wait_ge(lru_mm, NCH * t + 9 + 1)
                            sp_.dma_start(win[:, 1, :], a["w_in"][t + B_AGATE + 1]).then_inc(w_land[1], 16)
                            store(t)
                            load_vectors(t + 1)
                        store(NB - 1)
                        sp_.wait_ge(ya_out, 16 * NB + 16)

                    @block.tensor
                    def _(pe):
                        pe.nop().then_inc(lru_mm, 1)
                        with pe.Fori(0, NB) as t:
                            n = 0

                            def bank(width):
                                nonlocal n
                                pe.wait_ge(bank_read, NCH * t + n + 1)
                                n += 1
                                return pb[:, (n - 1) % 8, 0:width]
                            pe.wait_ge(w_land[0], 16 * t + 16)
                            for col, width in ALL_CHUNKS:
                                product(pe, bank(width), win[:, 0, :], col, width).then_inc(lru_mm, 1)
                            pe.wait_ge(w_land[1], 16 * t + 16)
                            for col, width in LAT_CHUNKS:
                                product(pe, bank(width), win[:, 1, :], col, width).then_inc(lru_mm, 1)
                            pe.wait_ge(lvec_land, 32 * t + 32)
                            pe.wait_ge(xc_done, t + 2)
                            for g in range(4):
                                for col, width in ALL_CHUNKS:
                                    pe.matmul(bank(width), lw[:, g, :], xc[:, col:col + width],
                                              start=True, stop=True).then_inc(lru_mm, 1)
                            pe.wait_ge(bank_read, NCH * t + NCH + 8)

                    @block.scalar
                    def _(act):
                        act.nop().then_inc(bank_read, 8)
                        with act.Fori(0, NB) as t:
                            n = 0
                            s = nc.scalar

                            def bank(width):
                                nonlocal n
                                act.wait_ge(lru_mm, NCH * t + n + 2)
                                n += 1
                                return pb[:, (n - 1) % 8, 0:width]
                            act.wait_ge(xc_done, t + 1)
                            for col, width in ALL_CHUNKS:
                                at = X0 if col == 0 else X1 + col - LC
                                s.copy(xin[:, at:at + width], bank(width)).then_inc(bank_read, 1)
                            act.wait_ge(ya_out, 16 * t + 16)
                            for col, width in LAT_CHUNKS:
                                s.activation(sg[:, col - LC:col - LC + width], bank(width), ACT.Silu).then_inc(bank_read, 1)
                            act.wait_ge(lvec_land, 32 * t + 32)
                            act.wait_ge(ya_done, t + 1)
                            for g in range(4):
                                d, which = g // 2, g % 2
                                dst = (rg, ig)[which][d]
                                for col, width in ALL_CHUNKS:
                                    s.activation(dst[:, col:col + width], bank(width), ACT.Sigmoid,
                                                 bias=lv[:, 5 + 2 * which + d:6 + 2 * which + d]).then_inc(bank_read, 1)
                            act.wait_ge(bank_read, NCH * t + NCH + 8)
                            for d in range(2):
                                s.activation(th[d][:, :], rg[d][:, :], ACT.Tanh,
                                             scale=decay[:, bass.ds(2 * t + d, 1), 1]).then_inc(a_done, 1)
                                act.wait_ge(a_done, 4 * t + 2 * d + 1)
                                s.activation(rg[d][:, :], rg[d][:, :], ACT.Exp,
                                             scale=decay[:, bass.ds(2 * t + d, 1), 0]).then_inc(a_done, 1)
                            for d in range(2):
                                act.wait_ge(sq_ready, 2 * t + d + 1)
                                s.activation(th[d][:, :], th[d][:, :], ACT.Sqrt).then_inc(sq_done, 1)

                    @block.vector
                    def _(dve):
                        v = nc.vector
                        dve.nop().then_inc(ya_done, 1)
                        v.memset(xin[:, :], 0.0).then_inc(xc_done, 1)
                        with dve.Fori(0, NB) as t:
                            st = Steps(dve, lru_dv, NV * t)
                            dve.wait_ge(lvec_land, 32 * t + 32)
                            dve.wait_ge(bank_read, NCH * t + 5 + 8)
                            dve.wait_ge(lru_mm, NCH * t + 1)
                            for first, at, width in ((X0, 0, LC), (X1, LC, L)):
                                o = xc[:, at:at + width]
                                for k in range(4):
                                    src = xin[:, first + k - 2:first + k - 2 + width]
                                    if k == 0:
                                        ins = v.tensor_scalar(o, src, lv[:, 0:1], lv[:, 4:5], ALU.mult, ALU.add)
                                    else:
                                        ins = v.scalar_tensor_tensor(o, src, lv[:, k:k + 1], o, ALU.mult, ALU.add)
                                    if k == 3 and at == LC:
                                        ins.then_inc(xc_done, 1)
                                        dve.wait_ge(xc_done, t + 2)
                                    else:
                                        st(ins)
                            for d in range(2):
                                if d == 0:
                                    dve.wait_ge(bank_read, NCH * t + NCH + 8)
                                st(v.tensor_tensor(ig[d][:, :], ig[d][:, :], xc[:, :], ALU.mult))
                                dve.wait_ge(a_done, 4 * t + 2 * d + 2)
                                st(v.tensor_tensor(h[d][:, :], rg[d][:, :], rg[d][:, :], ALU.mult))
                                v.scalar_tensor_tensor(th[d][:, :], h[d][:, :], 1.0, th[d][:, :], ALU.add, ALU.mult).then_inc(sq_ready, 1)
                            dve.wait_ge(sq_done, 2 * t + 1)
                            st(v.tensor_tensor(ig[0][:, :], ig[0][:, :], th[0][:, :], ALU.mult))
                            v.tensor_tensor_scan(h[0][:, :], rg[0][:, :], ig[0][:, :], 0.0, ALU.mult, ALU.add).then_inc(lru_dv, 1)
                            st.n += 1
                            dve.wait_ge(sq_done, 2 * t + 2)
                            dve.wait_ge(sq_ready, 2 * t + 2)
                            ins = v.tensor_tensor(ig[1][:, :], ig[1][:, :], th[1][:, :], ALU.mult)
                            st.n -= 0
                            st(ins)
                            st(v.tensor_tensor_scan(h[1][:, LC - 1::-1], rg[1][:, LC - 1::-1], ig[1][:, LC - 1::-1],
                                                    0.0, ALU.mult, ALU.add))
                            lat = slice(LT - 1, LC - 1, -1)
                            ins = v.tensor_tensor_scan(h[1][:, lat], rg[1][:, lat], ig[1][:, lat],
                                                       h[1][:, 0:1], ALU.mult, ALU.add)
                            ins.then_inc(lru_dv, 1)
                            st.n += 1
                            dve.wait_ge(lru_dv, NV * t + 16)
                            st(v.tensor_tensor(h[0][:, LC:LT], h[0][:, LC:LT], h[1][:, LC:LT], ALU.add))
                            v.tensor_tensor(sg[:, :], sg[:, :], h[0][:, LC:LT], ALU.mult).then_inc(ya_done, 1)
                            assert st.n == NV, st.n

            with ExitStack() as cx:
                win = sb(cx, "win", [P, 4, D])
                qs = sb(cx, "qs", [P, L])
                kt = sb(cx, "kt", [P, LT])
                vt = sb(cx, "vt", [P, LT])
                NVB = LT // P + L // P - 1
                vk = sb(cx, "vk", [P, NVB, P])
                sg = sb(cx, "sg", [P, L])
                bt = sb(cx, "bt", [P, NDR * GW])
                qbd = sb(cx, "qbd", [P, 2, P])
                ss = sb(cx, "ss", [P, 2, BAND])
                pr = sb(cx, "pr", [P, 2, BAND + LC])
                prt = sb(cx, "prt", [P, 2, BAND + LC])
                on = sb(cx, "on", [P, 2, P])
                row_stat = sb(cx, "row_stat", [P, 2, 8])
                psc = [ps(cx, f"psc{s}", [P, 2, CH]) for s in range(2)]
                ppt = ps(cx, "ppt", [P, 2, CH])
                po = ps(cx, "po", [P, CH])
                pot = ps(cx, "pot", [P, CH])
                w_land = [sem(f"att_w{n}") for n in range(4)]
                (bt_land, att_mm, att_read, vk_mm, vk_read, qbd_done, s_mm, ss_done, nm_done, exp_done, att_dv, p_mm,
                 pt_read_dve, pt_read_act, pv_mm, on_done, ot_mm, yb_done, yb_out) = [sem(n) for n in (
                     "bt_land", "att_mm", "att_read", "vk_mm", "vk_read", "qbd_done", "s_mm", "ss_done", "nm_done", "exp_done",
                     "att_dv", "p_mm", "pt_read_dve", "pt_read_act", "pv_mm", "on_done", "ot_mm", "yb_done", "yb_out")]
                BLOCKS = (B_V, B_Q, B_K, B_BGATE)
                CHUNKS = (ALL_CHUNKS, LAT_CHUNKS, ALL_CHUNKS, LAT_CHUNKS)
                NCH = sum(len(c) for c in CHUNKS)
                ENDS = np.cumsum([len(c) for c in CHUNKS]).tolist()
                NVG = (NVB + 3) // 4

                def band(r):
                    return min(max(r - NKH // 2, 0), ROWS - NKH)

                def v_block(r0, c):
                    return 2 + r0 // 2 + c if r0 % 2 == 0 else 2 + L // P + r0 // 2 + c

                def v_column(n):
                    return n * P if n < LT // P else LC + GW + (n - LT // P) * P
                with nc.Block() as block:
                    @block.sync
                    def _(sp_):
                        def store(t):
                            sp_.wait_ge(yb_done, ROWS * t + ROWS + 1)
                            sp_.dma_start(yg_dram[t + NB], sg[:, :]).then_inc(yb_out, 16)
                        sp_.nop().then_inc(yb_out, 16)
                        for n in range(4):
                            sp_.dma_start(win[:, n, :], a["w_in"][BLOCKS[n]]).then_inc(w_land[n], 16)
                        sp_.dma_start(bt[:, :], bias_tab[0]).then_inc(bt_land, 16)
                        with sp_.Fori(0, NB - 1) as t:
                            for n in range(4):
                                sp_.wait_ge(att_mm, NCH * t + ENDS[n])
                                sp_.dma_start(win[:, n, :], a["w_in"][t + BLOCKS[n] + 1]).then_inc(w_land[n], 16)
                            store(t)
                            sp_.dma_start(bt[:, :], bias_tab[t + 1]).then_inc(bt_land, 16)
                        store(NB - 1)
                        sp_.wait_ge(yb_out, 16 * NB + 16)

                    @block.gpsimd
                    def _(pool):
                        nc.gpsimd.memset(qbd[:, :, :], 0.0).then_inc(qbd_done, 2)
                        pool.wait_ge(qbd_done, 2)
                        with pool.Fori(0, NB) as t:
                            pool.wait_ge(att_read, NCH * t + ENDS[1] + 4)
                            for r in range(ROWS):
                                pool.wait_ge(s_mm, ROWS * t + r + 1)
                                for h in range(2):
                                    x = slice(DH * h, DH * h + DH)
                                    pool.nop(nofuse=True)
                                    nc.gpsimd.tensor_copy(qbd[x, r % 2, x], qs[x, r * GW:(r + 1) * GW]).then_inc(qbd_done, 1)

                    @block.tensor
                    def _(pe):
                        pe.nop().then_inc(s_mm, 2)
                        pe.nop().then_inc(p_mm, 2)
                        pe.nop().then_inc(pv_mm, 2)
                        pe.nop().then_inc(ot_mm, 2)
                        with pe.Fori(0, NB) as t:
                            n = 0
                            for b in range(4):
                                pe.wait_ge(w_land[b], 16 * t + 16)
                                for col, width in CHUNKS[b]:
                                    if n < 4:
                                        pe.wait_ge(exp_done, 2 * ROWS * t + 4)
                                        pe.wait_ge(ss_done, ROWS * t + 2)
                                    pe.wait_ge(att_read, NCH * t + n + 1 if n >= 4 else NCH * t + 4)
                                    product(pe, psc[n % 4 // 2][:, n % 2, 0:width], win[:, b, :], col, width).then_inc(att_mm, 1)
                                    n += 1
                            pe.wait_ge(pt_read_dve, ROWS * t + 1)
                            pe.wait_ge(pt_read_act, ROWS * t + 1)
                            pe.wait_ge(att_read, NCH * t + NCH + 4)
                            for g in range(NVG):
                                if g >= 2:
                                    pe.wait_ge(vk_read, NVG * t + g - 1)
                                for n in range(4 * g, min(4 * g + 4, NVB)):
                                    c = v_column(n)
                                    mm = pe.transpose(ppt[:, g % 2, (n % 4) * P:(n % 4 + 1) * P], vt[:, c:c + P], ident[:, :])
                                mm.then_inc(vk_mm, 1)

                            def scores(r):
                                i = ROWS * t + r
                                pe.wait_ge(qbd_done, 2 * i + 4)
                                pe.wait_ge(ss_done, i + 1)
                                pe.wait_ge(exp_done, 2 * i + 2)
                                c = LC + band(r) * GW
                                pe.matmul(psc[r % 2][:, 0, :], qbd[:, r % 2, :], kt[:, c:c + BAND], start=True, stop=True)
                                pe.matmul(psc[r % 2][:, 1, 0:LC], qbd[:, r % 2, :], kt[:, 0:LC], start=True, stop=True).then_inc(s_mm, 1)

                            def turn(r):
                                i = ROWS * t + r
                                pe.wait_ge(exp_done, 2 * i + 6)
                                pe.wait_ge(pt_read_dve, i + 1)
                                pe.wait_ge(pt_read_act, i + 1)
                                for c in range(6):
                                    mm = pe.transpose(ppt[:, c // 4, (c % 4) * P:(c % 4 + 1) * P],
                                                      pr[:, r % 2, c * P:(c + 1) * P], ident[:, :])
                                mm.then_inc(p_mm, 1)

                            def values(r):
                                i = ROWS * t + r
                                pe.wait_ge(pt_read_dve, i + 2)
                                pe.wait_ge(pt_read_act, i + 2)
                                pe.wait_ge(on_done, i + 1)
                                for c in range(6):
                                    b = v_block(band(r), c) if c < 4 else c - 4
                                    mm = pe.matmul(po[:, 0:P], prt[:, r % 2, c * P:(c + 1) * P], vk[:, b, :],
                                                   start=(c == 0), stop=(c == 5))
                                mm.then_inc(pv_mm, 1)

                            def turn_output(r):
                                i = ROWS * t + r
                                pe.wait_ge(on_done, i + 2)
                                pe.wait_ge(yb_done, i + 1)
                                pe.transpose(pot[:, 0:P], on[:, r % 2, :], ident[:, :]).then_inc(ot_mm, 1)
                            scores(0)
                            scores(1)
                            pe.wait_ge(vk_read, NVG * t + NVG)
                            for r in range(ROWS):
                                turn(r)
                                if r + 2 < ROWS:
                                    scores(r + 2)
                                values(r)
                                if r:
                                    turn_output(r - 1)
                            turn_output(ROWS - 1)

                    @block.scalar
                    def _(act):
                        s = nc.scalar
                        act.nop().then_inc(att_read, 4)
                        act.nop().then_inc(exp_done, 4)
                        act.nop().then_inc(pt_read_act, 1)
                        with act.Fori(0, NB) as t:
                            n = 0
                            act.wait_ge(pv_mm, ROWS * t + 2)
                            act.wait_ge(s_mm, ROWS * t + 2)
                            for b in range(4):
                                for col, width in CHUNKS[b]:
                                    act.wait_ge(att_mm, NCH * t + n + 1)
                                    src = psc[n % 4 // 2][:, n % 2, 0:width]
                                    if b == 0:
                                        ins = s.copy(vt[:, col:col + width], src)
                                    elif b == 1:
                                        ins = s.mul(qs[:, col - LC:col - LC + width], src, DH ** -0.5)
                                    elif b == 2:
                                        ins = s.copy(kt[:, col:col + width], src)
                                    else:
                                        if col == LC:
                                            act.wait_ge(yb_out, 16 * t + 16)
                                        ins = s.activation(sg[:, col - LC:col - LC + width], src, ACT.Silu)
                                    ins.then_inc(att_read, 1)
                                    n += 1
                            for g in range(NVG):
                                act.wait_ge(vk_mm, NVG * t + g + 1)
                                m = min(4, NVB - 4 * g)
                                s.copy(vk[:, 4 * g:4 * g + m, :], ppt[:, g % 2, 0:m * P].rearrange("p (a b) -> p a b", b=P)).then_inc(vk_read, 1)

                            def exps(r):
                                i = ROWS * t + r
                                act.wait_ge(nm_done, i + 1)
                                act.wait_ge(p_mm, i + 1)
                                q = row_stat[:, r % 2, :]
                                s.activation(pr[:, r % 2, 0:BAND], ss[:, r % 2, :], ACT.Exp, bias=q[:, 2:3],
                                             accum_out=q[:, 3:4]).then_inc(exp_done, 1)
                                s.activation(pr[:, r % 2, BAND:BAND + LC], psc[r % 2][:, 1, 0:LC], ACT.Exp, bias=q[:, 2:3],
                                             accum_out=q[:, 4:5]).then_inc(exp_done, 1)
                            exps(0)
                            exps(1)
                            for r in range(ROWS):
                                i = ROWS * t + r
                                act.wait_ge(p_mm, i + 3)
                                act.wait_ge(pv_mm, i + 1)
                                s.copy(prt[:, r % 2, BAND:BAND + LC], ppt[:, 1, 0:LC]).then_inc(pt_read_act, 1)
                                if r + 2 < ROWS:
                                    exps(r + 2)

                    @block.vector
                    def _(dve):
                        v = nc.vector
                        dve.nop().then_inc(ss_done, 2)
                        dve.nop().then_inc(pt_read_dve, 1)
                        dve.nop().then_inc(on_done, 1)
                        dve.nop().then_inc(yb_done, 1)
                        NV = 3 * ROWS
                        with dve.Fori(0, NB) as t:
                            st = Steps(dve, att_dv, NV * t)

                            def maxima(r):
                                i = ROWS * t + r
                                q = row_stat[:, r % 2, :]
                                dve.wait_ge(s_mm, i + 3)
                                dve.wait_ge(exp_done, 2 * i + 2)
                                off = (band(r) - r + NKH - 1) * GW
                                dve.nop(nofuse=True)
                                v.tensor_tensor_reduce(ss[:, r % 2, :], psc[r % 2][:, 0, :], bt[:, off:off + BAND], 1.0,
                                                       -3e38, ALU.add, ALU.max, q[:, 0:1]).then_inc(ss_done, 1)
                                st(v.tensor_reduce(q[:, 1:2], psc[r % 2][:, 1, 0:LC], AX_X, ALU.max))
                                dve.wait_ge(ss_done, i + 3)
                                v.tensor_scalar(q[:, 2:3], q[:, 0:1], q[:, 1:2], -1.0, ALU.max, ALU.mult).then_inc(nm_done, 1)

                            def gated(r):
                                i = ROWS * t + r
                                dve.wait_ge(ot_mm, i + 3)
                                for h in range(2):
                                    x = slice(DH * h, DH * h + DH)
                                    o = sg[x, r * GW:(r + 1) * GW]
                                    ins = v.tensor_tensor(o, pot[x, x], o, ALU.mult)
                                ins.then_inc(yb_done, 1)
                            dve.wait_ge(att_read, NCH * t + NCH + 4)
                            dve.wait_ge(bt_land, 16 * t + 16)
                            maxima(0)
                            maxima(1)
                            for r in range(ROWS):
                                i = ROWS * t + r
                                q = row_stat[:, r % 2, :]
                                dve.wait_ge(p_mm, i + 3)
                                dve.wait_ge(pv_mm, i + 1)
                                v.tensor_copy(prt[:, r % 2, 0:BAND], ppt[:, 0, :]).then_inc(pt_read_dve, 1)
                                dve.wait_ge(exp_done, 2 * i + 6)
                                st(v.tensor_tensor(q[:, 5:6], q[:, 3:4], q[:, 4:5], ALU.add))
                                st(v.reciprocal(q[:, 6:7], q[:, 5:6]))
                                if r + 2 < ROWS:
                                    maxima(r + 2)
                                dve.wait_ge(pv_mm, i + 3)
                                dve.wait_ge(ot_mm, i + 1)
                                v.tensor_scalar(on[:, r % 2, :], po[:, 0:P], q[:, 6:7], None, ALU.mult).then_inc(on_done, 1)
                                if r:
                                    gated(r - 1)
                            gated(ROWS - 1)
                            assert st.n == NV, st.n

            with ExitStack() as cx:
                win = sb(cx, "win", [P, 4, D])
                hv = sb(cx, "hv", [P, 13])
                pad = [sb(cx, f"pad{n}", [P, L + 2]) for n in range(3)]
                w = sb(cx, "w", [P, L])
                x0c = pad[1][:, 0:L]
                sg = sb(cx, "sg", [P, L])
                wt = sb(cx, "wt", [P, 16, P])
                flat = wt[:, :, :].rearrange("p a b -> p (a b)")
                sent = sb(cx, "sent", [P, NPR, P])
                x1c = sent[:, 0:16, :].rearrange("p a b -> p (a b)")
                vc = sent[:, 16:32, :].rearrange("p a b -> p (a b)")
                got = sb(cx, "got", [P, NPR, P])
                spec = sb(cx, "spec", [P, 2, 4, 2, P])
                tab = sb(cx, "tab", [P, 2, 4, 3 * P])
                prd = sb(cx, "prd", [P, 2, 2, 4, P])
                d1 = sb(cx, "d1", [P, P])
                d1i = sb(cx, "d1i", [P, R1])
                pb = ps(cx, "pb", [P, 4, CH])
                pf = ps(cx, "pf", [P, 4, CH])
                w_land = [sem(f"hy_w{n}") for n in range(4)]
                tab_land = [sem("tab_land0"), sem("tab_land1")]
                (hd_land, hv_land, hy_mm, hy_read, hy_dv, w_done, wt_mm, wt_read, s1_mm, s1_act, s1_dve, x1_out, x2_land, s2_mm, prd_done,
                 g_mm, g_read, inv_out, vf_land, fin_mm, fin_done, yc_done, yc_out) = [sem(n) for n in (
                     "hd_land", "hv_land", "hy_mm", "hy_read", "hy_dv", "w_done", "wt_mm", "wt_read", "s1_mm", "s1_act", "s1_dve", "x1_out",
                     "x2_land", "s2_mm", "prd_done", "g_mm", "g_read", "inv_out", "vf_land", "fin_mm", "fin_done", "yc_done", "yc_out")]
                BLOCKS = (B_X1, B_HV, B_X0, B_CGATE)
                NG = NPR // 4
                HV, HV_PAD = 11, 7
                with nc.Block() as block:
                    @block.sync
                    def _(sp_):
                        sp_.nop().then_inc(yc_out, 16)
                        sp_.nop().then_inc(inv_out, 64)
                        sp_.dma_start(d1[:, :], a["dft1"]).then_inc(hd_land, 16)
                        sp_.dma_start(d1i[:, :], a["idft1"]).then_inc(hd_land, 16)
                        for n in range(4):
                            sp_.dma_start(win[:, n, :], a["w_in"][BLOCKS[n]]).then_inc(w_land[n], 16)
                        sp_.dma_start(hv[:, :], a["hy_vec"][0]).then_inc(hv_land, 16)

                        def regroup(t):
                            sp_.wait_ge(s1_act, 4 * t + 4)
                            sp_.wait_ge(s1_dve, 4 * t + 4)
                            for b in range(4):
                                o = 2 * (b % 2) + b // 2
                                dst = fwd_mid[t][32 * o:32 * o + 32].rearrange("q k c -> k q c")
                                sp_.dma_start(dst, sent[32 * b:32 * b + 32, :, :]).then_inc(x1_out, 16)
                            sp_.wait_ge(x1_out, 64 * t + 64)
                            sp_.dma_start(got[:, :, :], fwd_mid[t]).then_inc(x2_land, 16)
                            sp_.wait_ge(g_read, NG * t + NG)
                            for b in range(4):
                                o = 2 * (b % 2) + b // 2
                                dst = inv_mid[t][32 * o:32 * o + 32].rearrange("k q c -> q k c")
                                sp_.dma_start(dst, sent[32 * b:32 * b + 32, :, :]).then_inc(inv_out, 16)
                            sp_.wait_ge(inv_out, 64 * t + 128)
                            sp_.dma_start(got[:, :, :], inv_mid[t]).then_inc(vf_land, 16)
                            sp_.wait_ge(yc_done, t + 2)
                            sp_.dma_start(yg_dram[t + 2 * NB], sg[:, :]).then_inc(yc_out, 16)
                        with sp_.Fori(0, NB - 1) as t:
                            for n in range(4):
                                sp_.wait_ge(hy_mm, 16 * t + 4 * n + 4)
                                sp_.dma_start(win[:, n, :], a["w_in"][t + BLOCKS[n] + 1]).then_inc(w_land[n], 16)
                            regroup(t)
                            sp_.dma_start(hv[:, :], a["hy_vec"][t + 1]).then_inc(hv_land, 16)
                        regroup(NB - 1)
                        sp_.wait_ge(yc_out, 16 * NB + 16)

                    @block.gpsimd
                    def _(pool):
                        with pool.Fori(0, NB) as t:
                            for g in range(NG):
                                pool.wait_ge(g_mm, NG * t + g + 1)
                                k = slice(4 * g, 4 * g + 4)
                                for b in range(2):
                                    pool.dma_start(spec[:, g % 2, :, b, :], filt_spec[k, b, :, bass.ds(t * P, P)].rearrange("k p c -> p k c")).then_inc(tab_land[g % 2], 16)
                                pool.dma_start(tab[:, g % 2, :, 0:P], a["dft2"][:, k, :]).then_inc(tab_land[g % 2], 16)
                                pool.dma_start(tab[:, g % 2, :, P:3 * P], a["idft2"][:, k, :]).then_inc(tab_land[g % 2], 16)
                        for s in range(2):
                            pool.wait_ge(tab_land[s], 64 * NB * NG // 2)

                    @block.tensor
                    def _(pe):
                        pe.nop().then_inc(g_mm, 2)
                        pe.wait_ge(hd_land, 32)
                        with pe.Fori(0, NB) as t:
                            for n in range(16):
                                if n % 4 == 0:
                                    pe.wait_ge(w_land[n // 4], 16 * t + 16)
                                pe.wait_ge(hy_read, 16 * t + n + 1)
                                product(pe, pb[:, n % 4, :], win[:, n // 4, :], *LAT_CHUNKS[n % 4]).then_inc(hy_mm, 1)
                            pe.wait_ge(w_done, t + 1)
                            pe.wait_ge(fin_done, 4 * t + 4)
                            for g in range(16):
                                mm = pe.transpose(pf[:, g // 4, (g % 4) * P:(g % 4 + 1) * P], w[:, g * P:(g + 1) * P], ident[:, :])
                                if g % 4 == 3:
                                    mm.then_inc(wt_mm, 1)
                            pe.wait_ge(wt_read, 4 * t + 4)
                            for q in range(4):
                                if q >= 2:
                                    pe.wait_ge(s1_act, 4 * t + q - 1)
                                    pe.wait_ge(s1_dve, 4 * t + q - 1)
                                for j in range(2):
                                    for g in range(4):
                                        x = slice(R1 * j, R1 * j + R1)
                                        mm = pe.matmul(pf[:, 2 * (q % 2) + j, g * P:(g + 1) * P], d1[x, :], wt[x, 4 * q + g, :],
                                                       start=True, stop=True)
                                mm.then_inc(s1_mm, 1)

                            def forward(g):
                                pe.wait_ge(tab_land[g % 2], 64 * (NG // 2) * t + 64 * (g // 2) + 64)
                                if g >= 2:
                                    pe.wait_ge(prd_done, NG * t + g - 1)
                                for k in range(4):
                                    mm = pe.matmul(pf[:, g % 2, k * P:(k + 1) * P], tab[:, g % 2, k, 0:P], got[:, 4 * g + k, :],
                                                   start=True, stop=True)
                                mm.then_inc(s2_mm, 1)

                            def inverse(g):
                                pe.wait_ge(prd_done, NG * t + g + 1)
                                if g >= 2:
                                    pe.wait_ge(g_read, NG * t + g - 1)
                                for k in range(4):
                                    o = pf[:, 2 + g % 2, k * P:(k + 1) * P]
                                    pe.matmul(o, tab[:, g % 2, k, P:2 * P], prd[:, g % 2, 0, k, :], start=True, stop=False)
                                    mm = pe.matmul(o, tab[:, g % 2, k, 2 * P:3 * P], prd[:, g % 2, 1, k, :], start=False, stop=True)
                                mm.then_inc(g_mm, 1)
                            pe.wait_ge(s1_act, 4 * t + 4)
                            pe.wait_ge(s1_dve, 4 * t + 4)
                            pe.wait_ge(x2_land, 16 * t + 16)
                            forward(0)
                            for g in range(NG):
                                if g + 1 < NG:
                                    forward(g + 1)
                                inverse(g)
                            pe.wait_ge(g_read, NG * t + NG)
                            pe.wait_ge(vf_land, 16 * t + 16)
                            for q in range(NPR):
                                mm = pe.matmul(pf[:, q // 8, (q % 8) * R1:(q % 8 + 1) * R1], got[:, q, :], d1i[:, :], start=True, stop=True)
                                if q % 8 == 7:
                                    mm.then_inc(fin_mm, 1)

                    @block.scalar
                    def _(act):
                        s = nc.scalar
                        act.nop().then_inc(hy_read, 4)
                        with act.Fori(0, NB) as t:
                            act.wait_ge(hy_dv, HV * t + HV_PAD)
                            for n in range(16):
                                act.wait_ge(hy_mm, 16 * t + n + 1)
                                c = n % 4 * CH
                                if n == 12:
                                    act.wait_ge(yc_out, 16 * t + 16)
                                if n < 12:
                                    ins = s.copy(pad[n // 4][:, 1 + c:1 + c + CH], pb[:, n % 4, :])
                                else:
                                    ins = s.activation(sg[:, c:c + CH], pb[:, n % 4, :], ACT.Silu)
                                ins.then_inc(hy_read, 1)
                            for g in range(4):
                                act.wait_ge(wt_mm, 4 * t + g + 1)
                                s.copy(wt[:, 4 * g:4 * g + 4, :], pf[:, g, :].rearrange("p (a b) -> p a b", b=P)).then_inc(wt_read, 1)
                            act.wait_ge(inv_out, 64 * t + 64)
                            pairs = sent[:, :, :].rearrange("p (g j) c -> p g j c", j=2)
                            for q in range(4):
                                act.wait_ge(s1_mm, 4 * t + q + 1)
                                s.copy(pairs[:, 4 * q:4 * q + 4, 0, :], pf[:, 2 * (q % 2), :].rearrange("p (a b) -> p a b", b=P)).then_inc(s1_act, 1)
                            act.wait_ge(x1_out, 64 * t + 64)
                            for g in range(NG):
                                act.wait_ge(g_mm, NG * t + g + 3)
                                s.copy(sent[:, 4 * g:4 * g + 4, :], pf[:, 2 + g % 2, :].rearrange("p (a b) -> p a b", b=P)).then_inc(g_read, 1)

                    @block.vector
                    def _(dve):
                        v = nc.vector
                        dve.nop().then_inc(yc_done, 1)
                        dve.nop().then_inc(fin_done, 4)
                        for n in range(3):
                            v.memset(pad[n][:, 0:1], 0.0).then_inc(hy_dv, 1)
                            v.memset(pad[n][:, L + 1:L + 2], 0.0).then_inc(hy_dv, 1)
                        v.memset(w[:, 0:1], 0.0).then_inc(hy_dv, 1)
                        with dve.Fori(0, NB) as t:
                            st = Steps(dve, hy_dv, HV * t + 7)
                            dve.wait_ge(hv_land, 16 * t + 16)

                            def conv3(dst, src, taps, bias):
                                st(v.tensor_scalar(dst, src[:, 0:L], hv[:, taps:taps + 1], hv[:, bias:bias + 1], ALU.mult, ALU.add))
                                for k in (1, 2):
                                    st(v.scalar_tensor_tensor(dst, src[:, k:k + L], hv[:, taps + k:taps + k + 1], dst, ALU.mult, ALU.add))
                            dve.wait_ge(hy_read, 16 * t + 4 + 4)
                            dve.wait_ge(inv_out, 64 * t + 64)
                            conv3(x1c, pad[0], 3, 10)
                            dve.wait_ge(hy_read, 16 * t + 8 + 4)
                            conv3(vc, pad[1], 6, 11)
                            v.tensor_tensor(w[:, :].rearrange("p (n2 n1) -> p n1 n2", n2=R1), x1c.rearrange("p (n1 n2) -> p n1 n2", n2=R1),
                                            vc.rearrange("p (n1 n2) -> p n1 n2", n2=R1), ALU.mult).then_inc(w_done, 1)
                            dve.wait_ge(hy_read, 16 * t + 12 + 4)
                            conv3(x0c, pad[2], 0, 9)
                            pairs = sent[:, :, :].rearrange("p (g j) c -> p g j c", j=2)
                            for q in range(4):
                                dve.wait_ge(s1_mm, 4 * t + q + 1)
                                v.tensor_copy(pairs[:, 4 * q:4 * q + 4, 1, :], pf[:, 2 * (q % 2) + 1, :].rearrange("p (a b) -> p a b", b=P)).then_inc(s1_dve, 1)
                            for g in range(NG):
                                dve.wait_ge(s2_mm, NG * t + g + 1)
                                dve.wait_ge(g_mm, NG * t + g + 1)
                                x = pf[:, g % 2, :].rearrange("p (a b) -> p a b", b=P)
                                for b in range(2):
                                    ins = v.tensor_tensor(prd[:, g % 2, b, :, :], x, spec[:, g % 2, :, b, :], ALU.mult)
                                ins.then_inc(prd_done, 1)
                            dve.wait_ge(w_done, t + 1)
                            for q in range(4):
                                dve.wait_ge(fin_mm, 4 * t + q + 1)
                                y = flat.rearrange("p (n1 n2) -> p n2 n1", n2=R1)[:, 16 * q:16 * q + 16, :]
                                wv = w[:, CH * q:CH * q + CH].rearrange("p (n2 n1) -> p n2 n1", n1=32)
                                v.scalar_tensor_tensor(y, wv, hv[:, 12:13], pf[:, q, :].rearrange("p (a b) -> p a b", b=32),
                                                       ALU.mult, ALU.add).then_inc(fin_done, 1)
                            dve.wait_ge(fin_done, 4 * t + 8)
                            st(v.tensor_tensor(flat, flat, x0c, ALU.mult))
                            st(v.memset(pad[1][:, 0:1], 0.0))
                            dve.wait_ge(hy_read, 16 * t + 16 + 4)
                            v.tensor_tensor(sg[:, :], sg[:, :], flat, ALU.mult).then_inc(yc_done, 1)
                            assert st.n == HV, st.n

            with ExitStack() as cx:
                win = sb(cx, "win", [P, 3, D])
                wb = sb(cx, "wb", [P, 3, 4 * P])
                yg = sb(cx, "yg", [P, 3 * NB, L])
                sig = sb(cx, "sig", [P, 2, CH])
                tmp = sb(cx, "tmp", [P, CH])
                m = sb(cx, "m", [P, 4, CH])
                pg = ps(cx, "pg", [P, 4, CH])
                pr_ = ps(cx, "pr", [P, 4, CH])
                w_land = [sem(f"mg_w{b}") for b in range(3)]
                yg_land = [sem(f"yg_land{b}") for b in range(3)]
                mg_mm, br_mm, sig_done, br_read, mg_dv, m_done = [sem(n) for n in (
                    "mg_mm", "br_mm", "sig_done", "br_read", "mg_dv", "m_done")]
                m_out = [sem(f"m_out{c}") for c in range(4)]
                with nc.Block() as block:
                    @block.sync
                    def _(sp_):
                        def load(j, b):
                            sp_.dma_start(win[:, b, :], a["w_in"][j + B_G + KD * b]).then_inc(w_land[b], 16)
                            sp_.dma_start(wb[:, b, :], a["w_branch"][j][:, b * 4 * P:(b + 1) * 4 * P]).then_inc(w_land[b], 16)

                        def store(j):
                            for c in range(4):
                                sp_.wait_ge(m_done, 4 * j + c + 1)
                                sp_.dma_start(m_dram[4 * c:4 * c + 4, :, bass.ds(j, 1), :].rearrange("n p o c -> p n (o c)"),
                                              m[:, c, :].rearrange("p (n c) -> p n c", c=P)).then_inc(m_out[c], 16)
                        for c in range(4):
                            sp_.nop().then_inc(m_out[c], 16)
                        for b in range(3):
                            load(0, b)
                            for k in range(NB):
                                sp_.dma_start(yg[:, NB * b + k, :], yg_dram[NB * b + k]).then_inc(yg_land[b], 16)
                        with sp_.Fori(0, KD - 1) as j:
                            for b in range(3):
                                sp_.wait_ge(br_mm, 12 * j + 4 * b + 4)
                                load(j + 1, b)
                            store(j)
                        store(KD - 1)
                        for c in range(4):
                            sp_.wait_ge(m_out[c], 16 * KD + 16)

                    @block.tensor
                    def _(pe):
                        with pe.Fori(0, KD) as j:
                            for b in range(3):
                                pe.wait_ge(w_land[b], 32 * j + 32)
                                pe.wait_ge(yg_land[b], 16 * NB)
                                for c in range(4):
                                    n = 12 * j + 4 * b + c
                                    pe.wait_ge(sig_done, n + 1)
                                    product(pe, pg[:, c, :], win[:, b, :], *LAT_CHUNKS[c]).then_inc(mg_mm, 1)
                                    pe.wait_ge(br_read, n + 1)
                                    for k in range(NB):
                                        mm = pe.matmul(pr_[:, c, :], wb[:, b, k * P:(k + 1) * P], yg[:, NB * b + k, c * CH:(c + 1) * CH],
                                                       start=(k == 0), stop=(k == NB - 1))
                                    mm.then_inc(br_mm, 1)

                    @block.scalar
                    def _(act):
                        act.nop().then_inc(sig_done, 4)
                        with act.Fori(0, KD) as j:
                            for i in range(12):
                                n = 12 * j + i
                                act.wait_ge(mg_mm, n + 1)
                                act.wait_ge(br_read, n + 3)
                                nc.scalar.activation(sig[:, i % 2, :], pg[:, i % 4, :], ACT.Sigmoid).then_inc(sig_done, 1)

                    @block.vector
                    def _(dve):
                        v = nc.vector
                        dve.nop().then_inc(br_read, 4)
                        with dve.Fori(0, KD) as j:
                            st = Steps(dve, mg_dv, 4 * j)
                            for i in range(12):
                                b, c = i // 4, i % 4
                                n = 12 * j + i
                                dve.wait_ge(sig_done, n + 5)
                                dve.wait_ge(br_mm, n + 1)
                                if b == 0:
                                    dve.wait_ge(m_out[c], 16 * j + 16)
                                    v.tensor_tensor(m[:, c, :], sig[:, c % 2, :], pr_[:, c, :], ALU.mult).then_inc(br_read, 1)
                                    continue
                                v.tensor_tensor(tmp[:, :], sig[:, c % 2, :], pr_[:, c, :], ALU.mult).then_inc(br_read, 1)
                                dve.wait_ge(br_read, n + 5)
                                ins = v.tensor_tensor(m[:, c, :], m[:, c, :], tmp[:, :], ALU.add)
                                if b == 1:
                                    st(ins)
                                else:
                                    ins.then_inc(m_done, 1)
                                    dve.wait_ge(m_done, 4 * j + c + 1)

        with ExitStack() as cx:
            wo = sb(cx, "wo", [P, KD, D])
            mt = sb(cx, "mt", [P, 2, D])
            xin = sb(cx, "xin", [P, 2, D])
            h = sb(cx, "h", [P, 2, D])
            stat = sb(cx, "stat", [P, 2, 18])
            gb = sb(cx, "gb", [P, 2, D])
            pout = ps(cx, "pout", [P, 2, 2, CH])
            wo_land, gb_land = sem("wo_land"), sem("gb_land")
            t_land = [sem("t_land0"), sem("t_land1")]
            out_mm, o_read, out_dv, ovar_done, ostd_done, h_done, y_done = [sem(n) for n in (
                "out_mm", "o_read", "out_dv", "ovar_done", "ostd_done", "h_done", "y_done")]
            stored, biased = [sem("stored0"), sem("stored1")], sem("biased")
            NV = 5
            NT = L // P
            with nc.Block() as block:
                @block.sync
                def _(sp_):
                    for s in range(2):
                        sp_.nop().then_inc(stored[s], 16)
                    for k in range(KD):
                        sp_.dma_start(wo[:, k, :], a["w_out"][:, k, :]).then_inc(wo_land, 16)
                    for n, name in enumerate(("ln_g", "ln_b")):
                        sp_.dma_start(gb[:, n, :], bass.AP(tensor=a[name].tensor, offset=0, ap=[[0, P], [1, D]])).then_inc(gb_land, 16)
                    with sp_.Fori(0, NT // 2) as i:
                        for s in range(2):
                            n = 2 * i + s
                            sp_.wait_ge(out_mm, n + 1)
                            sp_.wait_ge(h_done, n + 1)
                            sp_.dma_start(mt[:, s, :], m_dram[n].rearrange("p k c -> p (k c)")).then_inc(t_land[s], 16)
                            sp_.dma_start(xin[:, s, :], a["x"].rearrange("(n p) d -> n p d", p=P)[n]).then_inc(t_land[s], 16)

                @block.tensor
                def _(pe):
                    pe.nop().then_inc(out_mm, 2)
                    pe.wait_ge(wo_land, 16 * KD)
                    with pe.Fori(0, NT // 2) as i:
                        for s in range(2):
                            pe.wait_ge(t_land[s], 32 * i + 32)
                            pe.wait_ge(o_read, 2 * i + s + 1)
                            for half in range(2):
                                for k in range(KD):
                                    mm = pe.matmul(pout[:, s, half, :], mt[:, s, k * P:(k + 1) * P], wo[:, k, half * CH:(half + 1) * CH],
                                                   start=(k == 0), stop=(k == KD - 1))
                            mm.then_inc(out_mm, 1)

                @block.vector
                def _(dve):
                    v = nc.vector
                    dve.nop().then_inc(o_read, 2)
                    dve.nop().then_inc(h_done, 2)
                    with dve.Fori(0, NT // 2) as i:
                        for s in range(2):
                            n = 2 * i + s
                            st = Steps(dve, out_dv, NV * n)
                            x, q = h[:, s, :], stat[:, s, :]
                            dve.wait_ge(out_mm, n + 3)
                            dve.wait_ge(stored[s], 16 * i + 16)
                            v.tensor_tensor(x, pout[:, s, :, :].rearrange("p a b -> p (a b)"), gate_row[:, :], ALU.mult).then_inc(o_read, 1)
                            dve.wait_ge(o_read, n + 3)
                            dve.wait_ge(t_land[s], 32 * i + 32)
                            v.scalar_tensor_tensor(x, xin[:, s, :], ALPHA, x, ALU.mult, ALU.add).then_inc(h_done, 1)
                            dve.wait_ge(h_done, n + 3)
                            st(v.bn_stats(q[:, 0:6], x[:, 0:512]))
                            st(v.bn_stats(q[:, 6:12], x[:, 512:1024]))
                            dve.nop(nofuse=True)
                            st(v.bn_aggr(q[:, 12:14], q[:, 0:12]))
                            v.tensor_scalar(q[:, 14:15], q[:, 13:14], EPS, None, ALU.add).then_inc(ovar_done, 1)
                            dve.wait_ge(ostd_done, n + 1)
                            st(v.reciprocal(q[:, 16:17], q[:, 15:16]))
                            dve.wait_ge(gb_land, 32)
                            st(v.tensor_scalar(x, x, q[:, 12:13], q[:, 16:17], ALU.subtract, ALU.mult))
                            v.tensor_tensor(x, x, gb[:, 0, :], ALU.mult).then_inc(y_done, 1)

                @block.scalar
                def _(act):
                    with act.Fori(0, NT // 2) as i:
                        for s in range(2):
                            act.wait_ge(ovar_done, 2 * i + s + 1)
                            nc.scalar.activation(stat[:, s, 15:16], stat[:, s, 14:15], ACT.Sqrt).then_inc(ostd_done, 1)
                            act.wait_ge(biased, 2 * i + s + 1)
                            act.dma_start(out.rearrange("(n p) d -> n p d", p=P)[2 * i + s], h[:, s, :]).then_inc(stored[s], 16)
                    for s in range(2):
                        act.wait_ge(stored[s], 16 * (NT // 2) + 16)

                @block.gpsimd
                def _(pool):
                    pool.wait_ge(gb_land, 32)
                    with pool.Fori(0, NT // 2) as i:
                        for s in range(2):
                            n = 2 * i + s
                            pool.wait_ge(y_done, n + 1)
                            nc.gpsimd.tensor_tensor(h[:, s, :], h[:, s, :], gb[:, 1, :], ALU.add).then_inc(biased, 1)


def lay_out(x, c, ctx, c_ctx, w_mod, b_mod, w_in, lru_conv_w, lru_conv_b, lru_w_a, lru_b_a, lru_w_x, lru_b_x,
            lru_lambda, na_rpb, hy_conv_w, hy_conv_b, hy_w1, hy_b1, hy_freq1, hy_w2, hy_b2, hy_freq2, hy_w3,
            hy_d_skip, w_branch_out, w_out, ln_g, ln_b):
    def tiles(v):
        return v.reshape(-1, P).T

    def twice(v):
        return np.concatenate([v, v], -1)
    o = {"x": x[0], "ctx": ctx[0]}
    o["cvec"] = np.stack([tiles(c[0]), tiles(c_ctx)], -1)
    o["w_mod"] = w_mod[0].reshape(KD, P, 24, P).transpose(2, 1, 0, 3).reshape(24, P, D)
    o["bmod"] = np.stack([tiles(b_mod[0])] * 2, -1)
    o["w_in"] = w_in[0].reshape(KD, P, 64, P).transpose(2, 1, 0, 3).reshape(64, P, D)
    o["lam"] = lru_lambda[0].reshape(2, NB, P).transpose(2, 1, 0).reshape(P, 2 * NB)
    rpb = np.zeros((HEADS, NDR, TOE), np.float32)
    rpb[:, :, GW - NKW:GW + NKW - 1] = na_rpb[0]
    o["rpb"] = rpb
    o["lru_vec"] = np.stack([*lru_conv_w[0].reshape(4, NB, P), lru_conv_b[0].reshape(NB, P),
                             *lru_b_a[0].reshape(2, NB, P), *lru_b_x[0].reshape(2, NB, P)], -1)
    gate = np.zeros((NB, P, 4, P), np.float32)
    for d in range(2):
        for n, w in enumerate((lru_w_a, lru_w_x)):
            for b in range(8):
                r = slice(64 * (b % 2), 64 * (b % 2) + 64)
                gate[b // 2, r, 2 * d + n, r] = w[0, d, b]
    o["lru_gate"] = gate
    cw = hy_conv_w[0].reshape(3, 3, NB, P)
    cb = hy_conv_b[0].reshape(3, NB, P)
    o["hy_vec"] = np.stack([cw[k, part] for part in range(3) for k in range(3)] + [cb[0], cb[1], cb[2],
                           hy_d_skip[0].reshape(NB, P)], -1)
    o["hy_w1"] = twice(hy_w1[0])
    o["hy_w2"] = twice(hy_w2[0])
    o["hy_bf"] = np.stack([twice(v[0]) for v in (hy_b1, hy_freq1, hy_b2, hy_freq2)], -1)
    o["hy_w3"] = np.concatenate([hy_w3[0][:, :512], hy_w3[0][:, 512:]], 0)
    o["w_branch"] = w_branch_out[0].reshape(3, NB, P, KD, P).transpose(3, 2, 0, 1, 4).reshape(KD, P, 3 * NB * P)
    o["w_out"] = w_out[0].reshape(KD, P, D).transpose(1, 0, 2)
    o["ln_g"], o["ln_b"] = ln_g, ln_b
    return {k: np.ascontiguousarray(v) for k, v in o.items()}


def kernel(**inputs):
    import concourse.bacc as _bacc
    from concourse.bass_utils import run_bass_kernel_spmd as _run

    arrays = lay_out(**{k: np.asarray(v) for k, v in inputs.items()})
    arrays.update(shape_constants())
    nc = _bacc.Bacc("TRN2", target_bir_lowering=False, num_devices=1)
    aps = {n: nc.dram_tensor(f"in_{n}", v.shape, F32, kind="ExternalInput").ap() for n, v in arrays.items()}
    out = nc.dram_tensor("out_0", (L, D), F32, kind="ExternalOutput").ap()
    build_trunk(nc, aps, out)
    r = _run(nc, [{f"in_{n}": v for n, v in arrays.items()}], core_ids=[0])
    return r.results[0]["out_0"].reshape(1, L, D)
```

```python
import math
from contextlib import ExitStack

import numpy as np

import concourse.bass as bass
from concourse import mybir

F32 = mybir.dt.float32
ALU = mybir.AluOpType
ACT = mybir.ActivationFunctionType
AX_X = mybir.AxisListType.X

P = 128
D = 1024
KD = D // P
L = 2048
LC = 256
LT = LC + L
CH = 512
NB = 512 // P
GW = 64
ROWS = L // GW
NKH, NKW = 8, 16
BAND = NKH * GW
HEADS = 8
DH = 64
NDR = 2 * NKH - 1
TOE = 2 * GW - 1
NF = 2 * L
R1 = 64
NPR = R1 // 2
EMB = 33
HID = 64
ALPHA = 2.0 ** 0.25
EPS = 1e-5
MASKED = -1e30
LAT_CHUNKS = [(LC + CH * i, CH) for i in range(L // CH)]
ALL_CHUNKS = [(0, LC)] + LAT_CHUNKS
B_AIN, B_AGATE, B_Q, B_K, B_V, B_BGATE, B_X0, B_X1, B_HV, B_CGATE, B_G = 0, 4, 8, 12, 16, 20, 24, 28, 32, 36, 40


def shape_constants():
    f = {}
    n1 = np.arange(R1)
    kk = np.arange(R1)
    k1, ri = kk % 32, kk // 32
    ang = 2 * np.pi * np.outer(n1, k1) / R1
    one = np.where(ri == 0, np.cos(ang), -np.sin(ang))
    one[:, 0] = 1.0
    one[:, 32] = (-1.0) ** n1
    lat = np.kron(np.eye(2), one[:32])
    f["dft1"] = np.concatenate([lat, lat], 0)
    f["dft1_filter"] = np.kron(np.eye(2), one[np.where(n1 < 32, n1, 95 - n1)])
    inv = np.where(ri == 0, 2 * np.cos(ang), -2 * np.sin(ang))
    inv[:, 0] = 1.0
    inv[:, 32] = (-1.0) ** n1
    f["idft1"] = np.kron(np.eye(2), inv[:32].T) / NF
    n2 = 2 * (np.arange(64) % 32) + np.arange(64) // 32
    k2 = np.arange(64)
    fwd = np.zeros((32, 128, 128))
    inv2 = np.zeros((32, 128, 128))
    for k in range(1, 32):
        th = 2 * np.pi * np.outer(n2, k + 64 * k2) / NF
        c, s = np.cos(th), np.sin(th)
        fwd[k] = np.block([[c, -s], [s, c]])
        inv2[k] = np.block([[c.T, s.T], [-s.T, c.T]])
    h = np.arange(32)
    t0 = 2 * np.pi * np.outer(n2, 64 * h) / NF
    t1 = 2 * np.pi * np.outer(n2, 32 + 64 * h) / NF
    fwd[0, :64, :32], fwd[0, :64, 64:96] = np.cos(t0), -np.sin(t0)
    fwd[0, 64:, 32:64], fwd[0, 64:, 96:] = np.cos(t1), -np.sin(t1)
    fwd[0, :64, 64] = (-1.0) ** n2
    inv2[0, :32, :64], inv2[0, 64:96, :64] = 2 * np.cos(t0).T, -2 * np.sin(t0).T
    inv2[0, 32:64, 64:], inv2[0, 96:, 64:] = 2 * np.cos(t1).T, -2 * np.sin(t1).T
    inv2[0, 0, :64] = 1.0
    inv2[0, 64, :64] = (-1.0) ** n2
    swapped = np.concatenate([inv2[:, 64:], inv2[:, :64]], 1)
    tab = np.concatenate([fwd, inv2, swapped], 2)
    tab = tab.reshape(8, 4, P, 3 * P).transpose(0, 2, 1, 3)
    f["dft2"] = tab[..., :P].reshape(8, P, 4 * P)
    f["idft2"] = tab[..., P:].reshape(8, P, 8 * P)
    kb = np.concatenate([fwd[:, :, :64], fwd[:, :, :64]], 2)
    kb[0, :, 64] = fwd[0, :, 64]
    kc = np.concatenate([fwd[:, :, 64:], -fwd[:, :, 64:]], 2)
    kc[0, :, 0] = 0
    kc[0, :, 64] = 0
    f["dft2_filter"] = np.concatenate([kb, kc], 2).reshape(8, 4, P, 256).transpose(0, 2, 1, 3).reshape(8, P, 1024)
    t = np.arange(L) / np.float32(L)
    a = 2 * np.pi * t[:, None] * np.arange(1, 17)
    f["positions"] = np.concatenate([t[:, None], np.cos(a), np.sin(a)], 1).T
    tt = np.zeros((32, 2, 64))
    for pr in range(32):
        for j in range(2):
            tt[pr, j, :32] = 64 * np.arange(32) + 2 * pr + j
            tt[pr, j, 32:] = 64 * (np.arange(32) + 1) - (2 * pr + j)
    f["neg_time"] = -(tt / L).reshape(32, 128).T
    f["deltas"] = np.abs(np.linspace(math.log(1e-2) / 0.3, math.log(1e-2) / 1.5, 512))[None]
    cols = np.arange(GW)
    start = np.clip(cols - NKW // 2, 0, GW - NKW)
    ok = (cols[None] >= start[:, None]) & (cols[None] < start[:, None] + NKW)
    m = np.where(ok, 0.0, MASKED)
    f["col_mask"] = np.concatenate([m, m], 0)
    f["ident"] = np.eye(P)
    f["flip"] = np.kron(np.eye(2), np.eye(GW)[::-1])
    return {k: np.ascontiguousarray(v, np.float32) for k, v in f.items()}


class Steps:

    def __init__(self, eng, sem, base=0):
        self.eng, self.sem, self.base, self.n = eng, sem, base, 0

    def __call__(self, ins):
        ins.then_inc(self.sem, 1)
        self.n += 1
        self.eng.wait_ge(self.sem, self.base + self.n)


def build_trunk(nc, a, out, debug=False):
    scratch = "ExternalOutput" if debug else "Internal"

    def dram(name, shape):
        return nc.dram_tensor(name, shape, F32, kind=scratch).ap()

    bias_tab = dram("bias_tab", (NB, P, NDR * GW))
    filt_mid = dram("filt_mid", (2, NPR, R1, 512))
    filt_spec = dram("filt_spec", (NB, NPR // 4, P, 4, 2, P))
    fwd_mid = dram("fwd_mid", (NB, P, NPR, P))
    inv_mid = dram("inv_mid", (NB, P, NPR, P))
    yg_dram = dram("yg_dram", (3 * NB, P, L))
    m_dram = dram("m_dram", (L // P, P, KD, P))
    if debug:
        ut_dbg = dram("ut_dbg", (P, KD, LT))
    names = [0]

    def free_name(n):
        names[0] += 1
        return f"{n}_{names[0]}"

    top = ExitStack()

    def sb(ctx, name, shape):
        return ctx.enter_context(nc.sbuf_tensor(free_name(name), shape, F32))

    def ps(ctx, name, shape):
        return ctx.enter_context(nc.psum_tensor(free_name(name), shape, F32))

    def sem(name):
        return top.enter_context(nc.semaphore(name))

    with top:
        ident = sb(top, "ident", [P, P])
        mod = sb(top, "mod", [P, 24, 2])
        decay = sb(top, "decay", [P, 2 * NB, 2])
        gate_row = sb(top, "gate_row", [P, D])

        with ExitStack() as cx:
            WS = 8
            cvec = sb(cx, "cvec", [P, KD, 2])
            bmod = sb(cx, "bmod", [P, 24, 2])
            wm = sb(cx, "wm", [P, WS, D])
            lam = sb(cx, "lam", [P, 2 * NB])
            sp = sb(cx, "sp", [P, 6, 2 * NB])
            toe = sb(cx, "toe", [P, NB, NDR, GW])
            toe_flat = toe[:, :, :, :].rearrange("p a b c -> p (a b c)")
            toe_rows = toe[:, :, :, :].rearrange("p a b c -> p (a b) c")
            mask = sb(cx, "mask", [P, GW])
            flip = sb(cx, "flip", [P, P])
            spread = sb(cx, "spread", [P, KD, P])
            ones = sb(cx, "ones", [P, P])
            pos = sb(cx, "pos", [EMB, L])
            w1 = sb(cx, "w1", [EMB, 2 * HID])
            w2 = sb(cx, "w2", [HID, 2 * HID])
            w3 = sb(cx, "w3", [P, 512])
            bf = sb(cx, "bf", [P, 4])
            arg = sb(cx, "arg", [P, L])
            turns = sb(cx, "turns", [P, L])
            hid1 = sb(cx, "hid1", [P, L])
            hid = sb(cx, "hid", [P, R1, R1])
            negt = sb(cx, "negt", [P, NPR])
            deltas = sb(cx, "deltas", [P, 512])
            d1f = sb(cx, "d1f", [P, P])
            hpair = sb(cx, "hpair", [P, 4, P])
            window = sb(cx, "window", [P, 4, 512])
            filt = sb(cx, "filt", [P, 4, 512])
            mid = sb(cx, "mid", [P, 4, 512])
            mid2 = sb(cx, "mid2", [P, 2, 4, 512])
            d2f = sb(cx, "d2f", [P, 2, 4 * 256])
            spec = sb(cx, "spec", [P, 2, 4, 2, 512])
            lo = ps(cx, "lo", [P, 4, CH])
            hi = ps(cx, "hi", [P, 4, CH])
            TG = 6
            NTG = NB * NDR // TG
            NG = NPR // 4
            small_in, toe_in, f_in = sem("small_in"), sem("toe_in"), sem("f_in")
            wm_in = [sem(f"wm_in{s}") for s in range(WS)]
            (c_ready, mod_mm, mod_done, mod_dv, abs_lam, y_exp, spread_done, row_mm, flip_mm, toe_done, bias_out,
             hid_mm, hid_dv, sin_done, hid_zero, hpair_done, win_done, gen_mm, filt_done, mid_mm, mid_done,
             spec_mm, spec_b_done, spec_c_done) = [sem(n) for n in (
                 "c_ready", "mod_mm", "mod_done", "mod_dv", "abs_lam", "y_exp", "spread_done", "row_mm", "flip_mm", "toe_done",
                 "bias_out", "hid_mm", "hid_dv", "sin_done", "hid_zero", "hpair_done", "win_done", "gen_mm", "filt_done",
                 "mid_mm", "mid_done", "spec_mm", "spec_b_done", "spec_c_done")]
            mid_out = [sem(f"mid_out{s}") for s in range(4)]
            mid_in = [sem("mid_in0"), sem("mid_in1")]
            spec_out = [sem("spec_out0"), sem("spec_out1")]
            MAGIC = 1.5 * 2.0 ** 23
            TWO_PI = 2 * math.pi
            c1 = 6.28125
            c2 = float(np.round((TWO_PI - c1) * 2 ** 21) / 2 ** 21)
            c3 = float(TWO_PI - c1 - c2)
            with nc.Block() as block:
                @block.sync
                def _(sp_):
                    for dst, name in ((pos, "positions"), (w1, "hy_w1"), (bf, "hy_bf"), (w2, "hy_w2"), (w3, "hy_w3"),
                                      (negt, "neg_time"), (d1f, "dft1_filter")):
                        sp_.dma_start(dst[:, :], a[name]).then_inc(f_in, 16)
                    sp_.dma_start(deltas[:, :], bass.AP(tensor=a["deltas"].tensor, offset=0,
                                                        ap=[[0, P], [1, 512]])).then_inc(f_in, 16)
                    sp_.dma_start(cvec[:, :, :], a["cvec"]).then_inc(small_in, 16)
                    sp_.dma_start(bmod[:, :, :], a["bmod"]).then_inc(small_in, 16)
                    for dst, name in ((lam, "lam"), (ident, "ident"), (mask, "col_mask"), (flip, "flip")):
                        sp_.dma_start(dst[:, :], a[name]).then_inc(small_in, 16)
                    with sp_.Fori(0, 24 // WS) as i:
                        for s in range(WS):
                            sp_.wait_ge(mod_mm, WS * i + s + 1)
                            sp_.dma_start(wm[:, s, :], a["w_mod"][WS * i + s]).then_inc(wm_in[s], 16)
                    sp_.wait_ge(toe_done, NTG)
                    for p in range(NB):
                        sp_.dma_start(bias_tab[p], toe[:, p, :, :]).then_inc(bias_out, 16)
                    dst = filt_mid.rearrange("r k (j q) c -> q j (r k) c", j=2)
                    with sp_.Fori(0, NPR // 4) as i:
                        for s in range(4):
                            sp_.wait_ge(mid_done, 4 * i + s + 5)
                            for j in range(2):
                                sp_.dma_start(dst[4 * i + s, j], mid[R1 * j:R1 * (j + 1), s, :]).then_inc(mid_out[s], 16)
                    for s in range(4):
                        sp_.wait_ge(mid_out[s], 32 * (NPR // 4) + 32)
                    with sp_.Fori(0, NG // 2) as i:
                        for s in range(2):
                            g = 2 * i + s
                            sp_.wait_ge(spec_mm, 4 * g + 4)
                            for r in range(2):
                                sp_.dma_start(mid2[R1 * r:R1 * r + R1, s, :, :],
                                              filt_mid[r].rearrange("(g k) n c -> g n k c", k=4)[g]).then_inc(mid_in[s], 16)
                            sp_.dma_start(d2f[:, s, :], a["dft2_filter"][g]).then_inc(mid_in[s], 16)
                    sp_.wait_ge(bias_out, 16 * NB)

                @block.scalar
                def _(act):
                    act.nop().then_inc(mid_done, 4)
                    act.nop().then_inc(spec_c_done, 4)
                    act.wait_ge(small_in, 96)
                    nc.scalar.activation(cvec[:, :, :], cvec[:, :, :], ACT.Silu).then_inc(c_ready, 1)
                    act.wait_ge(hid_dv, 28)
                    nc.scalar.activation(hid1[:, :], arg[:, :], ACT.Sin).then_inc(sin_done, 1)
                    act.wait_ge(hid_dv, 56)
                    act.wait_ge(hid_zero, 1)
                    fw = arg[0:HID, :].rearrange("p (a b) -> p b a", b=R1)
                    nc.scalar.activation(hid[0:HID, :, 0:32], fw, ACT.Sin).then_inc(sin_done, 1)
                    bw = arg[HID:P, :].rearrange("p (a b) -> p b a", b=R1)
                    nc.scalar.activation(hid[HID:P, 1:R1, 32:R1], bw[:, R1 - 1:0:-1, :], ACT.Sin).then_inc(sin_done, 1)
                    nc.scalar.activation(hid[HID:P, 0, 32:R1 - 1], bw[:, 0, 1:32], ACT.Sin).then_inc(sin_done, 1)
                    act.wait_ge(abs_lam, 1)
                    nc.scalar.activation(sp[:, 1, :], sp[:, 0, :], ACT.Exp, scale=-1.0).then_inc(y_exp, 1)
                    act.wait_ge(f_in, 128)
                    with act.Fori(0, NPR // 4) as i:
                        for s in range(4):
                            act.wait_ge(filt_done, 4 * i + s + 1)
                            nc.scalar.activation(window[:, s, :], deltas[:, :], ACT.Exp,
                                                 scale=negt[:, bass.ds(4 * i + s, 1)]).then_inc(win_done, 1)
                        for s in range(4):
                            act.wait_ge(mid_mm, 4 * i + s + 5)
                            act.wait_ge(mid_out[s], 32 * i + 32)
                            nc.scalar.copy(mid[:, s, :], hi[:, s, :]).then_inc(mid_done, 1)
                    with act.Fori(0, NG // 2) as i:
                        for s in range(2):
                            g = 2 * i + s
                            act.wait_ge(spec_out[s], 64 * i + 64)
                            for k in range(4):
                                act.wait_ge(spec_mm, 4 * g + k + 9)
                                nc.scalar.copy(spec[:, s, k, 1, :], hi[:, k, :]).then_inc(spec_c_done, 1)
                            act.wait_ge(spec_b_done, 4 * g + 8)
                            act.wait_ge(spec_c_done, 4 * g + 8)
                            for t in range(NB):
                                act.dma_start(filt_spec[t, g].rearrange("p k b c -> p (k b) c"),
                                              spec[:, s, :, :, t * P:(t + 1) * P].rearrange("p k b c -> p (k b) c")).then_inc(spec_out[s], 16)
                    for s in range(2):
                        act.wait_ge(spec_out[s], 32 * NG + 64)

                @block.gpsimd
                def _(pool):
                    for s in range(4):
                        pool.nop().then_inc(mid_out[s], 32)
                    for s in range(2):
                        pool.nop().then_inc(spec_out[s], 64)
                    for h in range(HEADS):
                        src = bass.AP(tensor=a["rpb"].tensor, offset=h * NDR * TOE, ap=[[1, GW], [TOE, NDR], [1, GW]])
                        pool.dma_start(toe[GW * (h % 2):GW * (h % 2) + GW, h // 2, :, :], src).then_inc(toe_in, 16)
                    nc.gpsimd.memset(hid[:, :, :], 0.0).then_inc(hid_zero, 1)
                    pool.wait_ge(toe_in, 16 * HEADS)
                    pool.wait_ge(sin_done, 4)
                    pairs = hid[:, :, :].rearrange("p (r j) s -> p r (j s)", j=2)
                    with pool.Fori(0, NPR // 4) as i:
                        for s in range(4):
                            pool.wait_ge(gen_mm, 4 * i + s + 1)
                            nc.gpsimd.tensor_copy(hpair[:, s, :].unsqueeze(1), pairs[:, bass.ds(4 * i + s, 1), :]).then_inc(hpair_done, 1)

                @block.tensor
                def _(pe):
                    pe.nop().then_inc(mod_mm, WS)
                    pe.nop().then_inc(gen_mm, 4)
                    pe.nop().then_inc(mid_mm, 4)
                    pe.nop().then_inc(spec_mm, 8)
                    pe.wait_ge(f_in, 128)
                    for c in range(4):
                        mm = pe.matmul(lo[:, c, :], w1[:, :], pos[:, c * CH:(c + 1) * CH], start=True, stop=True)
                    mm.then_inc(hid_mm, 1)

                    def modulation(i):
                        for s in range(WS):
                            pe.wait_ge(wm_in[s], 16 * i + 16)
                            pe.wait_ge(mod_done, WS * i + s + 1)
                            for k in range(KD):
                                mm = pe.matmul(lo[:, s % 2, 0:2], wm[:, s, k * P:(k + 1) * P], cvec[:, k, :],
                                               start=(k == 0), stop=(k == KD - 1))
                            mm.then_inc(mod_mm, 1)
                    pe.wait_ge(sin_done, 1)
                    for c in range(4):
                        mm = pe.matmul(hi[:, c, :], w2[:, :], hid1[0:HID, c * CH:(c + 1) * CH], start=True, stop=True)
                    mm.then_inc(hid_mm, 1)
                    pe.wait_ge(c_ready, 1)
                    pe.wait_ge(hid_dv, 56)
                    with pe.Fori(0, 24 // WS) as i:
                        modulation(i)
                    pe.wait_ge(spread_done, 1)
                    for k in range(KD):
                        mm = pe.matmul(lo[:, 2 + k // 4, (k % 4) * P:(k % 4 + 1) * P], spread[:, k, :], ident[:, :],
                                       start=True, stop=True)
                    mm.then_inc(row_mm, 1)
                    pe.wait_ge(toe_in, 16 * HEADS)
                    for n in range(NTG):
                        if n >= 4:
                            pe.wait_ge(toe_done, n - 3)
                        pe.matmul(hi[:, n % 4, 0:TG * GW], flip[:, :], toe_flat[:, n * TG * GW:(n + 1) * TG * GW],
                                  start=True, stop=True).then_inc(flip_mm, 1)
                    pe.wait_ge(toe_done, NTG)
                    with pe.Fori(0, NPR // 4) as i:
                        def generate(n, s):
                            pe.wait_ge(hpair_done, n + 1)
                            pe.wait_ge(filt_done, n + 1)
                            pe.matmul(lo[:, s, :], hpair[:, s, :], w3[:, :], start=True, stop=True).then_inc(gen_mm, 1)
                        for s in range(4):
                            generate(4 * i + s, s)
                        for s in range(4):
                            pe.wait_ge(filt_done, 4 * i + s + 5)
                            pe.wait_ge(mid_done, 4 * i + s + 1)
                            pe.matmul(hi[:, s, :], d1f[:, :], filt[:, s, :], start=True, stop=True).then_inc(mid_mm, 1)
                    pe.wait_ge(mid_done, NPR + 4)
                    with pe.Fori(0, NG // 2) as i:
                        for s in range(2):
                            g = 2 * i + s
                            pe.wait_ge(mid_in[s], 48 * i + 48)
                            for k in range(4):
                                pe.wait_ge(spec_b_done, 4 * g + k + 1)
                                pe.wait_ge(spec_c_done, 4 * g + k + 1)
                                pe.matmul(lo[:, k, :], d2f[:, s, 256 * k:256 * k + P], mid2[:, s, k, :], start=True, stop=True)
                                pe.matmul(hi[:, k, :], d2f[:, s, 256 * k + P:256 * k + 256], mid2[:, s, k, :],
                                          start=True, stop=True).then_inc(spec_mm, 1)

                @block.vector
                def _(dve):
                    v = nc.vector
                    dve.nop().then_inc(mod_done, 2)
                    dve.nop().then_inc(filt_done, 4)
                    dve.nop().then_inc(spec_b_done, 4)
                    st = Steps(dve, hid_dv)
                    dve.wait_ge(f_in, 128)
                    for layer in range(2):
                        dve.wait_ge(hid_mm, layer + 1)
                        src = (lo, hi)[layer]
                        if layer:
                            dve.wait_ge(sin_done, 1)
                        for c in range(4):
                            x, n = arg[:, c * CH:(c + 1) * CH], turns[:, c * CH:(c + 1) * CH]
                            st(v.tensor_scalar(x, src[:, c, :], bf[:, 2 * layer:2 * layer + 1],
                                               bf[:, 2 * layer + 1:2 * layer + 2], ALU.add, ALU.mult))
                            st(v.tensor_scalar(n, x, 1 / TWO_PI, MAGIC, ALU.mult, ALU.add))
                            st(v.tensor_scalar(n, n, -MAGIC, None, ALU.add))
                            for part in (c1, c2, c3):
                                st(v.scalar_tensor_tensor(x, n, -part, x, ALU.mult, ALU.add))
                            st(v.tensor_scalar(x, x, 3.1415925, -3.1415925, ALU.min, ALU.max))
                    st = Steps(dve, mod_dv)
                    st(v.memset(ones[:, :], 1.0))
                    dve.wait_ge(small_in, 96)
                    st(v.tensor_scalar(sp[:, 2, :], lam[:, :], -1.0, None, ALU.mult))
                    v.tensor_tensor(sp[:, 0, :], lam[:, :], sp[:, 2, :], ALU.max).then_inc(abs_lam, 1)
                    dve.wait_ge(y_exp, 1)
                    st(v.tensor_scalar(sp[:, 3, :], sp[:, 1, :], 2.0, None, ALU.add))
                    st(v.reciprocal(sp[:, 4, :], sp[:, 3, :]))
                    st(v.tensor_tensor(sp[:, 0, :], sp[:, 4, :], sp[:, 1, :], ALU.mult))
                    st(v.tensor_tensor(sp[:, 4, :], sp[:, 0, :], sp[:, 0, :], ALU.mult))
                    st(v.tensor_scalar(sp[:, 5, :], sp[:, 4, :], 1.0 / 17, 1.0 / 15, ALU.mult, ALU.add))
                    for n in (13, 11, 9, 7, 5, 3, 1):
                        st(v.tensor_tensor(sp[:, 5, :], sp[:, 5, :], sp[:, 4, :], ALU.mult))
                        st(v.tensor_scalar(sp[:, 5, :], sp[:, 5, :], 1.0 / n, None, ALU.add))
                    st(v.tensor_tensor(sp[:, 5, :], sp[:, 5, :], sp[:, 0, :], ALU.mult))
                    st(v.tensor_scalar(sp[:, 2, :], sp[:, 2, :], 0.0, None, ALU.max))
                    st(v.scalar_tensor_tensor(sp[:, 3, :], sp[:, 5, :], 2.0, sp[:, 2, :], ALU.mult, ALU.add))
                    st(v.tensor_scalar(decay[:, :, 0], sp[:, 3, :], -8.0, None, ALU.mult))
                    st(v.tensor_scalar(decay[:, :, 1], sp[:, 3, :], 8.0, None, ALU.mult))
                    with dve.Fori(0, 24 // WS) as i:
                        for s in range(WS):
                            dve.wait_ge(mod_mm, WS * i + s + WS + 1)
                            v.tensor_tensor(mod[:, bass.ds(WS * i + s, 1), :], lo[:, s % 2, 0:2].rearrange("p (o c) -> p o c", o=1),
                                            bmod[:, bass.ds(WS * i + s, 1), :], ALU.add).then_inc(mod_done, 1)
                    dve.wait_ge(mod_done, 24 + 2)
                    st(v.tensor_scalar(mod[:, 8:16, :], mod[:, 8:16, :], 1.0, None, ALU.add))
                    for k in range(KD):
                        ins = v.tensor_scalar(spread[:, k, :], ones[:, :], mod[:, 16 + k, 0:1], None, ALU.mult)
                    ins.then_inc(spread_done, 1)
                    dve.wait_ge(row_mm, 1)
                    st(v.tensor_copy(gate_row[:, :].rearrange("p (a b) -> p a b", a=2), lo[:, 2:4, :]))
                    for n in range(NTG):
                        dve.wait_ge(flip_mm, n + 1)
                        v.tensor_tensor(toe_rows[:, n * TG:(n + 1) * TG, :], hi[:, n % 4, 0:TG * GW].rearrange("p (a b) -> p a b", b=GW),
                                        mask[:, :].unsqueeze(1).to_broadcast([P, TG, GW]), ALU.add).then_inc(toe_done, 1)
                    with dve.Fori(0, NPR // 4) as i:
                        for s in range(4):
                            n = 4 * i + s
                            dve.wait_ge(gen_mm, n + 5)
                            dve.wait_ge(win_done, n + 1)
                            dve.wait_ge(mid_mm, n + 1)
                            v.tensor_tensor(filt[:, s, :], lo[:, s, :], window[:, s, :], ALU.mult).then_inc(filt_done, 1)
                    with dve.Fori(0, NG // 2) as i:
                        for s in range(2):
                            dve.wait_ge(spec_out[s], 64 * i + 64)
                            for k in range(4):
                                dve.wait_ge(spec_mm, 8 * i + 4 * s + k + 9)
                                v.tensor_copy(spec[:, s, k, 0, :], lo[:, k, :]).then_inc(spec_b_done, 1)

        main = ExitStack()
        with main:
            ut = sb(main, "ut", [P, KD, LT])

            with ExitStack() as cx:
                xin = sb(cx, "xin", [P, 4, D])
                xn = sb(cx, "xn", [P, 2, D])
                stat = sb(cx, "stat", [P, 4, 18])
                pt = ps(cx, "pt", [P, 2, 2, CH])
                x_in = [sem(f"x_in{s}") for s in range(4)]
                norm_dv, var_done, std_done, xn_done, turn_mm, ut_act, ut_dve = [sem(n) for n in (
                    "norm_dv", "var_done", "std_done", "xn_done", "turn_mm", "ut_act", "ut_dve")]
                NV = 5
                NTILE = LT // P
                ROUNDS = (NTILE - 4) // 4

                def tiles(eng, do):
                    for n in range(4):
                        do(n, n, 1, n < 2, slice(n * P, (n + 1) * P))
                    with eng.Fori(0, ROUNDS) as i:
                        for s in range(4):
                            do(4 * i + s + 4, s, i + 2, 0, bass.ds((4 * i + s + 4) * P, P))
                    for n in range(4 + 4 * ROUNDS, NTILE):
                        do(n, n % 4, n // 4 + 1, 0, slice(n * P, (n + 1) * P))

                with nc.Block() as block:
                    @block.sync
                    def _(sp_):
                        def load(n, s, use, which, col):
                            if isinstance(n, int) and n < 2:
                                src = a["ctx"][n * P:(n + 1) * P]
                            else:
                                src = a["x"].rearrange("(n p) d -> n p d", p=P)[n - 2]
                            if not isinstance(n, int) or n >= 4:
                                sp_.wait_ge(xn_done, n - 3)
                            sp_.dma_start(xin[:, s, :], src).then_inc(x_in[s], 16)
                        tiles(sp_, load)

                    def modulate(eng, n, s, which, col, half, done):
                        eng.wait_ge(turn_mm, n + 3)
                        for k in range(4 * half, 4 * half + 4):
                            src = pt[:, s % 2, half, (k % 4) * P:(k % 4 + 1) * P]
                            dst = ut[:, k, col]
                            scale, shift = mod[:, 8 + k, which:which + 1], mod[:, k, which:which + 1]
                            if half:
                                ins = nc.vector.tensor_scalar(dst, src, scale, shift, ALU.mult, ALU.add)
                            else:
                                ins = nc.scalar.activation(dst, src, ACT.Identity, bias=shift, scale=scale)
                        ins.then_inc(done, 1)

                    @block.vector
                    def _(dve):
                        v = nc.vector
                        dve.nop().then_inc(ut_dve, 2)

                        def normalise(n, s, use, which, col):
                            b = n * NV
                            x, q = xin[:, s, :], stat[:, s, :]
                            dve.wait_ge(x_in[s], 16 * use)
                            v.bn_stats(q[:, 0:6], x[:, 0:512]).then_inc(norm_dv, 1)
                            v.bn_stats(q[:, 6:12], x[:, 512:1024]).then_inc(norm_dv, 1)
                            dve.wait_ge(norm_dv, b + 2)
                            dve.nop(nofuse=True)
                            v.bn_aggr(q[:, 12:14], q[:, 0:12]).then_inc(norm_dv, 1)
                            dve.wait_ge(norm_dv, b + 3)
                            v.tensor_scalar(q[:, 14:15], q[:, 13:14], EPS, None, ALU.add).then_inc(var_done, 1)
                            if not isinstance(n, int):
                                modulate(dve, n - 2, s, 0, bass.ds((n - 2) * P, P), 1, ut_dve)
                            elif n >= 2:
                                modulate(dve, n - 2, s, n < 4, slice((n - 2) * P, (n - 1) * P), 1, ut_dve)
                            dve.wait_ge(std_done, n + 1)
                            v.reciprocal(q[:, 16:17], q[:, 15:16]).then_inc(norm_dv, 1)
                            dve.wait_ge(turn_mm, n + 1)
                            dve.wait_ge(norm_dv, b + 4)
                            v.tensor_scalar(xn[:, s % 2, :], x, q[:, 12:13], q[:, 16:17], ALU.subtract, ALU.mult).then_inc(xn_done, 1)
                            dve.wait_ge(xn_done, n + 1)
                            dve.nop().then_inc(norm_dv, 1)
                        tiles(dve, normalise)
                        for n in range(NTILE - 2, NTILE):
                            modulate(dve, n, n, 0, slice(n * P, (n + 1) * P), 1, ut_dve)

                    @block.scalar
                    def _(act):
                        act.nop().then_inc(ut_act, 2)

                        def tile(n, s, use, which, col):
                            act.wait_ge(var_done, n + 1)
                            nc.scalar.activation(stat[:, s, 15:16], stat[:, s, 14:15], ACT.Sqrt).then_inc(std_done, 1)
                            if not isinstance(n, int):
                                modulate(act, n - 1, s + 1, 0, bass.ds((n - 1) * P, P), 0, ut_act)
                            elif n >= 1:
                                modulate(act, n - 1, s + 1, n < 3, slice((n - 1) * P, n * P), 0, ut_act)
                        tiles(act, tile)
                        modulate(act, NTILE - 1, NTILE - 1, 0, slice((NTILE - 1) * P, NTILE * P), 0, ut_act)

                    @block.tensor
                    def _(pe):
                        pe.nop().then_inc(turn_mm, 2)

                        def tile(n, s, use, which, col):
                            pe.wait_ge(xn_done, n + 1)
                            pe.wait_ge(ut_act, n + 1)
                            pe.wait_ge(ut_dve, n + 1)
                            for k in range(KD):
                                mm = pe.transpose(pt[:, s % 2, k // 4, (k % 4) * P:(k % 4 + 1) * P],
                                                  xn[:, s % 2, k * P:(k + 1) * P], ident[:, :])
                            mm.then_inc(turn_mm, 1)
                        tiles(pe, tile)

            if debug:
                dbg = sem("dbg")
                with nc.Block() as block:
                    @block.sync
                    def _(sp_):
                        sp_.dma_start(ut_dbg, ut[:, :, :]).then_inc(dbg, 16)
                        sp_.wait_ge(dbg, 16)

            def product(pe, bank, w, col, width):
                for k in range(KD):
                    mm = pe.matmul(bank, w[:, k * P:(k + 1) * P], ut[:, k, col:col + width],
                                   start=(k == 0), stop=(k == KD - 1))
                return mm

            with ExitStack() as cx:
                win = sb(cx, "win", [P, 2, D])
                lw = sb(cx, "lw", [P, 4, P])
                lv = sb(cx, "lv", [P, 9])
                X0, X1 = 2, LC + 5
                xin = sb(cx, "a_in", [P, LT + 6])
                xc = sb(cx, "xc", [P, LT])
                sg = sb(cx, "sg", [P, L])
                rg = [sb(cx, f"rg{d}", [P, LT]) for d in range(2)]
                ig = [sb(cx, f"ig{d}", [P, LT]) for d in range(2)]
                th = [sb(cx, f"th{d}", [P, LT]) for d in range(2)]
                h = [sb(cx, f"h{d}", [P, LT]) for d in range(2)]
                pb = ps(cx, "pb", [P, 8, CH])
                w_land = [sem("lru_w0"), sem("lru_w1")]
                lvec_land, lru_mm, bank_read, xc_done, lru_dv, a_done, sq_ready, sq_done, ya_done, ya_out = [
                    sem(n) for n in ("lvec_land", "lru_mm", "bank_read", "xc_done", "lru_dv", "a_done", "sq_ready",
                                     "sq_done", "ya_done", "ya_out")]
                NCH = 29
                NV = 17
                with nc.Block() as block:
                    @block.sync
                    def _(sp_):
                        def load_vectors(t):
                            sp_.dma_start(lw[:, :, :], a["lru_gate"][t]).then_inc(lvec_land, 16)
                            sp_.dma_start(lv[:, :], a["lru_vec"][t]).then_inc(lvec_land, 16)

                        def store(t):
                            sp_.wait_ge(ya_done, t + 2)
                            sp_.dma_start(yg_dram[t], sg[:, :]).then_inc(ya_out, 16)
                        sp_.nop().then_inc(ya_out, 16)
                        for n in range(2):
                            sp_.dma_start(win[:, n, :], a["w_in"][(B_AIN, B_AGATE)[n]]).then_inc(w_land[n], 16)
                        load_vectors(0)
                        with sp_.Fori(0, NB - 1) as t:
                            sp_.wait_ge(lru_mm, NCH * t + 5 + 1)
                            sp_.dma_start(win[:, 0, :], a["w_in"][t + B_AIN + 1]).then_inc(w_land[0], 16)
                            sp_.wait_ge(lru_mm, NCH * t + 9 + 1)
                            sp_.dma_start(win[:, 1, :], a["w_in"][t + B_AGATE + 1]).then_inc(w_land[1], 16)
                            store(t)
                            load_vectors(t + 1)
                        store(NB - 1)
                        sp_.wait_ge(ya_out, 16 * NB + 16)

                    @block.tensor
                    def _(pe):
                        pe.nop().then_inc(lru_mm, 1)
                        with pe.Fori(0, NB) as t:
                            n = 0

                            def bank(width):
                                nonlocal n
                                pe.wait_ge(bank_read, NCH * t + n + 1)
                                n += 1
                                return pb[:, (n - 1) % 8, 0:width]
                            pe.wait_ge(w_land[0], 16 * t + 16)
                            for col, width in ALL_CHUNKS:
                                product(pe, bank(width), win[:, 0, :], col, width).then_inc(lru_mm, 1)
                            pe.wait_ge(w_land[1], 16 * t + 16)
                            for col, width in LAT_CHUNKS:
                                product(pe, bank(width), win[:, 1, :], col, width).then_inc(lru_mm, 1)
                            pe.wait_ge(lvec_land, 32 * t + 32)
                            pe.wait_ge(xc_done, t + 2)
                            for g in range(4):
                                for col, width in ALL_CHUNKS:
                                    pe.matmul(bank(width), lw[:, g, :], xc[:, col:col + width],
                                              start=True, stop=True).then_inc(lru_mm, 1)
                            pe.wait_ge(bank_read, NCH * t + NCH + 8)

                    @block.scalar
                    def _(act):
                        act.nop().then_inc(bank_read, 8)
                        with act.Fori(0, NB) as t:
                            n = 0
                            s = nc.scalar

                            def bank(width):
                                nonlocal n
                                act.wait_ge(lru_mm, NCH * t + n + 2)
                                n += 1
                                return pb[:, (n - 1) % 8, 0:width]
                            act.wait_ge(xc_done, t + 1)
                            for col, width in ALL_CHUNKS:
                                at = X0 if col == 0 else X1 + col - LC
                                s.copy(xin[:, at:at + width], bank(width)).then_inc(bank_read, 1)
                            act.wait_ge(ya_out, 16 * t + 16)
                            for col, width in LAT_CHUNKS:
                                s.activation(sg[:, col - LC:col - LC + width], bank(width), ACT.Silu).then_inc(bank_read, 1)
                            act.wait_ge(lvec_land, 32 * t + 32)
                            act.wait_ge(ya_done, t + 1)
                            for g in range(4):
                                d, which = g // 2, g % 2
                                dst = (rg, ig)[which][d]
                                for col, width in ALL_CHUNKS:
                                    s.activation(dst[:, col:col + width], bank(width), ACT.Sigmoid,
                                                 bias=lv[:, 5 + 2 * which + d:6 + 2 * which + d]).then_inc(bank_read, 1)
                            act.wait_ge(bank_read, NCH * t + NCH + 8)
                            for d in range(2):
                                s.activation(th[d][:, :], rg[d][:, :], ACT.Tanh,
                                             scale=decay[:, bass.ds(2 * t + d, 1), 1]).then_inc(a_done, 1)
                                act.wait_ge(a_done, 4 * t + 2 * d + 1)
                                s.activation(rg[d][:, :], rg[d][:, :], ACT.Exp,
                                             scale=decay[:, bass.ds(2 * t + d, 1), 0]).then_inc(a_done, 1)
                            for d in range(2):
                                act.wait_ge(sq_ready, 2 * t + d + 1)
                                s.activation(th[d][:, :], th[d][:, :], ACT.Sqrt).then_inc(sq_done, 1)

                    @block.vector
                    def _(dve):
                        v = nc.vector
                        dve.nop().then_inc(ya_done, 1)
                        v.memset(xin[:, :], 0.0).then_inc(xc_done, 1)
                        with dve.Fori(0, NB) as t:
                            st = Steps(dve, lru_dv, NV * t)
                            dve.wait_ge(lvec_land, 32 * t + 32)
                            dve.wait_ge(bank_read, NCH * t + 5 + 8)
                            dve.wait_ge(lru_mm, NCH * t + 1)
                            for first, at, width in ((X0, 0, LC), (X1, LC, L)):
                                o = xc[:, at:at + width]
                                for k in range(4):
                                    src = xin[:, first + k - 2:first + k - 2 + width]
                                    if k == 0:
                                        ins = v.tensor_scalar(o, src, lv[:, 0:1], lv[:, 4:5], ALU.mult, ALU.add)
                                    else:
                                        ins = v.scalar_tensor_tensor(o, src, lv[:, k:k + 1], o, ALU.mult, ALU.add)
                                    if k == 3 and at == LC:
                                        ins.then_inc(xc_done, 1)
                                        dve.wait_ge(xc_done, t + 2)
                                    else:
                                        st(ins)
                            for d in range(2):
                                if d == 0:
                                    dve.wait_ge(bank_read, NCH * t + NCH + 8)
                                st(v.tensor_tensor(ig[d][:, :], ig[d][:, :], xc[:, :], ALU.mult))
                                dve.wait_ge(a_done, 4 * t + 2 * d + 2)
                                st(v.tensor_tensor(h[d][:, :], rg[d][:, :], rg[d][:, :], ALU.mult))
                                v.scalar_tensor_tensor(th[d][:, :], h[d][:, :], 1.0, th[d][:, :], ALU.add, ALU.mult).then_inc(sq_ready, 1)
                            dve.wait_ge(sq_done, 2 * t + 1)
                            st(v.tensor_tensor(ig[0][:, :], ig[0][:, :], th[0][:, :], ALU.mult))
                            v.tensor_tensor_scan(h[0][:, :], rg[0][:, :], ig[0][:, :], 0.0, ALU.mult, ALU.add).then_inc(lru_dv, 1)
                            st.n += 1
                            dve.wait_ge(sq_done, 2 * t + 2)
                            dve.wait_ge(sq_ready, 2 * t + 2)
                            ins = v.tensor_tensor(ig[1][:, :], ig[1][:, :], th[1][:, :], ALU.mult)
                            st.n -= 0
                            st(ins)
                            st(v.tensor_tensor_scan(h[1][:, LC - 1::-1], rg[1][:, LC - 1::-1], ig[1][:, LC - 1::-1],
                                                    0.0, ALU.mult, ALU.add))
                            lat = slice(LT - 1, LC - 1, -1)
                            ins = v.tensor_tensor_scan(h[1][:, lat], rg[1][:, lat], ig[1][:, lat],
                                                       h[1][:, 0:1], ALU.mult, ALU.add)
                            ins.then_inc(lru_dv, 1)
                            st.n += 1
                            dve.wait_ge(lru_dv, NV * t + 16)
                            st(v.tensor_tensor(h[0][:, LC:LT], h[0][:, LC:LT], h[1][:, LC:LT], ALU.add))
                            v.tensor_tensor(sg[:, :], sg[:, :], h[0][:, LC:LT], ALU.mult).then_inc(ya_done, 1)
                            assert st.n == NV, st.n

            with ExitStack() as cx:
                win = sb(cx, "win", [P, 4, D])
                qs = sb(cx, "qs", [P, L])
                kt = sb(cx, "kt", [P, LT])
                vt = sb(cx, "vt", [P, LT])
                NVB = LT // P + L // P - 1
                vk = sb(cx, "vk", [P, NVB, P])
                sg = sb(cx, "sg", [P, L])
                bt = sb(cx, "bt", [P, NDR * GW])
                qbd = sb(cx, "qbd", [P, 2, P])
                ss = sb(cx, "ss", [P, 2, BAND])
                pr = sb(cx, "pr", [P, 2, BAND + LC])
                prt = sb(cx, "prt", [P, 2, BAND + LC])
                on = sb(cx, "on", [P, 2, P])
                row_stat = sb(cx, "row_stat", [P, 2, 8])
                psc = [ps(cx, f"psc{s}", [P, 2, CH]) for s in range(2)]
                ppt = ps(cx, "ppt", [P, 2, CH])
                po = ps(cx, "po", [P, CH])
                pot = ps(cx, "pot", [P, CH])
                w_land = [sem(f"att_w{n}") for n in range(4)]
                (bt_land, att_mm, att_read, vk_mm, vk_read, qbd_done, s_mm, ss_done, nm_done, exp_done, att_dv, p_mm,
                 pt_read_dve, pt_read_act, pv_mm, on_done, ot_mm, yb_done, yb_out) = [sem(n) for n in (
                     "bt_land", "att_mm", "att_read", "vk_mm", "vk_read", "qbd_done", "s_mm", "ss_done", "nm_done", "exp_done",
                     "att_dv", "p_mm", "pt_read_dve", "pt_read_act", "pv_mm", "on_done", "ot_mm", "yb_done", "yb_out")]
                BLOCKS = (B_V, B_Q, B_K, B_BGATE)
                CHUNKS = (ALL_CHUNKS, LAT_CHUNKS, ALL_CHUNKS, LAT_CHUNKS)
                NCH = sum(len(c) for c in CHUNKS)
                ENDS = np.cumsum([len(c) for c in CHUNKS]).tolist()
                NVG = (NVB + 3) // 4

                def band(r):
                    return min(max(r - NKH // 2, 0), ROWS - NKH)

                def v_block(r0, c):
                    return 2 + r0 // 2 + c if r0 % 2 == 0 else 2 + L // P + r0 // 2 + c

                def v_column(n):
                    return n * P if n < LT // P else LC + GW + (n - LT // P) * P
                with nc.Block() as block:
                    @block.sync
                    def _(sp_):
                        def store(t):
                            sp_.wait_ge(yb_done, ROWS * t + ROWS + 1)
                            sp_.dma_start(yg_dram[t + NB], sg[:, :]).then_inc(yb_out, 16)
                        sp_.nop().then_inc(yb_out, 16)
                        for n in range(4):
                            sp_.dma_start(win[:, n, :], a["w_in"][BLOCKS[n]]).then_inc(w_land[n], 16)
                        sp_.dma_start(bt[:, :], bias_tab[0]).then_inc(bt_land, 16)
                        with sp_.Fori(0, NB - 1) as t:
                            for n in range(4):
                                sp_.wait_ge(att_mm, NCH * t + ENDS[n])
                                sp_.dma_start(win[:, n, :], a["w_in"][t + BLOCKS[n] + 1]).then_inc(w_land[n], 16)
                            store(t)
                            sp_.dma_start(bt[:, :], bias_tab[t + 1]).then_inc(bt_land, 16)
                        store(NB - 1)
                        sp_.wait_ge(yb_out, 16 * NB + 16)

                    @block.gpsimd
                    def _(pool):
                        nc.gpsimd.memset(qbd[:, :, :], 0.0).then_inc(qbd_done, 2)
                        pool.wait_ge(qbd_done, 2)
                        with pool.Fori(0, NB) as t:
                            pool.wait_ge(att_read, NCH * t + ENDS[1] + 4)
                            for r in range(ROWS):
                                pool.wait_ge(s_mm, ROWS * t + r + 1)
                                for h in range(2):
                                    x = slice(DH * h, DH * h + DH)
                                    pool.nop(nofuse=True)
                                    nc.gpsimd.tensor_copy(qbd[x, r % 2, x], qs[x, r * GW:(r + 1) * GW]).then_inc(qbd_done, 1)

                    @block.tensor
                    def _(pe):
                        pe.nop().then_inc(s_mm, 2)
                        pe.nop().then_inc(p_mm, 2)
                        pe.nop().then_inc(pv_mm, 2)
                        pe.nop().then_inc(ot_mm, 2)
                        with pe.Fori(0, NB) as t:
                            n = 0
                            for b in range(4):
                                pe.wait_ge(w_land[b], 16 * t + 16)
                                for col, width in CHUNKS[b]:
                                    if n < 4:
                                        pe.wait_ge(exp_done, 2 * ROWS * t + 4)
                                        pe.wait_ge(ss_done, ROWS * t + 2)
                                    pe.wait_ge(att_read, NCH * t + n + 1 if n >= 4 else NCH * t + 4)
                                    product(pe, psc[n % 4 // 2][:, n % 2, 0:width], win[:, b, :], col, width).then_inc(att_mm, 1)
                                    n += 1
                            pe.wait_ge(pt_read_dve, ROWS * t + 1)
                            pe.wait_ge(pt_read_act, ROWS * t + 1)
                            pe.wait_ge(att_read, NCH * t + NCH + 4)
                            for g in range(NVG):
                                if g >= 2:
                                    pe.wait_ge(vk_read, NVG * t + g - 1)
                                for n in range(4 * g, min(4 * g + 4, NVB)):
                                    c = v_column(n)
                                    mm = pe.transpose(ppt[:, g % 2, (n % 4) * P:(n % 4 + 1) * P], vt[:, c:c + P], ident[:, :])
                                mm.then_inc(vk_mm, 1)

                            def scores(r):
                                i = ROWS * t + r
                                pe.wait_ge(qbd_done, 2 * i + 4)
                                pe.wait_ge(ss_done, i + 1)
                                pe.wait_ge(exp_done, 2 * i + 2)
                                c = LC + band(r) * GW
                                pe.matmul(psc[r % 2][:, 0, :], qbd[:, r % 2, :], kt[:, c:c + BAND], start=True, stop=True)
                                pe.matmul(psc[r % 2][:, 1, 0:LC], qbd[:, r % 2, :], kt[:, 0:LC], start=True, stop=True).then_inc(s_mm, 1)

                            def turn(r):
                                i = ROWS * t + r
                                pe.wait_ge(exp_done, 2 * i + 6)
                                pe.wait_ge(pt_read_dve, i + 1)
                                pe.wait_ge(pt_read_act, i + 1)
                                for c in range(6):
                                    mm = pe.transpose(ppt[:, c // 4, (c % 4) * P:(c % 4 + 1) * P],
                                                      pr[:, r % 2, c * P:(c + 1) * P], ident[:, :])
                                mm.then_inc(p_mm, 1)

                            def values(r):
                                i = ROWS * t + r
                                pe.wait_ge(pt_read_dve, i + 2)
                                pe.wait_ge(pt_read_act, i + 2)
                                pe.wait_ge(on_done, i + 1)
                                for c in range(6):
                                    b = v_block(band(r), c) if c < 4 else c - 4
                                    mm = pe.matmul(po[:, 0:P], prt[:, r % 2, c * P:(c + 1) * P], vk[:, b, :],
                                                   start=(c == 0), stop=(c == 5))
                                mm.then_inc(pv_mm, 1)

                            def turn_output(r):
                                i = ROWS * t + r
                                pe.wait_ge(on_done, i + 2)
                                pe.wait_ge(yb_done, i + 1)
                                pe.transpose(pot[:, 0:P], on[:, r % 2, :], ident[:, :]).then_inc(ot_mm, 1)
                            scores(0)
                            scores(1)
                            pe.wait_ge(vk_read, NVG * t + NVG)
                            for r in range(ROWS):
                                turn(r)
                                if r + 2 < ROWS:
                                    scores(r + 2)
                                values(r)
                                if r:
                                    turn_output(r - 1)
                            turn_output(ROWS - 1)

                    @block.scalar
                    def _(act):
                        s = nc.scalar
                        act.nop().then_inc(att_read, 4)
                        act.nop().then_inc(exp_done, 4)
                        act.nop().then_inc(pt_read_act, 1)
                        with act.Fori(0, NB) as t:
                            n = 0
                            act.wait_ge(pv_mm, ROWS * t + 2)
                            act.wait_ge(s_mm, ROWS * t + 2)
                            for b in range(4):
                                for col, width in CHUNKS[b]:
                                    act.wait_ge(att_mm, NCH * t + n + 1)
                                    src = psc[n % 4 // 2][:, n % 2, 0:width]
                                    if b == 0:
                                        ins = s.copy(vt[:, col:col + width], src)
                                    elif b == 1:
                                        ins = s.mul(qs[:, col - LC:col - LC + width], src, DH ** -0.5)
                                    elif b == 2:
                                        ins = s.copy(kt[:, col:col + width], src)
                                    else:
                                        if col == LC:
                                            act.wait_ge(yb_out, 16 * t + 16)
                                        ins = s.activation(sg[:, col - LC:col - LC + width], src, ACT.Silu)
                                    ins.then_inc(att_read, 1)
                                    n += 1
                            for g in range(NVG):
                                act.wait_ge(vk_mm, NVG * t + g + 1)
                                m = min(4, NVB - 4 * g)
                                s.copy(vk[:, 4 * g:4 * g + m, :], ppt[:, g % 2, 0:m * P].rearrange("p (a b) -> p a b", b=P)).then_inc(vk_read, 1)

                            def exps(r):
                                i = ROWS * t + r
                                act.wait_ge(nm_done, i + 1)
                                act.wait_ge(p_mm, i + 1)
                                q = row_stat[:, r % 2, :]
                                s.activation(pr[:, r % 2, 0:BAND], ss[:, r % 2, :], ACT.Exp, bias=q[:, 2:3],
                                             accum_out=q[:, 3:4]).then_inc(exp_done, 1)
                                s.activation(pr[:, r % 2, BAND:BAND + LC], psc[r % 2][:, 1, 0:LC], ACT.Exp, bias=q[:, 2:3],
                                             accum_out=q[:, 4:5]).then_inc(exp_done, 1)
                            exps(0)
                            exps(1)
                            for r in range(ROWS):
                                i = ROWS * t + r
                                act.wait_ge(p_mm, i + 3)
                                act.wait_ge(pv_mm, i + 1)
                                s.copy(prt[:, r % 2, BAND:BAND + LC], ppt[:, 1, 0:LC]).then_inc(pt_read_act, 1)
                                if r + 2 < ROWS:
                                    exps(r + 2)

                    @block.vector
                    def _(dve):
                        v = nc.vector
                        dve.nop().then_inc(ss_done, 2)
                        dve.nop().then_inc(pt_read_dve, 1)
                        dve.nop().then_inc(on_done, 1)
                        dve.nop().then_inc(yb_done, 1)
                        NV = 3 * ROWS
                        with dve.Fori(0, NB) as t:
                            st = Steps(dve, att_dv, NV * t)

                            def maxima(r):
                                i = ROWS * t + r
                                q = row_stat[:, r % 2, :]
                                dve.wait_ge(s_mm, i + 3)
                                dve.wait_ge(exp_done, 2 * i + 2)
                                off = (band(r) - r + NKH - 1) * GW
                                dve.nop(nofuse=True)
                                v.tensor_tensor_reduce(ss[:, r % 2, :], psc[r % 2][:, 0, :], bt[:, off:off + BAND], 1.0,
                                                       -3e38, ALU.add, ALU.max, q[:, 0:1]).then_inc(ss_done, 1)
                                st(v.tensor_reduce(q[:, 1:2], psc[r % 2][:, 1, 0:LC], AX_X, ALU.max))
                                dve.wait_ge(ss_done, i + 3)
                                v.tensor_scalar(q[:, 2:3], q[:, 0:1], q[:, 1:2], -1.0, ALU.max, ALU.mult).then_inc(nm_done, 1)

                            def gated(r):
                                i = ROWS * t + r
                                dve.wait_ge(ot_mm, i + 3)
                                for h in range(2):
                                    x = slice(DH * h, DH * h + DH)
                                    o = sg[x, r * GW:(r + 1) * GW]
                                    ins = v.tensor_tensor(o, pot[x, x], o, ALU.mult)
                                ins.then_inc(yb_done, 1)
                            dve.wait_ge(att_read, NCH * t + NCH + 4)
                            dve.wait_ge(bt_land, 16 * t + 16)
                            maxima(0)
                            maxima(1)
                            for r in range(ROWS):
                                i = ROWS * t + r
                                q = row_stat[:, r % 2, :]
                                dve.wait_ge(p_mm, i + 3)
                                dve.wait_ge(pv_mm, i + 1)
                                v.tensor_copy(prt[:, r % 2, 0:BAND], ppt[:, 0, :]).then_inc(pt_read_dve, 1)
                                dve.wait_ge(exp_done, 2 * i + 6)
                                st(v.tensor_tensor(q[:, 5:6], q[:, 3:4], q[:, 4:5], ALU.add))
                                st(v.reciprocal(q[:, 6:7], q[:, 5:6]))
                                if r + 2 < ROWS:
                                    maxima(r + 2)
                                dve.wait_ge(pv_mm, i + 3)
                                dve.wait_ge(ot_mm, i + 1)
                                v.tensor_scalar(on[:, r % 2, :], po[:, 0:P], q[:, 6:7], None, ALU.mult).then_inc(on_done, 1)
                                if r:
                                    gated(r - 1)
                            gated(ROWS - 1)
                            assert st.n == NV, st.n

            with ExitStack() as cx:
                win = sb(cx, "win", [P, 4, D])
                hv = sb(cx, "hv", [P, 13])
                pad = [sb(cx, f"pad{n}", [P, L + 2]) for n in range(3)]
                w = sb(cx, "w", [P, L])
                x0c = pad[1][:, 0:L]
                sg = sb(cx, "sg", [P, L])
                wt = sb(cx, "wt", [P, 16, P])
                flat = wt[:, :, :].rearrange("p a b -> p (a b)")
                sent = sb(cx, "sent", [P, NPR, P])
                x1c = sent[:, 0:16, :].rearrange("p a b -> p (a b)")
                vc = sent[:, 16:32, :].rearrange("p a b -> p (a b)")
                got = sb(cx, "got", [P, NPR, P])
                spec = sb(cx, "spec", [P, 2, 4, 2, P])
                tabf = sb(cx, "tabf", [P, 2, 4, P])
                tabi = sb(cx, "tabi", [P, 2, 4, 2 * P])
                prd = sb(cx, "prd", [P, 2, 2, 4, P])
                d1 = sb(cx, "d1", [P, P])
                d1i = sb(cx, "d1i", [P, R1])
                pb = ps(cx, "pb", [P, 4, CH])
                pf = ps(cx, "pf", [P, 4, CH])
                w_land = [sem(f"hy_w{n}") for n in range(4)]
                tabf_land, spec_land, tabi_land = [[sem(f"{n}{s}") for s in range(2)] for n in ("tabf_land", "spec_land", "tabi_land")]
                (hd_land, hv_land, hy_mm, hy_read, hy_dv, w_done, wt_mm, wt_read, s1_mm, s1_act, s1_dve, x1_out, x2_land, s2_mm, prd_done,
                 g_mm, g_read, inv_out, vf_land, fin_mm, fin_done, yc_done, yc_out) = [sem(n) for n in (
                     "hd_land", "hv_land", "hy_mm", "hy_read", "hy_dv", "w_done", "wt_mm", "wt_read", "s1_mm", "s1_act", "s1_dve", "x1_out",
                     "x2_land", "s2_mm", "prd_done", "g_mm", "g_read", "inv_out", "vf_land", "fin_mm", "fin_done", "yc_done", "yc_out")]
                BLOCKS = (B_HV, B_X1, B_X0, B_CGATE)
                C_W, C_FWD = 10, 13
                NG = NPR // 4
                HV, HV_PAD = 11, 7
                with nc.Block() as block:
                    @block.sync
                    def _(sp_):
                        sp_.nop().then_inc(yc_out, 16)
                        sp_.nop().then_inc(inv_out, 64)
                        sp_.dma_start(d1[:, :], a["dft1"]).then_inc(hd_land, 16)
                        sp_.dma_start(d1i[:, :], a["idft1"]).then_inc(hd_land, 16)
                        for n in range(4):
                            sp_.dma_start(win[:, n, :], a["w_in"][BLOCKS[n]]).then_inc(w_land[n], 16)
                        sp_.dma_start(hv[:, :], a["hy_vec"][0]).then_inc(hv_land, 16)

                        def turn_forward(t):
                            sp_.wait_ge(s1_act, 4 * t + 4)
                            sp_.wait_ge(s1_dve, 4 * t + 4)
                            for b in range(4):
                                o = 2 * (b % 2) + b // 2
                                dst = fwd_mid[t][32 * o:32 * o + 32].rearrange("q k c -> k q c")
                                sp_.dma_start(dst, sent[32 * b:32 * b + 32, :, :]).then_inc(x1_out, 16)
                            sp_.wait_ge(x1_out, 64 * t + 64)
                            sp_.dma_start(got[:, :, :], fwd_mid[t]).then_inc(x2_land, 16)

                        def tables(t, g):
                            sp_.dma_start(tabf[:, g % 2, :, :].rearrange("p k c -> p (k c)"), a["dft2"][g]).then_inc(tabf_land[g % 2], 16)

                        def spectrum(t, g):
                            sp_.dma_start(spec[:, g % 2, :, :, :].rearrange("p k b c -> p (k b c)"),
                                          filt_spec[t, g].rearrange("p k b c -> p (k b c)")).then_inc(spec_land[g % 2], 16)

                        def inverse_tables(t, g):
                            sp_.dma_start(tabi[:, g % 2, :, :].rearrange("p k c -> p (k c)"), a["idft2"][g]).then_inc(tabi_land[g % 2], 16)

                        def next_groups(t, last):
                            for g in range(NG):
                                if g + 2 >= NG and last:
                                    break
                                ahead = (t, g + 2) if g + 2 < NG else (t + 1, g + 2 - NG)
                                for left, count, load in ((s2_mm, 1, tables), (prd_done, 1, spectrum), (g_mm, 3, inverse_tables)):
                                    sp_.wait_ge(left, NG * t + g + count)
                                    load(*ahead)

                        def turn_back(t):
                            sp_.wait_ge(g_read, NG * t + NG)
                            for b in range(4):
                                o = 2 * (b % 2) + b // 2
                                dst = inv_mid[t][32 * o:32 * o + 32].rearrange("k q c -> q k c")
                                sp_.dma_start(dst, sent[32 * b:32 * b + 32, :, :]).then_inc(inv_out, 16)
                            sp_.wait_ge(inv_out, 64 * t + 128)
                            sp_.dma_start(got[:, :, :], inv_mid[t]).then_inc(vf_land, 16)

                        def store(t):
                            sp_.wait_ge(yc_done, t + 2)
                            sp_.dma_start(yg_dram[t + 2 * NB], sg[:, :]).then_inc(yc_out, 16)
                        for g in range(2):
                            for load in (tables, spectrum, inverse_tables):
                                load(0, g)
                        with sp_.Fori(0, NB - 1) as t:
                            for n, step in ((0, None), (1, turn_forward), (2, turn_back), (3, store)):
                                sp_.wait_ge(hy_mm, 16 * t + 4 * n + 4)
                                sp_.dma_start(win[:, n, :], a["w_in"][t + BLOCKS[n] + 1]).then_inc(w_land[n], 16)
                                if n == 2:
                                    next_groups(t, False)
                                if step:
                                    step(t)
                            sp_.dma_start(hv[:, :], a["hy_vec"][t + 1]).then_inc(hv_land, 16)
                        turn_forward(NB - 1)
                        next_groups(NB - 1, True)
                        turn_back(NB - 1)
                        store(NB - 1)
                        sp_.wait_ge(yc_out, 16 * NB + 16)

                    @block.tensor
                    def _(pe):
                        pe.nop().then_inc(g_mm, 2)
                        pe.wait_ge(hd_land, 32)
                        with pe.Fori(0, NB) as t:
                            def chunks(first, end):
                                for n in range(first, end):
                                    if n % 4 == 0:
                                        pe.wait_ge(w_land[n // 4], 16 * t + 16)
                                    pe.wait_ge(hy_read, 16 * t + n + 1)
                                    product(pe, pb[:, n % 4, :], win[:, n // 4, :], *LAT_CHUNKS[n % 4]).then_inc(hy_mm, 1)
                            chunks(0, C_W)
                            pe.wait_ge(w_done, t + 2)
                            pe.wait_ge(fin_done, 4 * t + 4)
                            for g in range(16):
                                mm = pe.transpose(pf[:, g // 4, (g % 4) * P:(g % 4 + 1) * P], w[:, g * P:(g + 1) * P], ident[:, :])
                                if g % 4 == 3:
                                    mm.then_inc(wt_mm, 1)
                            pe.wait_ge(wt_read, 4 * t + 4)
                            for q in range(4):
                                if q >= 2:
                                    pe.wait_ge(s1_act, 4 * t + q - 1)
                                    pe.wait_ge(s1_dve, 4 * t + q - 1)
                                for j in range(2):
                                    for g in range(4):
                                        x = slice(R1 * j, R1 * j + R1)
                                        mm = pe.matmul(pf[:, 2 * (q % 2) + j, g * P:(g + 1) * P], d1[x, :], wt[x, 4 * q + g, :],
                                                       start=True, stop=True)
                                mm.then_inc(s1_mm, 1)

                            def forward(g):
                                pe.wait_ge(tabf_land[g % 2], 16 * (NG // 2) * t + 16 * (g // 2) + 16)
                                if g >= 2:
                                    pe.wait_ge(prd_done, NG * t + g - 1)
                                for k in range(4):
                                    mm = pe.matmul(pf[:, g % 2, k * P:(k + 1) * P], tabf[:, g % 2, k, :], got[:, 4 * g + k, :],
                                                   start=True, stop=True)
                                mm.then_inc(s2_mm, 1)

                            def inverse(g):
                                pe.wait_ge(prd_done, NG * t + g + 1)
                                pe.wait_ge(tabi_land[g % 2], 16 * (NG // 2) * t + 16 * (g // 2) + 16)
                                if g >= 2:
                                    pe.wait_ge(g_read, NG * t + g - 1)
                                for k in range(4):
                                    o = pf[:, 2 + g % 2, k * P:(k + 1) * P]
                                    pe.matmul(o, tabi[:, g % 2, k, 0:P], prd[:, g % 2, 0, k, :], start=True, stop=False)
                                    mm = pe.matmul(o, tabi[:, g % 2, k, P:2 * P], prd[:, g % 2, 1, k, :], start=False, stop=True)
                                mm.then_inc(g_mm, 1)
                            chunks(C_W, C_FWD)
                            pe.wait_ge(s1_act, 4 * t + 4)
                            pe.wait_ge(s1_dve, 4 * t + 4)
                            pe.wait_ge(x2_land, 16 * t + 16)
                            forward(0)
                            for g in range(NG):
                                if g + 1 < NG:
                                    forward(g + 1)
                                inverse(g)
                            chunks(C_FWD, 16)
                            pe.wait_ge(g_read, NG * t + NG)
                            pe.wait_ge(vf_land, 16 * t + 16)
                            for q in range(NPR):
                                mm = pe.matmul(pf[:, q // 8, (q % 8) * R1:(q % 8 + 1) * R1], got[:, q, :], d1i[:, :], start=True, stop=True)
                                if q % 8 == 7:
                                    mm.then_inc(fin_mm, 1)

                    @block.scalar
                    def _(act):
                        s = nc.scalar
                        act.nop().then_inc(hy_read, 4)
                        with act.Fori(0, NB) as t:
                            act.wait_ge(w_done, t + 1)

                            def chunks(first, end):
                                for n in range(first, end):
                                    act.wait_ge(hy_mm, 16 * t + n + 1)
                                    c = n % 4 * CH
                                    if n == 4:
                                        act.wait_ge(yc_done, t + 1)
                                    if n == 8:
                                        act.wait_ge(hy_dv, HV * t + HV_PAD - 2)
                                    if n == 12:
                                        act.wait_ge(yc_out, 16 * t + 16)
                                    if n < 12:
                                        ins = s.copy(pad[n // 4][:, 1 + c:1 + c + CH], pb[:, n % 4, :])
                                    else:
                                        ins = s.activation(sg[:, c:c + CH], pb[:, n % 4, :], ACT.Silu)
                                    ins.then_inc(hy_read, 1)
                            chunks(0, C_W)
                            for g in range(4):
                                act.wait_ge(wt_mm, 4 * t + g + 1)
                                s.copy(wt[:, 4 * g:4 * g + 4, :], pf[:, g, :].rearrange("p (a b) -> p a b", b=P)).then_inc(wt_read, 1)
                            act.wait_ge(inv_out, 64 * t + 64)
                            pairs = sent[:, :, :].rearrange("p (g j) c -> p g j c", j=2)
                            for q in range(4):
                                act.wait_ge(s1_mm, 4 * t + q + 1)
                                s.copy(pairs[:, 4 * q:4 * q + 4, 0, :], pf[:, 2 * (q % 2), :].rearrange("p (a b) -> p a b", b=P)).then_inc(s1_act, 1)
                            chunks(C_W, C_FWD)
                            act.wait_ge(x1_out, 64 * t + 64)
                            for g in range(NG):
                                act.wait_ge(g_mm, NG * t + g + 3)
                                s.copy(sent[:, 4 * g:4 * g + 4, :], pf[:, 2 + g % 2, :].rearrange("p (a b) -> p a b", b=P)).then_inc(g_read, 1)
                            chunks(C_FWD, 16)

                    @block.vector
                    def _(dve):
                        v = nc.vector
                        dve.nop().then_inc(yc_done, 1)
                        dve.nop().then_inc(w_done, 1)
                        dve.nop().then_inc(fin_done, 4)
                        for n in range(3):
                            v.memset(pad[n][:, 0:1], 0.0).then_inc(hy_dv, 1)
                            v.memset(pad[n][:, L + 1:L + 2], 0.0).then_inc(hy_dv, 1)
                        v.memset(w[:, 0:1], 0.0).then_inc(hy_dv, 1)
                        dve.wait_ge(hy_dv, HV_PAD)
                        with dve.Fori(0, NB) as t:
                            st = Steps(dve, hy_dv, HV * t + 7)
                            dve.wait_ge(hv_land, 16 * t + 16)

                            def conv3(dst, src, taps, bias):
                                st(v.tensor_scalar(dst, src[:, 0:L], hv[:, taps:taps + 1], hv[:, bias:bias + 1], ALU.mult, ALU.add))
                                for k in (1, 2):
                                    st(v.scalar_tensor_tensor(dst, src[:, k:k + L], hv[:, taps + k:taps + k + 1], dst, ALU.mult, ALU.add))
                            dve.wait_ge(hy_read, 16 * t + 4 + 4)
                            dve.wait_ge(inv_out, 64 * t + 64)
                            conv3(vc, pad[0], 6, 11)
                            dve.wait_ge(hy_read, 16 * t + 8 + 4)
                            conv3(x1c, pad[1], 3, 10)
                            v.tensor_tensor(w[:, :].rearrange("p (n2 n1) -> p n1 n2", n2=R1), x1c.rearrange("p (n1 n2) -> p n1 n2", n2=R1),
                                            vc.rearrange("p (n1 n2) -> p n1 n2", n2=R1), ALU.mult).then_inc(w_done, 1)
                            pairs = sent[:, :, :].rearrange("p (g j) c -> p g j c", j=2)
                            for q in range(4):
                                dve.wait_ge(s1_mm, 4 * t + q + 1)
                                v.tensor_copy(pairs[:, 4 * q:4 * q + 4, 1, :], pf[:, 2 * (q % 2) + 1, :].rearrange("p (a b) -> p a b", b=P)).then_inc(s1_dve, 1)
                            for g in range(NG):
                                dve.wait_ge(s2_mm, NG * t + g + 1)
                                dve.wait_ge(g_mm, NG * t + g + 1)
                                dve.wait_ge(spec_land[g % 2], 16 * (NG // 2) * t + 16 * (g // 2) + 16)
                                x = pf[:, g % 2, :].rearrange("p (a b) -> p a b", b=P)
                                for b in range(2):
                                    ins = v.tensor_tensor(prd[:, g % 2, b, :, :], x, spec[:, g % 2, :, b, :], ALU.mult)
                                ins.then_inc(prd_done, 1)
                                if g == NG - 1:
                                    conv3(x0c, pad[2], 0, 9)
                            dve.wait_ge(w_done, t + 2)
                            for q in range(4):
                                dve.wait_ge(fin_mm, 4 * t + q + 1)
                                y = flat.rearrange("p (n1 n2) -> p n2 n1", n2=R1)[:, 16 * q:16 * q + 16, :]
                                wv = w[:, CH * q:CH * q + CH].rearrange("p (n2 n1) -> p n2 n1", n1=32)
                                v.scalar_tensor_tensor(y, wv, hv[:, 12:13], pf[:, q, :].rearrange("p (a b) -> p a b", b=32),
                                                       ALU.mult, ALU.add).then_inc(fin_done, 1)
                            dve.wait_ge(fin_done, 4 * t + 8)
                            st(v.tensor_tensor(flat, flat, x0c, ALU.mult))
                            st(v.memset(pad[1][:, 0:1], 0.0))
                            dve.wait_ge(hy_read, 16 * t + 16 + 4)
                            v.tensor_tensor(sg[:, :], sg[:, :], flat, ALU.mult).then_inc(yc_done, 1)
                            assert st.n == HV, st.n

            with ExitStack() as cx:
                win = sb(cx, "win", [P, 3, D])
                wb = sb(cx, "wb", [P, 3, 4 * P])
                yg = sb(cx, "yg", [P, 3 * NB, L])
                sig = sb(cx, "sig", [P, 2, CH])
                tmp = sb(cx, "tmp", [P, CH])
                m = sb(cx, "m", [P, 4, CH])
                pg = ps(cx, "pg", [P, 4, CH])
                pr_ = ps(cx, "pr", [P, 4, CH])
                w_land = [sem(f"mg_w{b}") for b in range(3)]
                yg_land = [sem(f"yg_land{b}") for b in range(3)]
                mg_mm, br_mm, sig_done, br_read, mg_dv, m_done = [sem(n) for n in (
                    "mg_mm", "br_mm", "sig_done", "br_read", "mg_dv", "m_done")]
                m_out = [sem(f"m_out{c}") for c in range(4)]
                with nc.Block() as block:
                    @block.sync
                    def _(sp_):
                        def load(j, b):
                            sp_.dma_start(win[:, b, :], a["w_in"][j + B_G + KD * b]).then_inc(w_land[b], 16)
                            sp_.dma_start(wb[:, b, :], a["w_branch"][j][:, b * 4 * P:(b + 1) * 4 * P]).then_inc(w_land[b], 16)

                        def store(j):
                            for c in range(4):
                                sp_.wait_ge(m_done, 4 * j + c + 1)
                                sp_.dma_start(m_dram[4 * c:4 * c + 4, :, bass.ds(j, 1), :].rearrange("n p o c -> p n (o c)"),
                                              m[:, c, :].rearrange("p (n c) -> p n c", c=P)).then_inc(m_out[c], 16)
                        for c in range(4):
                            sp_.nop().then_inc(m_out[c], 16)
                        for b in range(3):
                            load(0, b)
                            for k in range(NB):
                                sp_.dma_start(yg[:, NB * b + k, :], yg_dram[NB * b + k]).then_inc(yg_land[b], 16)
                        with sp_.Fori(0, KD - 1) as j:
                            for b in range(3):
                                sp_.wait_ge(br_mm, 12 * j + 4 * b + 4)
                                load(j + 1, b)
                            store(j)
                        store(KD - 1)
                        for c in range(4):
                            sp_.wait_ge(m_out[c], 16 * KD + 16)

                    @block.tensor
                    def _(pe):
                        with pe.Fori(0, KD) as j:
                            for b in range(3):
                                pe.wait_ge(w_land[b], 32 * j + 32)
                                for c in range(4):
                                    n = 12 * j + 4 * b + c
                                    pe.wait_ge(sig_done, n + 1)
                                    product(pe, pg[:, c, :], win[:, b, :], *LAT_CHUNKS[c]).then_inc(mg_mm, 1)
                                    pe.wait_ge(br_read, n + 1)
                                    pe.wait_ge(yg_land[b], 16 * NB)
                                    for k in range(NB):
                                        mm = pe.matmul(pr_[:, c, :], wb[:, b, k * P:(k + 1) * P], yg[:, NB * b + k, c * CH:(c + 1) * CH],
                                                       start=(k == 0), stop=(k == NB - 1))
                                    mm.then_inc(br_mm, 1)

                    @block.scalar
                    def _(act):
                        act.nop().then_inc(sig_done, 4)
                        with act.Fori(0, KD) as j:
                            for i in range(12):
                                n = 12 * j + i
                                act.wait_ge(mg_mm, n + 1)
                                act.wait_ge(br_read, n + 3)
                                nc.scalar.activation(sig[:, i % 2, :], pg[:, i % 4, :], ACT.Sigmoid).then_inc(sig_done, 1)

                    @block.vector
                    def _(dve):
                        v = nc.vector
                        dve.nop().then_inc(br_read, 4)
                        with dve.Fori(0, KD) as j:
                            st = Steps(dve, mg_dv, 4 * j)
                            for i in range(12):
                                b, c = i // 4, i % 4
                                n = 12 * j + i
                                dve.wait_ge(sig_done, n + 5)
                                dve.wait_ge(br_mm, n + 1)
                                if b == 0:
                                    dve.wait_ge(m_out[c], 16 * j + 16)
                                    v.tensor_tensor(m[:, c, :], sig[:, c % 2, :], pr_[:, c, :], ALU.mult).then_inc(br_read, 1)
                                    continue
                                v.tensor_tensor(tmp[:, :], sig[:, c % 2, :], pr_[:, c, :], ALU.mult).then_inc(br_read, 1)
                                dve.wait_ge(br_read, n + 5)
                                ins = v.tensor_tensor(m[:, c, :], m[:, c, :], tmp[:, :], ALU.add)
                                if b == 1:
                                    st(ins)
                                else:
                                    ins.then_inc(m_done, 1)
                                    dve.wait_ge(m_done, 4 * j + c + 1)

        with ExitStack() as cx:
            wo = sb(cx, "wo", [P, KD, D])
            mt = sb(cx, "mt", [P, 2, D])
            xin = sb(cx, "xin", [P, 2, D])
            h = sb(cx, "h", [P, 2, D])
            stat = sb(cx, "stat", [P, 2, 18])
            gb = sb(cx, "gb", [P, 2, D])
            pout = ps(cx, "pout", [P, 2, 2, CH])
            wo_land, gb_land = sem("wo_land"), sem("gb_land")
            t_land = [sem("t_land0"), sem("t_land1")]
            out_mm, o_read, out_dv, ovar_done, ostd_done, h_done, y_done = [sem(n) for n in (
                "out_mm", "o_read", "out_dv", "ovar_done", "ostd_done", "h_done", "y_done")]
            stored, biased = [sem("stored0"), sem("stored1")], sem("biased")
            NV = 5
            NT = L // P
            with nc.Block() as block:
                @block.sync
                def _(sp_):
                    for s in range(2):
                        sp_.nop().then_inc(stored[s], 16)
                    for k in range(KD):
                        sp_.dma_start(wo[:, k, :], a["w_out"][:, k, :]).then_inc(wo_land, 16)
                    for n, name in enumerate(("ln_g", "ln_b")):
                        sp_.dma_start(gb[:, n, :], bass.AP(tensor=a[name].tensor, offset=0, ap=[[0, P], [1, D]])).then_inc(gb_land, 16)
                    with sp_.Fori(0, NT // 2) as i:
                        for s in range(2):
                            n = 2 * i + s
                            sp_.wait_ge(out_mm, n + 1)
                            sp_.wait_ge(h_done, n + 1)
                            sp_.dma_start(mt[:, s, :], m_dram[n].rearrange("p k c -> p (k c)")).then_inc(t_land[s], 16)
                            sp_.dma_start(xin[:, s, :], a["x"].rearrange("(n p) d -> n p d", p=P)[n]).then_inc(t_land[s], 16)

                @block.tensor
                def _(pe):
                    pe.nop().then_inc(out_mm, 2)
                    pe.wait_ge(wo_land, 16 * KD)
                    with pe.Fori(0, NT // 2) as i:
                        for s in range(2):
                            pe.wait_ge(t_land[s], 32 * i + 32)
                            pe.wait_ge(o_read, 2 * i + s + 1)
                            for half in range(2):
                                for k in range(KD):
                                    mm = pe.matmul(pout[:, s, half, :], mt[:, s, k * P:(k + 1) * P], wo[:, k, half * CH:(half + 1) * CH],
                                                   start=(k == 0), stop=(k == KD - 1))
                            mm.then_inc(out_mm, 1)

                @block.vector
                def _(dve):
                    v = nc.vector
                    dve.nop().then_inc(o_read, 2)
                    dve.nop().then_inc(h_done, 2)
                    with dve.Fori(0, NT // 2) as i:
                        for s in range(2):
                            n = 2 * i + s
                            st = Steps(dve, out_dv, NV * n)
                            x, q = h[:, s, :], stat[:, s, :]
                            dve.wait_ge(out_mm, n + 3)
                            dve.wait_ge(stored[s], 16 * i + 16)
                            v.tensor_tensor(x, pout[:, s, :, :].rearrange("p a b -> p (a b)"), gate_row[:, :], ALU.mult).then_inc(o_read, 1)
                            dve.wait_ge(o_read, n + 3)
                            dve.wait_ge(t_land[s], 32 * i + 32)
                            v.scalar_tensor_tensor(x, xin[:, s, :], ALPHA, x, ALU.mult, ALU.add).then_inc(h_done, 1)
                            dve.wait_ge(h_done, n + 3)
                            st(v.bn_stats(q[:, 0:6], x[:, 0:512]))
                            st(v.bn_stats(q[:, 6:12], x[:, 512:1024]))
                            dve.nop(nofuse=True)
                            st(v.bn_aggr(q[:, 12:14], q[:, 0:12]))
                            v.tensor_scalar(q[:, 14:15], q[:, 13:14], EPS, None, ALU.add).then_inc(ovar_done, 1)
                            dve.wait_ge(ostd_done, n + 1)
                            st(v.reciprocal(q[:, 16:17], q[:, 15:16]))
                            dve.wait_ge(gb_land, 32)
                            st(v.tensor_scalar(x, x, q[:, 12:13], q[:, 16:17], ALU.subtract, ALU.mult))
                            v.tensor_tensor(x, x, gb[:, 0, :], ALU.mult).then_inc(y_done, 1)

                @block.scalar
                def _(act):
                    with act.Fori(0, NT // 2) as i:
                        for s in range(2):
                            act.wait_ge(ovar_done, 2 * i + s + 1)
                            nc.scalar.activation(stat[:, s, 15:16], stat[:, s, 14:15], ACT.Sqrt).then_inc(ostd_done, 1)
                            act.wait_ge(biased, 2 * i + s + 1)
                            act.dma_start(out.rearrange("(n p) d -> n p d", p=P)[2 * i + s], h[:, s, :]).then_inc(stored[s], 16)
                    for s in range(2):
                        act.wait_ge(stored[s], 16 * (NT // 2) + 16)

                @block.gpsimd
                def _(pool):
                    pool.wait_ge(gb_land, 32)
                    with pool.Fori(0, NT // 2) as i:
                        for s in range(2):
                            n = 2 * i + s
                            pool.wait_ge(y_done, n + 1)
                            nc.gpsimd.tensor_tensor(h[:, s, :], h[:, s, :], gb[:, 1, :], ALU.add).then_inc(biased, 1)


def lay_out(x, c, ctx, c_ctx, w_mod, b_mod, w_in, lru_conv_w, lru_conv_b, lru_w_a, lru_b_a, lru_w_x, lru_b_x,
            lru_lambda, na_rpb, hy_conv_w, hy_conv_b, hy_w1, hy_b1, hy_freq1, hy_w2, hy_b2, hy_freq2, hy_w3,
            hy_d_skip, w_branch_out, w_out, ln_g, ln_b):
    def tiles(v):
        return v.reshape(-1, P).T

    def twice(v):
        return np.concatenate([v, v], -1)
    o = {"x": x[0], "ctx": ctx[0]}
    o["cvec"] = np.stack([tiles(c[0]), tiles(c_ctx)], -1)
    o["w_mod"] = w_mod[0].reshape(KD, P, 24, P).transpose(2, 1, 0, 3).reshape(24, P, D)
    o["bmod"] = np.stack([tiles(b_mod[0])] * 2, -1)
    o["w_in"] = w_in[0].reshape(KD, P, 64, P).transpose(2, 1, 0, 3).reshape(64, P, D)
    o["lam"] = lru_lambda[0].reshape(2, NB, P).transpose(2, 1, 0).reshape(P, 2 * NB)
    rpb = np.zeros((HEADS, NDR, TOE), np.float32)
    rpb[:, :, GW - NKW:GW + NKW - 1] = na_rpb[0]
    o["rpb"] = rpb
    o["lru_vec"] = np.stack([*lru_conv_w[0].reshape(4, NB, P), lru_conv_b[0].reshape(NB, P),
                             *lru_b_a[0].reshape(2, NB, P), *lru_b_x[0].reshape(2, NB, P)], -1)
    gate = np.zeros((NB, P, 4, P), np.float32)
    for d in range(2):
        for n, w in enumerate((lru_w_a, lru_w_x)):
            for b in range(8):
                r = slice(64 * (b % 2), 64 * (b % 2) + 64)
                gate[b // 2, r, 2 * d + n, r] = w[0, d, b]
    o["lru_gate"] = gate
    cw = hy_conv_w[0].reshape(3, 3, NB, P)
    cb = hy_conv_b[0].reshape(3, NB, P)
    o["hy_vec"] = np.stack([cw[k, part] for part in range(3) for k in range(3)] + [cb[0], cb[1], cb[2],
                           hy_d_skip[0].reshape(NB, P)], -1)
    o["hy_w1"] = twice(hy_w1[0])
    o["hy_w2"] = twice(hy_w2[0])
    o["hy_bf"] = np.stack([twice(v[0]) for v in (hy_b1, hy_freq1, hy_b2, hy_freq2)], -1)
    o["hy_w3"] = np.concatenate([hy_w3[0][:, :512], hy_w3[0][:, 512:]], 0)
    o["w_branch"] = w_branch_out[0].reshape(3, NB, P, KD, P).transpose(3, 2, 0, 1, 4).reshape(KD, P, 3 * NB * P)
    o["w_out"] = w_out[0].reshape(KD, P, D).transpose(1, 0, 2)
    o["ln_g"], o["ln_b"] = ln_g, ln_b
    return {k: np.ascontiguousarray(v) for k, v in o.items()}


def kernel(**inputs):
    import concourse.bacc as _bacc
    from concourse.bass_utils import run_bass_kernel_spmd as _run

    arrays = lay_out(**{k: np.asarray(v) for k, v in inputs.items()})
    arrays.update(shape_constants())
    nc = _bacc.Bacc("TRN2", target_bir_lowering=False, num_devices=1)
    aps = {n: nc.dram_tensor(f"in_{n}", v.shape, F32, kind="ExternalInput").ap() for n, v in arrays.items()}
    out = nc.dram_tensor("out_0", (L, D), F32, kind="ExternalOutput").ap()
    build_trunk(nc, aps, out)
    r = _run(nc, [{f"in_{n}": v for n, v in arrays.items()}], core_ids=[0])
    return r.results[0]["out_0"].reshape(1, L, D)
```

```python
import math
from contextlib import ExitStack

import numpy as np

import concourse.bass as bass
from concourse import mybir

F32 = mybir.dt.float32
F32R = mybir.dt.float32r
ALU = mybir.AluOpType
ACT = mybir.ActivationFunctionType
AX_X = mybir.AxisListType.X

P = 128
D = 1024
KD = D // P
L = 2048
LC = 256
LT = LC + L
CH = 512
NB = 512 // P
GW = 64
ROWS = L // GW
NKH, NKW = 8, 16
BAND = NKH * GW
HEADS = 8
DH = 64
NDR = 2 * NKH - 1
TOE = 2 * GW - 1
NF = 2 * L
R1 = 64
NPR = R1 // 2
EMB = 33
HID = 64
ALPHA = 2.0 ** 0.25
EPS = 1e-5
MASKED = -1e30
NQ = L // CH
LAT_CHUNKS = [(LC + CH * i, CH) for i in range(L // CH)]
ALL_CHUNKS = [(0, LC)] + LAT_CHUNKS
B_AIN, B_AGATE, B_Q, B_K, B_V, B_BGATE, B_X0, B_X1, B_HV, B_CGATE, B_G = 0, 4, 8, 12, 16, 20, 24, 28, 32, 36, 40


def shape_constants():
    f = {}
    n1 = np.arange(R1)
    kk = np.arange(R1)
    k1, ri = kk % 32, kk // 32
    ang = 2 * np.pi * np.outer(n1, k1) / R1
    one = np.where(ri == 0, np.cos(ang), -np.sin(ang))
    one[:, 0] = 1.0
    one[:, 32] = (-1.0) ** n1
    lat = np.kron(np.eye(2), one[:32])
    f["dft1"] = np.concatenate([lat, lat], 0)
    f["dft1_filter"] = np.kron(np.eye(2), one[np.where(n1 < 32, n1, 95 - n1)])
    inv = np.where(ri == 0, 2 * np.cos(ang), -2 * np.sin(ang))
    inv[:, 0] = 1.0
    inv[:, 32] = (-1.0) ** n1
    f["idft1"] = np.kron(np.eye(2), inv[:32].T) / NF
    n2 = 2 * (np.arange(64) % 32) + np.arange(64) // 32
    k2 = np.arange(64)
    fwd = np.zeros((32, 128, 128))
    inv2 = np.zeros((32, 128, 128))
    for k in range(1, 32):
        th = 2 * np.pi * np.outer(n2, k + 64 * k2) / NF
        c, s = np.cos(th), np.sin(th)
        fwd[k] = np.block([[c, -s], [s, c]])
        inv2[k] = np.block([[c.T, s.T], [-s.T, c.T]])
    h = np.arange(32)
    t0 = 2 * np.pi * np.outer(n2, 64 * h) / NF
    t1 = 2 * np.pi * np.outer(n2, 32 + 64 * h) / NF
    fwd[0, :64, :32], fwd[0, :64, 64:96] = np.cos(t0), -np.sin(t0)
    fwd[0, 64:, 32:64], fwd[0, 64:, 96:] = np.cos(t1), -np.sin(t1)
    fwd[0, :64, 64] = (-1.0) ** n2
    inv2[0, :32, :64], inv2[0, 64:96, :64] = 2 * np.cos(t0).T, -2 * np.sin(t0).T
    inv2[0, 32:64, 64:], inv2[0, 96:, 64:] = 2 * np.cos(t1).T, -2 * np.sin(t1).T
    inv2[0, 0, :64] = 1.0
    inv2[0, 64, :64] = (-1.0) ** n2
    swapped = np.concatenate([inv2[:, 64:], -inv2[:, :64]], 1)
    tab = np.concatenate([fwd, inv2, swapped], 2)
    tab = tab.reshape(8, 4, P, 3 * P).transpose(0, 2, 1, 3)
    f["dft2"] = tab[..., :P].reshape(8, P, 4 * P)
    f["idft2"] = tab[..., P:].reshape(8, P, 8 * P)
    kb = np.concatenate([fwd[0, :, :64], fwd[0, :, :64]], 1)
    kb[:, 64] = fwd[0, :, 64]
    kc = np.concatenate([fwd[0, :, 64:], fwd[0, :, 64:]], 1)
    kc[:, [0, 64]] = 0
    f["dft2_first"] = np.concatenate([kb, kc], 1)
    t = np.arange(L) / np.float32(L)
    a = 2 * np.pi * t[:, None] * np.arange(1, 17)
    f["positions"] = np.concatenate([t[:, None], np.cos(a), np.sin(a)], 1).T
    tt = np.zeros((32, 2, 64))
    for pr in range(32):
        for j in range(2):
            tt[pr, j, :32] = 64 * np.arange(32) + 2 * pr + j
            tt[pr, j, 32:] = 64 * (np.arange(32) + 1) - (2 * pr + j)
    f["neg_time"] = -(tt / L).reshape(32, 128).T
    f["deltas"] = np.abs(np.linspace(math.log(1e-2) / 0.3, math.log(1e-2) / 1.5, 512))[None]
    cols = np.arange(GW)
    start = np.clip(cols - NKW // 2, 0, GW - NKW)
    ok = (cols[None] >= start[:, None]) & (cols[None] < start[:, None] + NKW)
    m = np.where(ok, 0.0, MASKED)
    f["col_mask"] = np.concatenate([m, m], 0)
    f["ident"] = np.eye(P)
    f["flip"] = np.kron(np.eye(2), np.eye(GW)[::-1])
    return {k: np.ascontiguousarray(v, np.float32) for k, v in f.items()}


class Steps:

    def __init__(self, eng, sem, base=0):
        self.eng, self.sem, self.base, self.n = eng, sem, base, 0

    def __call__(self, ins):
        ins.then_inc(self.sem, 1)
        self.n += 1
        self.eng.wait_ge(self.sem, self.base + self.n)


def build_trunk(nc, a, out):
    def dram(name, shape):
        return nc.dram_tensor(name, shape, F32, kind="Internal").ap()

    bias_tab = dram("bias_tab", (NB, P, NDR * GW))
    filt_mid = dram("filt_mid", (2, NPR, R1, 512))
    filt_spec = dram("filt_spec", (NB, NPR // 4, 2, R1, 4 * P))
    filt_spec0 = dram("filt_spec0", (NB, P, 2, P))
    fwd_mid = dram("fwd_mid", (NB, P, NPR, P))
    inv_mid = dram("inv_mid", (NB, P, NPR, P))
    yg_dram = dram("yg_dram", (NQ, 3, P, NB * CH))
    m_dram = dram("m_dram", (NQ, L // P // NQ, P, KD, P))
    names = [0]

    def free_name(n):
        names[0] += 1
        return f"{n}_{names[0]}"

    top = ExitStack()

    def sb(ctx, name, shape, dtype=F32):
        return ctx.enter_context(nc.sbuf_tensor(free_name(name), shape, dtype))

    def ps(ctx, name, shape):
        return ctx.enter_context(nc.psum_tensor(free_name(name), shape, F32))

    def sem(name):
        return top.enter_context(nc.semaphore(name))

    with top:
        ident = sb(top, "ident", [P, P])
        mod = sb(top, "mod", [P, 24, 2])
        decay = sb(top, "decay", [P, 2 * NB, 2])
        gate_row = sb(top, "gate_row", [P, D])

        with ExitStack() as cx:
            WS = 4
            NP = 2 * 3 * D // CH
            cvec = sb(cx, "cvec", [P, KD, 2])
            bmod = sb(cx, "bmod", [P, 24, 2])
            wm = sb(cx, "wm", [P, WS, KD // 2, CH])
            mod_row = sb(cx, "mod_row", [2, 3 * D])
            lam = sb(cx, "lam", [P, 2 * NB])
            sp = sb(cx, "sp", [P, 6, 2 * NB])
            toe = sb(cx, "toe", [P, NB, NDR, GW])
            toe_flat = toe[:, :, :, :].rearrange("p a b c -> p (a b c)")
            toe_rows = toe[:, :, :, :].rearrange("p a b c -> p (a b) c")
            mask = sb(cx, "mask", [P, GW])
            flip = sb(cx, "flip", [P, P])
            spread = sb(cx, "spread", [P, KD, P])
            ones = sb(cx, "ones", [P, P])
            pos = sb(cx, "pos", [EMB, L])
            w1 = sb(cx, "w1", [EMB, 2 * HID])
            w2 = sb(cx, "w2", [HID, 2 * HID])
            w3 = sb(cx, "w3", [P, 512])
            bf = sb(cx, "bf", [P, 4])
            arg = sb(cx, "arg", [P, L])
            turns = sb(cx, "turns", [P, L])
            hid1 = sb(cx, "hid1", [P, L])
            hid = sb(cx, "hid", [P, R1, R1])
            negt = sb(cx, "negt", [P, NPR])
            deltas = sb(cx, "deltas", [P, 512])
            d1f = sb(cx, "d1f", [P, P])
            hpair = sb(cx, "hpair", [P, 4, P])
            window = sb(cx, "window", [P, 4, 512])
            filt = sb(cx, "filt", [P, 4, 512])
            mid = sb(cx, "mid", [P, 4, 512])
            mid2 = sb(cx, "mid2", [P, 2, 4, 512])
            d2f = sb(cx, "d2f", [P, 2, 4 * P])
            spec = sb(cx, "spec", [P, 2, 4, 512])
            mid0 = sb(cx, "mid0", [P, 512])
            d20 = sb(cx, "d20", [P, 2 * P])
            spec0 = sb(cx, "spec0", [P, 2, 512])
            lo = ps(cx, "lo", [P, 4, CH])
            hi = ps(cx, "hi", [P, 4, CH])
            TG = 6
            NTG = NB * NDR // TG
            NG = NPR // 4
            small_in, toe_in, f_in = sem("small_in"), sem("toe_in"), sem("f_in")
            wm_in = [sem(f"wm_in{s}") for s in range(WS)]
            (c_ready, mod_mm, mod_done, abs_lam, y_exp, spread_done, flip_mm, toe_done, bias_out,
             pre_mm, pre_dv, sin_done, hid_zero, hpair_done, win_done, gen_mm, filt_done, mid_mm, mid_done,
             spec_mm, spec_dve, spec_act) = [sem(n) for n in (
                 "c_ready", "mod_mm", "mod_done", "abs_lam", "y_exp", "spread_done", "flip_mm", "toe_done",
                 "bias_out", "pre_mm", "pre_dv", "sin_done", "hid_zero", "hpair_done", "win_done", "gen_mm", "filt_done",
                 "mid_mm", "mid_done", "spec_mm", "spec_dve", "spec_act")]
            mid_out = [sem(f"mid_out{s}") for s in range(4)]
            mid_in = [sem("mid_in0"), sem("mid_in1")]
            spec_out = [sem("spec_out0"), sem("spec_out1")]
            MAGIC = 1.5 * 2.0 ** 23
            TWO_PI = 2 * math.pi
            c1 = 6.28125
            c2 = float(np.round((TWO_PI - c1) * 2 ** 21) / 2 ** 21)
            c3 = float(TWO_PI - c1 - c2)
            with nc.Block() as block:
                @block.sync
                def _(sp_):
                    for dst, name in ((pos, "positions"), (w1, "hy_w1"), (bf, "hy_bf"), (w2, "hy_w2"), (w3, "hy_w3"),
                                      (negt, "neg_time"), (d1f, "dft1_filter"), (d20, "dft2_first")):
                        sp_.dma_start(dst[:, :], a[name]).then_inc(f_in, 16)
                    sp_.dma_start(deltas[:, :], bass.AP(tensor=a["deltas"].tensor, offset=0,
                                                        ap=[[0, P], [1, 512]])).then_inc(f_in, 16)
                    sp_.dma_start(cvec[:, :, :], a["cvec"]).then_inc(small_in, 16)
                    sp_.dma_start(bmod[:, :, :], a["bmod"]).then_inc(small_in, 16)
                    for dst, name in ((lam, "lam"), (ident, "ident"), (mask, "col_mask"), (flip, "flip")):
                        sp_.dma_start(dst[:, :], a[name]).then_inc(small_in, 16)
                    with sp_.Fori(0, NP // WS) as i:
                        for s in range(WS):
                            sp_.wait_ge(mod_mm, WS * i + s + 1)
                            sp_.dma_start(wm[:, s, :, :].rearrange("p k c -> p (k c)"), a["w_mod"][WS * i + s]).then_inc(wm_in[s], 16)
                    sp_.wait_ge(toe_done, NTG)
                    for p in range(NB):
                        sp_.dma_start(bias_tab[p], toe[:, p, :, :]).then_inc(bias_out, 16)
                    dst = filt_mid.rearrange("r k (j q) c -> q j (r k) c", j=2)
                    with sp_.Fori(0, NPR // 4) as i:
                        for s in range(4):
                            sp_.wait_ge(mid_done, 4 * i + s + 5)
                            for j in range(2):
                                sp_.dma_start(dst[4 * i + s, j], mid[R1 * j:R1 * (j + 1), s, :]).then_inc(mid_out[s], 16)
                    for s in range(4):
                        sp_.wait_ge(mid_out[s], 32 * (NPR // 4) + 32)
                    for r in range(2):
                        sp_.dma_start(mid0[R1 * r:R1 * r + R1, :], filt_mid[r, 0]).then_inc(f_in, 16)
                    with sp_.Fori(0, NG // 2) as i:
                        for s in range(2):
                            g = 2 * i + s
                            sp_.wait_ge(spec_mm, 4 * g + 4)
                            for r in range(2):
                                sp_.dma_start(mid2[R1 * r:R1 * r + R1, s, :, :],
                                              filt_mid[r].rearrange("(g k) n c -> g n k c", k=4)[g]).then_inc(mid_in[s], 16)
                            sp_.dma_start(d2f[:, s, :], a["dft2"][g]).then_inc(mid_in[s], 16)
                    sp_.wait_ge(bias_out, 32 * NB)

                @block.scalar
                def _(act):
                    act.nop().then_inc(mid_done, 4)
                    act.nop().then_inc(spec_act, 2)
                    act.wait_ge(small_in, 96)
                    nc.scalar.activation(cvec[:, :, :], cvec[:, :, :], ACT.Silu).then_inc(c_ready, 1)
                    act.nop().then_inc(mod_done, 2)

                    def modulation(i, bank):
                        for s in range(2):
                            act.wait_ge(mod_mm, WS * i + 2 * s + WS + 2)
                            nc.scalar.copy(mod_row[:, bass.ds((2 * i + s) * CH, CH)], bank[0:2, s, :]).then_inc(mod_done, 1)
                    modulation(0, hi)
                    act.wait_ge(pre_dv, 28)
                    nc.scalar.activation(hid1[:, :], arg[:, :], ACT.Sin).then_inc(sin_done, 1)
                    with act.Fori(1, NP // WS) as i:
                        modulation(i, lo)
                    act.wait_ge(pre_dv, 56)
                    act.wait_ge(hid_zero, 1)
                    fw = arg[0:HID, :].rearrange("p (a b) -> p b a", b=R1)
                    nc.scalar.activation(hid[0:HID, :, 0:32], fw, ACT.Sin).then_inc(sin_done, 1)
                    bw = arg[HID:P, :].rearrange("p (a b) -> p b a", b=R1)
                    nc.scalar.activation(hid[HID:P, 1:R1, 32:R1], bw[:, R1 - 1:0:-1, :], ACT.Sin).then_inc(sin_done, 1)
                    nc.scalar.activation(hid[HID:P, 0, 32:R1 - 1], bw[:, 0, 1:32], ACT.Sin).then_inc(sin_done, 1)
                    act.wait_ge(abs_lam, 1)
                    nc.scalar.activation(sp[:, 1, :], sp[:, 0, :], ACT.Exp, scale=-1.0).then_inc(y_exp, 1)
                    act.wait_ge(f_in, 144)
                    with act.Fori(0, NPR // 4) as i:
                        for s in range(4):
                            act.wait_ge(filt_done, 4 * i + s + 1)
                            nc.scalar.activation(window[:, s, :], deltas[:, :], ACT.Exp,
                                                 scale=negt[:, bass.ds(4 * i + s, 1)]).then_inc(win_done, 1)
                        for s in range(4):
                            act.wait_ge(mid_mm, 4 * i + s + 5)
                            act.wait_ge(mid_out[s], 32 * i + 32)
                            nc.scalar.copy(mid[:, s, :], hi[:, s, :]).then_inc(mid_done, 1)
                    act.wait_ge(pre_mm, 5)
                    for b in range(2):
                        nc.scalar.copy(spec0[:, b, :], hi[:, 2 * b, :]).then_inc(spec_act, 1)
                    act.wait_ge(spec_act, 4)
                    for t in range(NB):
                        act.dma_start(filt_spec0[t], spec0[:, :, t * P:(t + 1) * P]).then_inc(bias_out, 16)
                    with act.Fori(0, NG // 2) as i:
                        for s in range(2):
                            g = 2 * i + s
                            act.wait_ge(spec_out[s], 64 * i + 64)
                            for k in (0, 2):
                                act.wait_ge(spec_mm, 4 * g + k + 9)
                                nc.scalar.copy(spec[:, s, k, :], (lo, hi)[s][:, k, :]).then_inc(spec_act, 1)
                            act.wait_ge(spec_dve, 2 * g + 6)
                            act.wait_ge(spec_act, 2 * g + 6)
                            for t in range(NB):
                                act.dma_start(filt_spec[t, g].rearrange("b q (k c) -> (b q) k c", c=P),
                                              spec[:, s, :, t * P:(t + 1) * P]).then_inc(spec_out[s], 16)
                    for s in range(2):
                        act.wait_ge(spec_out[s], 32 * NG + 64)

                @block.gpsimd
                def _(pool):
                    for s in range(4):
                        pool.nop().then_inc(mid_out[s], 32)
                    for s in range(2):
                        pool.nop().then_inc(spec_out[s], 64)
                    for h in range(HEADS):
                        src = bass.AP(tensor=a["rpb"].tensor, offset=h * NDR * TOE, ap=[[1, GW], [TOE, NDR], [1, GW]])
                        pool.dma_start(toe[GW * (h % 2):GW * (h % 2) + GW, h // 2, :, :], src).then_inc(toe_in, 16)
                    nc.gpsimd.memset(hid[:, :, :], 0.0).then_inc(hid_zero, 1)
                    pool.wait_ge(toe_in, 16 * HEADS)
                    pool.wait_ge(sin_done, 4)
                    pairs = hid[:, :, :].rearrange("p (r j) s -> p r (j s)", j=2)
                    with pool.Fori(0, NPR // 4) as i:
                        for s in range(4):
                            pool.wait_ge(gen_mm, 4 * i + s + 1)
                            nc.gpsimd.tensor_copy(hpair[:, s, :].unsqueeze(1), pairs[:, bass.ds(4 * i + s, 1), :]).then_inc(hpair_done, 1)

                @block.tensor
                def _(pe):
                    pe.nop().then_inc(mod_mm, WS)
                    pe.nop().then_inc(gen_mm, 4)
                    pe.nop().then_inc(mid_mm, 4)
                    pe.nop().then_inc(spec_mm, 8)
                    pe.wait_ge(f_in, 144)
                    for c in range(4):
                        mm = pe.matmul(lo[:, c, :], w1[:, :], pos[:, c * CH:(c + 1) * CH], start=True, stop=True)
                    mm.then_inc(pre_mm, 1)

                    def modulation(i, bank):
                        for s in range(WS):
                            pe.wait_ge(wm_in[s], 16 * i + 16)
                            if s % 2 == 0:
                                pe.wait_ge(mod_done, 2 * i + s // 2 + 1)
                            for n in range(KD // 2):
                                k = KD // 2 * (s % 2) + n
                                mm = pe.matmul(bank[0:2, s // 2, :], cvec[:, k, :], wm[:, s, n, :], start=(k == 0), stop=(k == KD - 1))
                            mm.then_inc(mod_mm, 1)
                    pe.wait_ge(c_ready, 1)
                    modulation(0, hi)
                    pe.wait_ge(sin_done, 1)
                    pe.wait_ge(mod_done, 4)
                    for c in range(4):
                        mm = pe.matmul(hi[:, c, :], w2[:, :], hid1[0:HID, c * CH:(c + 1) * CH], start=True, stop=True)
                    mm.then_inc(pre_mm, 1)
                    with pe.Fori(1, NP // WS) as i:
                        modulation(i, lo)
                    pe.wait_ge(pre_dv, 56)
                    pe.wait_ge(mod_done, NP // 2 + 2)
                    for b in range(24):
                        mm = pe.transpose(lo[:, 2, 2 * b:2 * b + 2], mod_row[:, b * P:(b + 1) * P], ident[0:2, 0:2])
                    mm.then_inc(pre_mm, 1)
                    pe.wait_ge(spread_done, 1)
                    for k in range(KD):
                        mm = pe.matmul(lo[:, 2 + k // 4, (k % 4) * P:(k % 4 + 1) * P], spread[:, k, :], ident[:, :],
                                       start=True, stop=True)
                    mm.then_inc(pre_mm, 1)
                    pe.wait_ge(toe_in, 16 * HEADS)
                    for n in range(NTG):
                        if n >= 4:
                            pe.wait_ge(toe_done, n - 3)
                        pe.matmul(hi[:, n % 4, 0:TG * GW], flip[:, :], toe_flat[:, n * TG * GW:(n + 1) * TG * GW],
                                  start=True, stop=True).then_inc(flip_mm, 1)
                    pe.wait_ge(toe_done, NTG)
                    with pe.Fori(0, NPR // 4) as i:
                        def generate(n, s):
                            pe.wait_ge(hpair_done, n + 1)
                            pe.wait_ge(filt_done, n + 1)
                            pe.matmul(lo[:, s, :], hpair[:, s, :], w3[:, :], start=True, stop=True).then_inc(gen_mm, 1)
                        for s in range(4):
                            generate(4 * i + s, s)
                        for s in range(4):
                            pe.wait_ge(filt_done, 4 * i + s + 5)
                            pe.wait_ge(mid_done, 4 * i + s + 1)
                            pe.matmul(hi[:, s, :], d1f[:, :], filt[:, s, :], start=True, stop=True).then_inc(mid_mm, 1)
                    pe.wait_ge(mid_done, NPR + 4)
                    pe.wait_ge(f_in, 144 + 32)
                    for b in range(2):
                        mm = pe.matmul(hi[:, 2 * b, :], d20[:, b * P:(b + 1) * P], mid0[:, :], start=True, stop=True)
                    mm.then_inc(pre_mm, 1)
                    with pe.Fori(0, NG // 2) as i:
                        for s in range(2):
                            g = 2 * i + s
                            pe.wait_ge(mid_in[s], 48 * i + 48)
                            for k in range(4):
                                pe.wait_ge((spec_act, spec_dve)[k % 2], 2 * g + k // 2 + 1)
                                pe.matmul((lo, hi)[s][:, k, :], d2f[:, s, P * k:P * k + P], mid2[:, s, k, :],
                                          start=True, stop=True).then_inc(spec_mm, 1)

                @block.vector
                def _(dve):
                    v = nc.vector
                    dve.nop().then_inc(filt_done, 4)
                    dve.nop().then_inc(spec_dve, 4)
                    st = Steps(dve, pre_dv)
                    dve.wait_ge(f_in, 144)
                    for layer in range(2):
                        dve.wait_ge(pre_mm, layer + 1)
                        src = (lo, hi)[layer]
                        if layer:
                            dve.wait_ge(sin_done, 1)
                        for c in range(4):
                            x, n = arg[:, c * CH:(c + 1) * CH], turns[:, c * CH:(c + 1) * CH]
                            st(v.tensor_scalar(x, src[:, c, :], bf[:, 2 * layer:2 * layer + 1],
                                               bf[:, 2 * layer + 1:2 * layer + 2], ALU.add, ALU.mult))
                            st(v.tensor_scalar(n, x, 1 / TWO_PI, MAGIC, ALU.mult, ALU.add))
                            st(v.tensor_scalar(n, n, -MAGIC, None, ALU.add))
                            for part in (c1, c2, c3):
                                st(v.scalar_tensor_tensor(x, n, -part, x, ALU.mult, ALU.add))
                            st(v.tensor_scalar(x, x, 3.1415925, -3.1415925, ALU.min, ALU.max))
                    st = Steps(dve, pre_dv, 56)
                    st(v.memset(ones[:, :], 1.0))
                    dve.wait_ge(small_in, 96)
                    st(v.tensor_scalar(sp[:, 2, :], lam[:, :], -1.0, None, ALU.mult))
                    v.tensor_tensor(sp[:, 0, :], lam[:, :], sp[:, 2, :], ALU.max).then_inc(abs_lam, 1)
                    dve.wait_ge(pre_mm, 3)
                    st(v.tensor_tensor(mod[:, :, :], lo[:, 2, 0:48].rearrange("p (b c) -> p b c", c=2), bmod[:, :, :], ALU.add))
                    st(v.tensor_scalar(mod[:, 8:16, :], mod[:, 8:16, :], 1.0, None, ALU.add))
                    for k in range(KD):
                        ins = v.tensor_scalar(spread[:, k, :], ones[:, :], mod[:, 16 + k, 0:1], None, ALU.mult)
                    ins.then_inc(spread_done, 1)
                    dve.wait_ge(y_exp, 1)
                    st(v.tensor_scalar(sp[:, 3, :], sp[:, 1, :], 2.0, None, ALU.add))
                    st(v.reciprocal(sp[:, 4, :], sp[:, 3, :]))
                    st(v.tensor_tensor(sp[:, 0, :], sp[:, 4, :], sp[:, 1, :], ALU.mult))
                    st(v.tensor_tensor(sp[:, 4, :], sp[:, 0, :], sp[:, 0, :], ALU.mult))
                    st(v.tensor_scalar(sp[:, 5, :], sp[:, 4, :], 1.0 / 17, 1.0 / 15, ALU.mult, ALU.add))
                    for n in (13, 11, 9, 7, 5, 3, 1):
                        st(v.tensor_tensor(sp[:, 5, :], sp[:, 5, :], sp[:, 4, :], ALU.mult))
                        st(v.tensor_scalar(sp[:, 5, :], sp[:, 5, :], 1.0 / n, None, ALU.add))
                    st(v.tensor_tensor(sp[:, 5, :], sp[:, 5, :], sp[:, 0, :], ALU.mult))
                    st(v.tensor_scalar(sp[:, 2, :], sp[:, 2, :], 0.0, None, ALU.max))
                    st(v.scalar_tensor_tensor(sp[:, 3, :], sp[:, 5, :], 2.0, sp[:, 2, :], ALU.mult, ALU.add))
                    st(v.tensor_scalar(decay[:, :, 0], sp[:, 3, :], -8.0, None, ALU.mult))
                    st(v.tensor_scalar(decay[:, :, 1], sp[:, 3, :], 8.0, None, ALU.mult))
                    dve.wait_ge(pre_mm, 4)
                    st(v.tensor_copy(gate_row[:, :].rearrange("p (a b) -> p a b", a=2), lo[:, 2:4, :]))
                    for n in range(NTG):
                        dve.wait_ge(flip_mm, n + 1)
                        v.tensor_tensor(toe_rows[:, n * TG:(n + 1) * TG, :], hi[:, n % 4, 0:TG * GW].rearrange("p (a b) -> p a b", b=GW),
                                        mask[:, :].unsqueeze(1).to_broadcast([P, TG, GW]), ALU.add).then_inc(toe_done, 1)
                    with dve.Fori(0, NPR // 4) as i:
                        for s in range(4):
                            n = 4 * i + s
                            dve.wait_ge(gen_mm, n + 5)
                            dve.wait_ge(win_done, n + 1)
                            dve.wait_ge(mid_mm, n + 1)
                            v.tensor_tensor(filt[:, s, :], lo[:, s, :], window[:, s, :], ALU.mult).then_inc(filt_done, 1)
                    with dve.Fori(0, NG // 2) as i:
                        for s in range(2):
                            dve.wait_ge(spec_out[s], 64 * i + 64)
                            for k in (1, 3):
                                dve.wait_ge(spec_mm, 8 * i + 4 * s + k + 9)
                                v.tensor_copy(spec[:, s, k, :], (lo, hi)[s][:, k, :]).then_inc(spec_dve, 1)

        main = ExitStack()
        with main:
            ut = sb(main, "ut", [P, KD, LT])

            with ExitStack() as cx:
                xin = sb(cx, "xin", [P, 4, D])
                xn = sb(cx, "xn", [P, 2, D])
                stat = sb(cx, "stat", [P, 4, 18])
                pt = ps(cx, "pt", [P, 2, 2, CH])
                x_in = [sem(f"x_in{s}") for s in range(4)]
                norm_dv, var_done, std_done, xn_done, turn_mm, ut_act, ut_dve = [sem(n) for n in (
                    "norm_dv", "var_done", "std_done", "xn_done", "turn_mm", "ut_act", "ut_dve")]
                NV_NORM = 5
                NTILE = LT // P
                ROUNDS = (NTILE - 4) // 4

                def tiles(eng, do):
                    for n in range(4):
                        do(n, n, 1, n < 2, slice(n * P, (n + 1) * P))
                    with eng.Fori(0, ROUNDS) as i:
                        for s in range(4):
                            do(4 * i + s + 4, s, i + 2, 0, bass.ds((4 * i + s + 4) * P, P))
                    for n in range(4 + 4 * ROUNDS, NTILE):
                        do(n, n % 4, n // 4 + 1, 0, slice(n * P, (n + 1) * P))

                with nc.Block() as block:
                    @block.sync
                    def _(sp_):
                        def load(n, s, use, which, col):
                            if isinstance(n, int) and n < 2:
                                src = a["ctx"][n * P:(n + 1) * P]
                            else:
                                src = a["x"].rearrange("(n p) d -> n p d", p=P)[n - 2]
                            if not isinstance(n, int) or n >= 4:
                                sp_.wait_ge(xn_done, n - 3)
                            sp_.dma_start(xin[:, s, :], src).then_inc(x_in[s], 16)
                        tiles(sp_, load)

                    def modulate(eng, n, s, which, col, half, done):
                        eng.wait_ge(turn_mm, n + 3)
                        for k in range(4 * half, 4 * half + 4):
                            src = pt[:, s % 2, half, (k % 4) * P:(k % 4 + 1) * P]
                            dst = ut[:, k, col]
                            scale, shift = mod[:, 8 + k, which:which + 1], mod[:, k, which:which + 1]
                            if half:
                                ins = nc.vector.tensor_scalar(dst, src, scale, shift, ALU.mult, ALU.add)
                            else:
                                ins = nc.scalar.activation(dst, src, ACT.Identity, bias=shift, scale=scale)
                        ins.then_inc(done, 1)

                    @block.vector
                    def _(dve):
                        v = nc.vector
                        dve.nop().then_inc(ut_dve, 2)

                        def normalise(n, s, use, which, col):
                            b = n * NV_NORM
                            x, q = xin[:, s, :], stat[:, s, :]
                            dve.wait_ge(x_in[s], 16 * use)
                            v.bn_stats(q[:, 0:6], x[:, 0:512]).then_inc(norm_dv, 1)
                            v.bn_stats(q[:, 6:12], x[:, 512:1024]).then_inc(norm_dv, 1)
                            dve.wait_ge(norm_dv, b + 2)
                            dve.nop(nofuse=True)
                            v.bn_aggr(q[:, 12:14], q[:, 0:12]).then_inc(norm_dv, 1)
                            dve.wait_ge(norm_dv, b + 3)
                            v.tensor_scalar(q[:, 14:15], q[:, 13:14], EPS, None, ALU.add).then_inc(var_done, 1)
                            if not isinstance(n, int):
                                modulate(dve, n - 2, s, 0, bass.ds((n - 2) * P, P), 1, ut_dve)
                            elif n >= 2:
                                modulate(dve, n - 2, s, n < 4, slice((n - 2) * P, (n - 1) * P), 1, ut_dve)
                            dve.wait_ge(std_done, n + 1)
                            v.reciprocal(q[:, 16:17], q[:, 15:16]).then_inc(norm_dv, 1)
                            dve.wait_ge(norm_dv, b + 4)
                            v.tensor_scalar(q[:, 17:18], q[:, 12:13], q[:, 16:17], -1.0, ALU.mult, ALU.mult).then_inc(norm_dv, 1)
                        tiles(dve, normalise)
                        for n in range(NTILE - 2, NTILE):
                            modulate(dve, n, n, 0, slice(n * P, (n + 1) * P), 1, ut_dve)

                    @block.scalar
                    def _(act):
                        act.nop().then_inc(ut_act, 2)

                        def tile(n, s, use, which, col):
                            act.wait_ge(var_done, n + 1)
                            nc.scalar.activation(stat[:, s, 15:16], stat[:, s, 14:15], ACT.Sqrt).then_inc(std_done, 1)
                            if not isinstance(n, int):
                                modulate(act, n - 2, s, 0, bass.ds((n - 2) * P, P), 0, ut_act)
                            elif n >= 2:
                                modulate(act, n - 2, s, n < 4, slice((n - 2) * P, (n - 1) * P), 0, ut_act)
                            act.wait_ge(norm_dv, NV_NORM * n + NV_NORM)
                            act.wait_ge(turn_mm, n + 1)
                            nc.scalar.activation(xn[:, s % 2, :], xin[:, s, :], ACT.Identity,
                                                 bias=stat[:, s, 17:18], scale=stat[:, s, 16:17]).then_inc(xn_done, 1)
                        tiles(act, tile)
                        for n in range(NTILE - 2, NTILE):
                            modulate(act, n, n, 0, slice(n * P, (n + 1) * P), 0, ut_act)

                    @block.tensor
                    def _(pe):
                        pe.nop().then_inc(turn_mm, 2)

                        def tile(n, s, use, which, col):
                            pe.wait_ge(xn_done, n + 1)
                            pe.wait_ge(ut_act, n + 1)
                            pe.wait_ge(ut_dve, n + 1)
                            for k in range(KD):
                                mm = pe.transpose(pt[:, s % 2, k // 4, (k % 4) * P:(k % 4 + 1) * P],
                                                  xn[:, s % 2, k * P:(k + 1) * P], ident[:, :])
                            mm.then_inc(turn_mm, 1)
                        tiles(pe, tile)

            def product(pe, bank, w, col, width):
                for k in range(KD):
                    mm = pe.matmul(bank, w[:, k * P:(k + 1) * P], ut[:, k, col:col + width],
                                   start=(k == 0), stop=(k == KD - 1))
                return mm

            with ExitStack() as cx:
                win = sb(cx, "win", [P, 2, D])
                lw = sb(cx, "lw", [P, 4, P])
                lv = sb(cx, "lv", [P, 9])
                X0, X1 = 2, LC + 5
                xin = sb(cx, "a_in", [P, LT + 6])
                xc = sb(cx, "xc", [P, LT])
                sg = sb(cx, "sg", [P, L])
                rg = [sb(cx, f"rg{d}", [P, LT]) for d in range(2)]
                ig = [sb(cx, f"ig{d}", [P, LT]) for d in range(2)]
                th = [sb(cx, f"th{d}", [P, LT]) for d in range(2)]
                h = [sb(cx, f"h{d}", [P, LT]) for d in range(2)]
                pb = ps(cx, "pb", [P, 8, CH])
                w_land = [sem("lru_w0"), sem("lru_w1")]
                lvec_land, lru_mm, bank_read, xc_done, lru_dv, a_done, sq_ready, sq_done, ya_done, ya_out = [
                    sem(n) for n in ("lvec_land", "lru_mm", "bank_read", "xc_done", "lru_dv", "a_done", "sq_ready",
                                     "sq_done", "ya_done", "ya_out")]
                NCH = 29
                NV = 17
                with nc.Block() as block:
                    @block.sync
                    def _(sp_):
                        def load_vectors(t):
                            sp_.dma_start(lw[:, :, :], a["lru_gate"][t]).then_inc(lvec_land, 16)
                            sp_.dma_start(lv[:, :], a["lru_vec"][t]).then_inc(lvec_land, 16)

                        def store(t):
                            sp_.wait_ge(ya_done, t + 2)
                            sp_.dma_start(yg_dram[:, 0, :, bass.ds(t * CH, CH)].rearrange("q p c -> p q c"),
                                          sg[:, :].rearrange("p (q c) -> p q c", c=CH)).then_inc(ya_out, 16)
                        sp_.nop().then_inc(ya_out, 16)
                        for n in range(2):
                            sp_.dma_start(win[:, n, :], a["w_in"][(B_AIN, B_AGATE)[n]]).then_inc(w_land[n], 16)
                        load_vectors(0)
                        with sp_.Fori(0, NB - 1) as t:
                            sp_.wait_ge(lru_mm, NCH * t + 5 + 1)
                            sp_.dma_start(win[:, 0, :], a["w_in"][t + B_AIN + 1]).then_inc(w_land[0], 16)
                            sp_.wait_ge(lru_mm, NCH * t + 9 + 1)
                            sp_.dma_start(win[:, 1, :], a["w_in"][t + B_AGATE + 1]).then_inc(w_land[1], 16)
                            store(t)
                            load_vectors(t + 1)
                        store(NB - 1)
                        sp_.wait_ge(ya_out, 16 * NB + 16)

                    @block.tensor
                    def _(pe):
                        pe.nop().then_inc(lru_mm, 1)
                        with pe.Fori(0, NB) as t:
                            n = 0

                            def bank(width):
                                nonlocal n
                                pe.wait_ge(bank_read, NCH * t + n + 1)
                                n += 1
                                return pb[:, (n - 1) % 8, 0:width]
                            pe.wait_ge(w_land[0], 16 * t + 16)
                            for col, width in ALL_CHUNKS:
                                product(pe, bank(width), win[:, 0, :], col, width).then_inc(lru_mm, 1)
                            pe.wait_ge(w_land[1], 16 * t + 16)
                            for col, width in LAT_CHUNKS:
                                product(pe, bank(width), win[:, 1, :], col, width).then_inc(lru_mm, 1)
                            pe.wait_ge(lvec_land, 32 * t + 32)
                            pe.wait_ge(xc_done, t + 2)
                            for g in range(4):
                                for col, width in ALL_CHUNKS:
                                    pe.matmul(bank(width), lw[:, g, :], xc[:, col:col + width],
                                              start=True, stop=True).then_inc(lru_mm, 1)
                            pe.wait_ge(bank_read, NCH * t + NCH + 8)

                    @block.scalar
                    def _(act):
                        act.nop().then_inc(bank_read, 8)
                        with act.Fori(0, NB) as t:
                            n = 0
                            s = nc.scalar

                            def bank(width):
                                nonlocal n
                                act.wait_ge(lru_mm, NCH * t + n + 2)
                                n += 1
                                return pb[:, (n - 1) % 8, 0:width]
                            act.wait_ge(xc_done, t + 1)
                            for col, width in ALL_CHUNKS:
                                at = X0 if col == 0 else X1 + col - LC
                                s.copy(xin[:, at:at + width], bank(width)).then_inc(bank_read, 1)
                            act.wait_ge(ya_out, 16 * t + 16)
                            for col, width in LAT_CHUNKS:
                                s.activation(sg[:, col - LC:col - LC + width], bank(width), ACT.Silu).then_inc(bank_read, 1)
                            act.wait_ge(lvec_land, 32 * t + 32)
                            act.wait_ge(ya_done, t + 1)
                            for g in range(4):
                                d, which = g // 2, g % 2
                                dst = (rg, ig)[which][d]
                                for col, width in ALL_CHUNKS:
                                    s.activation(dst[:, col:col + width], bank(width), ACT.Sigmoid,
                                                 bias=lv[:, 5 + 2 * which + d:6 + 2 * which + d]).then_inc(bank_read, 1)
                            act.wait_ge(bank_read, NCH * t + NCH + 8)
                            for d in range(2):
                                s.activation(th[d][:, :], rg[d][:, :], ACT.Tanh,
                                             scale=decay[:, bass.ds(2 * t + d, 1), 1]).then_inc(a_done, 1)
                                act.wait_ge(a_done, 4 * t + 2 * d + 1)
                                s.activation(rg[d][:, :], rg[d][:, :], ACT.Exp,
                                             scale=decay[:, bass.ds(2 * t + d, 1), 0]).then_inc(a_done, 1)
                            for d in range(2):
                                act.wait_ge(sq_ready, 2 * t + d + 1)
                                s.activation(th[d][:, :], th[d][:, :], ACT.Sqrt).then_inc(sq_done, 1)

                    @block.vector
                    def _(dve):
                        v = nc.vector
                        dve.nop().then_inc(ya_done, 1)
                        v.memset(xin[:, :], 0.0).then_inc(xc_done, 1)
                        with dve.Fori(0, NB) as t:
                            st = Steps(dve, lru_dv, NV * t)
                            dve.wait_ge(lvec_land, 32 * t + 32)
                            dve.wait_ge(bank_read, NCH * t + 5 + 8)
                            dve.wait_ge(lru_mm, NCH * t + 1)
                            for first, at, width in ((X0, 0, LC), (X1, LC, L)):
                                o = xc[:, at:at + width]
                                for k in range(4):
                                    src = xin[:, first + k - 2:first + k - 2 + width]
                                    if k == 0:
                                        ins = v.tensor_scalar(o, src, lv[:, 0:1], lv[:, 4:5], ALU.mult, ALU.add)
                                    else:
                                        ins = v.scalar_tensor_tensor(o, src, lv[:, k:k + 1], o, ALU.mult, ALU.add)
                                    if k == 3 and at == LC:
                                        ins.then_inc(xc_done, 1)
                                        dve.wait_ge(xc_done, t + 2)
                                    else:
                                        st(ins)
                            for d in range(2):
                                if d == 0:
                                    dve.wait_ge(bank_read, NCH * t + NCH + 8)
                                st(v.tensor_tensor(ig[d][:, :], ig[d][:, :], xc[:, :], ALU.mult))
                                dve.wait_ge(a_done, 4 * t + 2 * d + 2)
                                st(v.tensor_tensor(h[d][:, :], rg[d][:, :], rg[d][:, :], ALU.mult))
                                v.scalar_tensor_tensor(th[d][:, :], h[d][:, :], 1.0, th[d][:, :], ALU.add, ALU.mult).then_inc(sq_ready, 1)
                            dve.wait_ge(sq_done, 2 * t + 1)
                            st(v.tensor_tensor(ig[0][:, :], ig[0][:, :], th[0][:, :], ALU.mult))
                            v.tensor_tensor_scan(h[0][:, :], rg[0][:, :], ig[0][:, :], 0.0, ALU.mult, ALU.add).then_inc(lru_dv, 1)
                            st.n += 1
                            dve.wait_ge(sq_done, 2 * t + 2)
                            dve.wait_ge(sq_ready, 2 * t + 2)
                            st(v.tensor_tensor(ig[1][:, :], ig[1][:, :], th[1][:, :], ALU.mult))
                            st(v.tensor_tensor_scan(h[1][:, LC - 1::-1], rg[1][:, LC - 1::-1], ig[1][:, LC - 1::-1],
                                                    0.0, ALU.mult, ALU.add))
                            lat = slice(LT - 1, LC - 1, -1)
                            ins = v.tensor_tensor_scan(h[1][:, lat], rg[1][:, lat], ig[1][:, lat],
                                                       h[1][:, 0:1], ALU.mult, ALU.add)
                            ins.then_inc(lru_dv, 1)
                            st.n += 1
                            dve.wait_ge(lru_dv, NV * t + 16)
                            st(v.tensor_tensor(h[0][:, LC:LT], h[0][:, LC:LT], h[1][:, LC:LT], ALU.add))
                            v.tensor_tensor(sg[:, :], sg[:, :], h[0][:, LC:LT], ALU.mult).then_inc(ya_done, 1)
                            assert st.n == NV, st.n

            with ExitStack() as cx:
                win = sb(cx, "win", [P, 2, D])
                wh = sb(cx, "wh", [P, 2, D], F32R)
                wl = sb(cx, "wl", [P, 2, D], F32R)
                uh = sb(cx, "uh", [P, KD, CH], F32R)
                ul = sb(cx, "ul", [P, KD, CH], F32R)
                qs = sb(cx, "qs", [P, L])
                kt = sb(cx, "kt", [P, LT])
                vt = sb(cx, "vt", [P, LT])
                NVB = LT // P + L // P - 1
                vk = sb(cx, "vk", [P, NVB, P])
                sg = sb(cx, "sg", [P, L])
                bt = sb(cx, "bt", [P, NDR * GW])
                qbd = sb(cx, "qbd", [P, 2, P])
                ss = sb(cx, "ss", [P, 2, BAND])
                pr = sb(cx, "pr", [P, 2, BAND + LC])
                prt = sb(cx, "prt", [P, 2, BAND + LC])
                on = sb(cx, "on", [P, 2, P])
                row_stat = sb(cx, "row_stat", [P, 2, 8])
                psc = [ps(cx, f"psc{s}", [P, 2, CH]) for s in range(2)]
                ppt = ps(cx, "ppt", [P, 2, CH])
                po = ps(cx, "po", [P, CH])
                pot = ps(cx, "pot", [P, CH])
                w_land = [sem(f"att_w{n}") for n in range(2)]
                uh_done, ul_done, wh_done, wl_done, u_used = [sem(n) for n in ("auh_done", "aul_done", "awh_done", "awl_done", "u_used")]
                (bt_land, att_mm, att_read, vk_mm, vk_read, qbd_done, s_mm, ss_done, nm_done, exp_done, att_dv, p_mm,
                 pt_read_dve, pt_read_act, pv_mm, on_done, ot_mm, yb_done, yb_out) = [sem(n) for n in (
                     "bt_land", "att_mm", "att_read", "vk_mm", "vk_read", "qbd_done", "s_mm", "ss_done", "nm_done", "exp_done",
                     "att_dv", "p_mm", "pt_read_dve", "pt_read_act", "pv_mm", "on_done", "ot_mm", "yb_done", "yb_out")]
                BLOCKS = (B_V, B_K, B_Q, B_BGATE)
                CHUNKS = ALL_CHUNKS + LAT_CHUNKS
                NS = len(CHUNKS)
                SWITCH = len(ALL_CHUNKS)
                NCH = 2 * NS
                NVG = (NVB + 3) // 4

                def split_ahead(t, g, split, split_weights):
                    if g < KD:
                        split(t, 0, g)
                    if g in (2, 5):
                        split_weights(t, g // 3)

                def band(r):
                    return min(max(r - NKH // 2, 0), ROWS - NKH)

                def v_block(r0, c):
                    return 2 + r0 // 2 + c if r0 % 2 == 0 else 2 + L // P + r0 // 2 + c

                def v_column(n):
                    return n * P if n < LT // P else LC + GW + (n - LT // P) * P
                with nc.Block() as block:
                    @block.sync
                    def _(sp_):
                        def store(t):
                            sp_.wait_ge(yb_done, ROWS * t + ROWS + 1)
                            sp_.dma_start(yg_dram[:, 1, :, bass.ds(t * CH, CH)].rearrange("q p c -> p q c"),
                                          sg[:, :].rearrange("p (q c) -> p q c", c=CH)).then_inc(yb_out, 16)
                        sp_.nop().then_inc(yb_out, 16)
                        for n in range(2):
                            sp_.dma_start(win[:, n, :], a["w_in"][BLOCKS[n]]).then_inc(w_land[n], 16)

                        def weights(t):
                            for n in range(2, 6):
                                sp_.wait_ge(wl_done, 4 * t + n)
                                sp_.dma_start(win[:, n % 2, :], a["w_in"][t + BLOCKS[n % 4] + n // 4]).then_inc(w_land[n % 2], 16)
                        sp_.dma_start(bt[:, :], bias_tab[0]).then_inc(bt_land, 16)
                        with sp_.Fori(0, NB - 1) as t:
                            weights(t)
                            store(t)
                            sp_.dma_start(bt[:, :], bias_tab[t + 1]).then_inc(bt_land, 16)
                        weights(NB - 1)
                        store(NB - 1)
                        sp_.wait_ge(yb_out, 16 * NB + 16)

                    @block.gpsimd
                    def _(pool):
                        nc.gpsimd.memset(qbd[:, :, :], 0.0).then_inc(qbd_done, 2)
                        pool.wait_ge(qbd_done, 2)
                        with pool.Fori(0, NB) as t:
                            pool.wait_ge(att_read, NCH * t + NCH - 1 + 4)
                            for r in range(ROWS):
                                pool.wait_ge(s_mm, ROWS * t + r + 1)
                                for h in range(2):
                                    x = slice(DH * h, DH * h + DH)
                                    pool.nop(nofuse=True)
                                    nc.gpsimd.tensor_copy(qbd[x, r % 2, x], qs[x, r * GW:(r + 1) * GW]).then_inc(qbd_done, 1)

                    @block.tensor
                    def _(pe):
                        pe.nop().then_inc(s_mm, 2)
                        pe.nop().then_inc(p_mm, 2)
                        pe.nop().then_inc(pv_mm, 2)
                        pe.nop().then_inc(ot_mm, 2)
                        pe.nop().then_inc(u_used, KD)
                        with pe.Fori(0, NB) as t:
                            for m, (col, width) in enumerate(CHUNKS):
                                for b in range(2):
                                    n = 2 * m + b
                                    if n < 4:
                                        pe.wait_ge(exp_done, 2 * ROWS * t + 4)
                                        pe.wait_ge(ss_done, ROWS * t + 2)
                                    pe.wait_ge(att_read, NCH * t + n + 1 if n >= 4 else NCH * t + 4)
                                    if m in (0, SWITCH):
                                        pe.wait_ge(wl_done, 4 * t + b + 2 + 2 * (m > 0))
                                    for k in range(KD):
                                        if b == 0:
                                            pe.wait_ge(ul_done, KD * NS * t + KD * m + k + 1)
                                        o, x = psc[n % 4 // 2][:, n % 2, 0:width], slice(k * P, (k + 1) * P)
                                        pe.matmul(o, wh[:, b, x], uh[:, k, 0:width], start=(k == 0), stop=False)
                                        pe.matmul(o, wh[:, b, x], ul[:, k, 0:width], start=False, stop=False)
                                        mm = pe.matmul(o, wl[:, b, x], uh[:, k, 0:width], start=False, stop=(k == KD - 1))
                                        if b:
                                            mm.then_inc(u_used, 1)
                                    if b == 0:
                                        mm.then_inc(att_mm, 1)
                            pe.wait_ge(pt_read_dve, ROWS * t + 1)
                            pe.wait_ge(pt_read_act, ROWS * t + 1)
                            pe.wait_ge(att_read, NCH * t + NCH + 4)
                            for g in range(NVG):
                                if g >= 2:
                                    pe.wait_ge(vk_read, NVG * t + g - 1)
                                for n in range(4 * g, min(4 * g + 4, NVB)):
                                    c = v_column(n)
                                    mm = pe.transpose(ppt[:, g % 2, (n % 4) * P:(n % 4 + 1) * P], vt[:, c:c + P], ident[:, :])
                                mm.then_inc(vk_mm, 1)

                            def scores(r):
                                i = ROWS * t + r
                                pe.wait_ge(qbd_done, 2 * i + 4)
                                pe.wait_ge(ss_done, i + 1)
                                pe.wait_ge(exp_done, 2 * i + 2)
                                c = LC + band(r) * GW
                                pe.matmul(psc[r % 2][:, 0, :], qbd[:, r % 2, :], kt[:, c:c + BAND], start=True, stop=True)
                                pe.matmul(psc[r % 2][:, 1, 0:LC], qbd[:, r % 2, :], kt[:, 0:LC], start=True, stop=True).then_inc(s_mm, 1)

                            def turn(r):
                                i = ROWS * t + r
                                pe.wait_ge(exp_done, 2 * i + 6)
                                pe.wait_ge(pt_read_dve, i + 1)
                                pe.wait_ge(pt_read_act, i + 1)
                                for c in range(6):
                                    mm = pe.transpose(ppt[:, c // 4, (c % 4) * P:(c % 4 + 1) * P],
                                                      pr[:, r % 2, c * P:(c + 1) * P], ident[:, :])
                                mm.then_inc(p_mm, 1)

                            def values(r):
                                i = ROWS * t + r
                                pe.wait_ge(pt_read_dve, i + 2)
                                pe.wait_ge(pt_read_act, i + 2)
                                pe.wait_ge(on_done, i + 1)
                                for c in range(6):
                                    b = v_block(band(r), c) if c < 4 else c - 4
                                    mm = pe.matmul(po[:, 0:P], prt[:, r % 2, c * P:(c + 1) * P], vk[:, b, :],
                                                   start=(c == 0), stop=(c == 5))
                                mm.then_inc(pv_mm, 1)

                            def turn_output(r):
                                i = ROWS * t + r
                                pe.wait_ge(on_done, i + 2)
                                pe.wait_ge(yb_done, i + 1)
                                pe.transpose(pot[:, 0:P], on[:, r % 2, :], ident[:, :]).then_inc(ot_mm, 1)
                            scores(0)
                            scores(1)
                            pe.wait_ge(vk_read, NVG * t + NVG)
                            for r in range(ROWS):
                                turn(r)
                                if r + 2 < ROWS:
                                    scores(r + 2)
                                values(r)
                                if r:
                                    turn_output(r - 1)
                            turn_output(ROWS - 1)

                    @block.scalar
                    def _(act):
                        s = nc.scalar
                        act.nop().then_inc(att_read, 4)
                        act.nop().then_inc(exp_done, 4)
                        act.nop().then_inc(pt_read_act, 1)

                        def split_weights(t, n):
                            act.wait_ge(w_land[n % 2], 32 * t + 16 * (n // 2) + 16)
                            s.copy(wh[:, n % 2, :], win[:, n % 2, :]).then_inc(wh_done, 1)

                        def split(t, m, k):
                            col, width = CHUNKS[m]
                            act.wait_ge(u_used, KD * NS * t + KD * m + k + 1)
                            s.copy(uh[:, k, 0:width], ut[:, k, col:col + width]).then_inc(uh_done, 1)

                        def read(t, m, b):
                            n, (col, width) = 2 * m + b, CHUNKS[m]
                            if b:
                                act.wait_ge(u_used, KD * NS * t + KD * m + 2 * KD)
                            else:
                                act.wait_ge(att_mm, NS * t + m + 1)
                            src = psc[n % 4 // 2][:, n % 2, 0:width]
                            if m < SWITCH:
                                ins = s.copy((vt, kt)[b][:, col:col + width], src)
                            elif b == 0:
                                ins = s.mul(qs[:, col - LC:col - LC + width], src, DH ** -0.5)
                            else:
                                if m == SWITCH:
                                    act.wait_ge(yb_out, 16 * t + 16)
                                ins = s.activation(sg[:, col - LC:col - LC + width], src, ACT.Silu)
                            ins.then_inc(att_read, 1)
                        for n in range(2):
                            split_weights(0, n)
                        for k in range(KD):
                            split(0, 0, k)
                        with act.Fori(0, NB) as t:
                            act.wait_ge(pv_mm, ROWS * t + 2)
                            act.wait_ge(s_mm, ROWS * t + 2)
                            for m in range(NS):
                                read(t, m, 0)
                                if m + 1 == SWITCH:
                                    split_weights(t, 2)
                                if m + 1 < NS:
                                    for k in range(KD):
                                        split(t, m + 1, k)
                                read(t, m, 1)
                                if m + 1 == SWITCH:
                                    split_weights(t, 3)
                            for g in range(NVG):
                                act.wait_ge(vk_mm, NVG * t + g + 1)
                                m = min(4, NVB - 4 * g)
                                s.copy(vk[:, 4 * g:4 * g + m, :], ppt[:, g % 2, 0:m * P].rearrange("p (a b) -> p a b", b=P)).then_inc(vk_read, 1)
                                split_ahead(t + 1, g, split, split_weights)

                            def exps(r):
                                i = ROWS * t + r
                                act.wait_ge(nm_done, i + 1)
                                act.wait_ge(p_mm, i + 1)
                                q = row_stat[:, r % 2, :]
                                s.activation(pr[:, r % 2, 0:BAND], ss[:, r % 2, :], ACT.Exp, bias=q[:, 2:3],
                                             accum_out=q[:, 3:4]).then_inc(exp_done, 1)
                                s.activation(pr[:, r % 2, BAND:BAND + LC], psc[r % 2][:, 1, 0:LC], ACT.Exp, bias=q[:, 2:3],
                                             accum_out=q[:, 4:5]).then_inc(exp_done, 1)
                            exps(0)
                            exps(1)
                            for r in range(ROWS):
                                i = ROWS * t + r
                                act.wait_ge(p_mm, i + 3)
                                act.wait_ge(pv_mm, i + 1)
                                s.copy(prt[:, r % 2, BAND:BAND + LC], ppt[:, 1, 0:LC]).then_inc(pt_read_act, 1)
                                if r + 2 < ROWS:
                                    exps(r + 2)

                    @block.vector
                    def _(dve):
                        v = nc.vector
                        dve.nop().then_inc(ss_done, 2)
                        dve.nop().then_inc(pt_read_dve, 1)
                        dve.nop().then_inc(on_done, 1)
                        dve.nop().then_inc(yb_done, 1)
                        NV = 3 * ROWS
                        dve.nop().then_inc(wl_done, 1)

                        def split_weights(t, n):
                            dve.wait_ge(wh_done, 4 * t + n + 1)
                            v.tensor_tensor(wl[:, n % 2, :], win[:, n % 2, :], wh[:, n % 2, :].bitcast(F32), ALU.subtract).then_inc(wl_done, 1)

                        def split(t, m, k):
                            col, width = CHUNKS[m]
                            dve.wait_ge(uh_done, KD * NS * t + KD * m + k + 1)
                            v.tensor_tensor(ul[:, k, 0:width], ut[:, k, col:col + width], uh[:, k, 0:width].bitcast(F32),
                                            ALU.subtract).then_inc(ul_done, 1)
                        for n in range(2):
                            split_weights(0, n)
                        for k in range(KD):
                            split(0, 0, k)
                        with dve.Fori(0, NB) as t:
                            for m in range(1, NS):
                                if m == SWITCH:
                                    split_weights(t, 2)
                                for k in range(KD):
                                    split(t, m, k)
                                if m == SWITCH:
                                    split_weights(t, 3)
                            for g in range(NVG):
                                split_ahead(t + 1, g, split, split_weights)
                            st = Steps(dve, att_dv, NV * t)

                            def maxima(r):
                                i = ROWS * t + r
                                q = row_stat[:, r % 2, :]
                                dve.wait_ge(s_mm, i + 3)
                                dve.wait_ge(exp_done, 2 * i + 2)
                                off = (band(r) - r + NKH - 1) * GW
                                dve.nop(nofuse=True)
                                v.tensor_tensor_reduce(ss[:, r % 2, :], psc[r % 2][:, 0, :], bt[:, off:off + BAND], 1.0,
                                                       -3e38, ALU.add, ALU.max, q[:, 0:1]).then_inc(ss_done, 1)
                                st(v.tensor_reduce(q[:, 1:2], psc[r % 2][:, 1, 0:LC], AX_X, ALU.max))
                                dve.wait_ge(ss_done, i + 3)
                                v.tensor_scalar(q[:, 2:3], q[:, 0:1], q[:, 1:2], -1.0, ALU.max, ALU.mult).then_inc(nm_done, 1)

                            def gated(r):
                                i = ROWS * t + r
                                dve.wait_ge(ot_mm, i + 3)
                                for h in range(2):
                                    x = slice(DH * h, DH * h + DH)
                                    o = sg[x, r * GW:(r + 1) * GW]
                                    ins = v.tensor_tensor(o, pot[x, x], o, ALU.mult)
                                ins.then_inc(yb_done, 1)
                            dve.wait_ge(att_read, NCH * t + NCH + 4)
                            dve.wait_ge(bt_land, 16 * t + 16)
                            maxima(0)
                            maxima(1)
                            for r in range(ROWS):
                                i = ROWS * t + r
                                q = row_stat[:, r % 2, :]
                                dve.wait_ge(p_mm, i + 3)
                                dve.wait_ge(pv_mm, i + 1)
                                v.tensor_copy(prt[:, r % 2, 0:BAND], ppt[:, 0, :]).then_inc(pt_read_dve, 1)
                                dve.wait_ge(exp_done, 2 * i + 6)
                                st(v.tensor_tensor(q[:, 5:6], q[:, 3:4], q[:, 4:5], ALU.add))
                                st(v.reciprocal(q[:, 6:7], q[:, 5:6]))
                                if r + 2 < ROWS:
                                    maxima(r + 2)
                                dve.wait_ge(pv_mm, i + 3)
                                dve.wait_ge(ot_mm, i + 1)
                                v.tensor_scalar(on[:, r % 2, :], po[:, 0:P], q[:, 6:7], None, ALU.mult).then_inc(on_done, 1)
                                if r:
                                    gated(r - 1)
                            gated(ROWS - 1)
                            assert st.n == NV, st.n

            with ExitStack() as cx:
                win = sb(cx, "win", [P, 4, D])
                hv = sb(cx, "hv", [P, 13])
                pad = [sb(cx, f"pad{n}", [P, L + 2]) for n in range(3)]
                w = sb(cx, "w", [P, L])
                x0c = pad[1][:, 0:L]
                sg = sb(cx, "sg", [P, L])
                wt = sb(cx, "wt", [P, 16, P])
                flat = wt[:, :, :].rearrange("p a b -> p (a b)")
                sent = sb(cx, "sent", [P, NPR, P])
                x1c = sent[:, 0:16, :].rearrange("p a b -> p (a b)")
                vc = sent[:, 16:32, :].rearrange("p a b -> p (a b)")
                got = sb(cx, "got", [P, NPR, P])
                spec = sb(cx, "spec", [P, 2, 2, 4 * P])
                tabf = sb(cx, "tabf", [P, 2, 4, P])
                tabi = sb(cx, "tabi", [P, 2, 4, 2 * P])
                prd = sb(cx, "prd", [P, 2, 2, 4, P])
                d1 = sb(cx, "d1", [P, P])
                d1i = sb(cx, "d1i", [P, R1])
                pb = ps(cx, "pb", [P, 4, CH])
                pf = ps(cx, "pf", [P, 4, CH])
                w_land = [sem(f"hy_w{n}") for n in range(4)]
                tabf_land, spec_land, tabi_land = [[sem(f"{n}{s}") for s in range(2)] for n in ("tabf_land", "spec_land", "tabi_land")]
                (hd_land, hv_land, hy_mm, hy_read, hy_dv, w_done, wt_mm, wt_read, s1_mm, s1_act, s1_dve, x1_out, x2_land, s2_mm, prd_done,
                 g_mm, g_read, inv_out, vf_land, fin_mm, fin_done, yc_done, yc_out) = [sem(n) for n in (
                     "hd_land", "hv_land", "hy_mm", "hy_read", "hy_dv", "w_done", "wt_mm", "wt_read", "s1_mm", "s1_act", "s1_dve", "x1_out",
                     "x2_land", "s2_mm", "prd_done", "g_mm", "g_read", "inv_out", "vf_land", "fin_mm", "fin_done", "yc_done", "yc_out")]
                BLOCKS = (B_HV, B_X1, B_X0, B_CGATE)
                C_W, C_FWD = 10, 13
                NG = NPR // 4
                HV, HV_PAD = 11, 7
                with nc.Block() as block:
                    @block.sync
                    def _(sp_):
                        sp_.nop().then_inc(yc_out, 16)
                        sp_.nop().then_inc(inv_out, 64)
                        sp_.dma_start(d1[:, :], a["dft1"]).then_inc(hd_land, 16)
                        sp_.dma_start(d1i[:, :], a["idft1"]).then_inc(hd_land, 16)
                        for n in range(4):
                            sp_.dma_start(win[:, n, :], a["w_in"][BLOCKS[n]]).then_inc(w_land[n], 16)
                        sp_.dma_start(hv[:, :], a["hy_vec"][0]).then_inc(hv_land, 16)

                        def turn_forward(t):
                            sp_.wait_ge(s1_act, 4 * t + 4)
                            sp_.wait_ge(s1_dve, 4 * t + 4)
                            for b in range(4):
                                o = 2 * (b % 2) + b // 2
                                dst = fwd_mid[t][32 * o:32 * o + 32].rearrange("q k c -> k q c")
                                sp_.dma_start(dst, sent[32 * b:32 * b + 32, :, :]).then_inc(x1_out, 16)
                            sp_.wait_ge(x1_out, 64 * t + 64)
                            sp_.dma_start(got[:, :, :], fwd_mid[t]).then_inc(x2_land, 16)

                        def tables(t, g):
                            sp_.dma_start(tabf[:, g % 2, :, :].rearrange("p k c -> p (k c)"), a["dft2"][g]).then_inc(tabf_land[g % 2], 16)

                        def spectrum(t, g):
                            first = P if g == 0 else 0
                            for r in range(2):
                                sp_.dma_start(spec[R1 * r:R1 * r + R1, g % 2, :, first:],
                                              filt_spec[t, g].rearrange("b q c -> q b c")[:, :, first:]).then_inc(spec_land[g % 2], 16)
                            if g == 0:
                                sp_.dma_start(spec[:, 0, :, 0:P], filt_spec0[t]).then_inc(spec_land[0], 16)

                        def inverse_tables(t, g):
                            sp_.dma_start(tabi[:, g % 2, :, :].rearrange("p k c -> p (k c)"), a["idft2"][g]).then_inc(tabi_land[g % 2], 16)

                        def next_groups(t, last):
                            for g in range(NG):
                                if g + 2 >= NG and last:
                                    break
                                ahead = (t, g + 2) if g + 2 < NG else (t + 1, g + 2 - NG)
                                for left, count, load in ((s2_mm, 1, tables), (prd_done, 1, spectrum), (g_mm, 3, inverse_tables)):
                                    sp_.wait_ge(left, NG * t + g + count)
                                    load(*ahead)

                        def turn_back(t):
                            sp_.wait_ge(g_read, NG * t + NG)
                            for b in range(4):
                                o = 2 * (b % 2) + b // 2
                                dst = inv_mid[t][32 * o:32 * o + 32].rearrange("k q c -> q k c")
                                sp_.dma_start(dst, sent[32 * b:32 * b + 32, :, :]).then_inc(inv_out, 16)
                            sp_.wait_ge(inv_out, 64 * t + 128)
                            sp_.dma_start(got[:, :, :], inv_mid[t]).then_inc(vf_land, 16)

                        def store(t):
                            sp_.wait_ge(yc_done, t + 2)
                            sp_.dma_start(yg_dram[:, 2, :, bass.ds(t * CH, CH)].rearrange("q p c -> p q c"),
                                          sg[:, :].rearrange("p (q c) -> p q c", c=CH)).then_inc(yc_out, 16)
                        for g in range(2):
                            for load in (tables, spectrum, inverse_tables):
                                load(0, g)
                        with sp_.Fori(0, NB - 1) as t:
                            for n, step in ((0, None), (1, turn_forward), (2, turn_back), (3, store)):
                                sp_.wait_ge(hy_mm, 16 * t + 4 * n + 4)
                                sp_.dma_start(win[:, n, :], a["w_in"][t + BLOCKS[n] + 1]).then_inc(w_land[n], 16)
                                if n == 2:
                                    next_groups(t, False)
                                if step:
                                    step(t)
                            sp_.dma_start(hv[:, :], a["hy_vec"][t + 1]).then_inc(hv_land, 16)
                        turn_forward(NB - 1)
                        next_groups(NB - 1, True)
                        turn_back(NB - 1)
                        store(NB - 1)
                        sp_.wait_ge(yc_out, 16 * NB + 16)

                    @block.tensor
                    def _(pe):
                        pe.nop().then_inc(g_mm, 2)
                        pe.wait_ge(hd_land, 32)
                        with pe.Fori(0, NB) as t:
                            def chunks(first, end):
                                for n in range(first, end):
                                    if n % 4 == 0:
                                        pe.wait_ge(w_land[n // 4], 16 * t + 16)
                                    pe.wait_ge(hy_read, 16 * t + n + 1)
                                    product(pe, pb[:, n % 4, :], win[:, n // 4, :], *LAT_CHUNKS[n % 4]).then_inc(hy_mm, 1)
                            chunks(0, C_W)
                            pe.wait_ge(w_done, t + 2)
                            pe.wait_ge(fin_done, 4 * t + 4)
                            for g in range(16):
                                mm = pe.transpose(pf[:, g // 4, (g % 4) * P:(g % 4 + 1) * P], w[:, g * P:(g + 1) * P], ident[:, :])
                                if g % 4 == 3:
                                    mm.then_inc(wt_mm, 1)
                            pe.wait_ge(wt_read, 4 * t + 4)
                            for q in range(4):
                                if q >= 2:
                                    pe.wait_ge(s1_act, 4 * t + q - 1)
                                    pe.wait_ge(s1_dve, 4 * t + q - 1)
                                for j in range(2):
                                    for g in range(4):
                                        x = slice(R1 * j, R1 * j + R1)
                                        mm = pe.matmul(pf[:, 2 * (q % 2) + j, g * P:(g + 1) * P], d1[x, :], wt[x, 4 * q + g, :],
                                                       start=True, stop=True)
                                mm.then_inc(s1_mm, 1)

                            def forward(g):
                                pe.wait_ge(tabf_land[g % 2], 16 * (NG // 2) * t + 16 * (g // 2) + 16)
                                if g >= 2:
                                    pe.wait_ge(prd_done, NG * t + g - 1)
                                for k in range(4):
                                    mm = pe.matmul(pf[:, g % 2, k * P:(k + 1) * P], tabf[:, g % 2, k, :], got[:, 4 * g + k, :],
                                                   start=True, stop=True)
                                mm.then_inc(s2_mm, 1)

                            def inverse(g):
                                pe.wait_ge(prd_done, NG * t + g + 1)
                                pe.wait_ge(tabi_land[g % 2], 16 * (NG // 2) * t + 16 * (g // 2) + 16)
                                if g >= 2:
                                    pe.wait_ge(g_read, NG * t + g - 1)
                                for k in range(4):
                                    o = pf[:, 2 + g % 2, k * P:(k + 1) * P]
                                    pe.matmul(o, tabi[:, g % 2, k, 0:P], prd[:, g % 2, 0, k, :], start=True, stop=False)
                                    mm = pe.matmul(o, tabi[:, g % 2, k, P:2 * P], prd[:, g % 2, 1, k, :], start=False, stop=True)
                                mm.then_inc(g_mm, 1)
                            chunks(C_W, C_FWD)
                            pe.wait_ge(s1_act, 4 * t + 4)
                            pe.wait_ge(s1_dve, 4 * t + 4)
                            pe.wait_ge(x2_land, 16 * t + 16)
                            forward(0)
                            for g in range(NG):
                                if g + 1 < NG:
                                    forward(g + 1)
                                inverse(g)
                            chunks(C_FWD, 16)
                            pe.wait_ge(g_read, NG * t + NG)
                            pe.wait_ge(vf_land, 16 * t + 16)
                            for q in range(NPR):
                                mm = pe.matmul(pf[:, q // 8, (q % 8) * R1:(q % 8 + 1) * R1], got[:, q, :], d1i[:, :], start=True, stop=True)
                                if q % 8 == 7:
                                    mm.then_inc(fin_mm, 1)

                    @block.scalar
                    def _(act):
                        s = nc.scalar
                        act.nop().then_inc(hy_read, 4)
                        with act.Fori(0, NB) as t:
                            act.wait_ge(w_done, t + 1)

                            def chunks(first, end):
                                for n in range(first, end):
                                    act.wait_ge(hy_mm, 16 * t + n + 1)
                                    c = n % 4 * CH
                                    if n == 4:
                                        act.wait_ge(yc_done, t + 1)
                                    if n == 8:
                                        act.wait_ge(hy_dv, HV * t + HV_PAD - 2)
                                    if n == 12:
                                        act.wait_ge(yc_out, 16 * t + 16)
                                    if n < 12:
                                        ins = s.copy(pad[n // 4][:, 1 + c:1 + c + CH], pb[:, n % 4, :])
                                    else:
                                        ins = s.activation(sg[:, c:c + CH], pb[:, n % 4, :], ACT.Silu)
                                    ins.then_inc(hy_read, 1)
                            chunks(0, C_W)
                            for g in range(4):
                                act.wait_ge(wt_mm, 4 * t + g + 1)
                                s.copy(wt[:, 4 * g:4 * g + 4, :], pf[:, g, :].rearrange("p (a b) -> p a b", b=P)).then_inc(wt_read, 1)
                            act.wait_ge(inv_out, 64 * t + 64)
                            pairs = sent[:, :, :].rearrange("p (g j) c -> p g j c", j=2)
                            for q in range(4):
                                act.wait_ge(s1_mm, 4 * t + q + 1)
                                s.copy(pairs[:, 4 * q:4 * q + 4, 0, :], pf[:, 2 * (q % 2), :].rearrange("p (a b) -> p a b", b=P)).then_inc(s1_act, 1)
                            chunks(C_W, C_FWD)
                            act.wait_ge(x1_out, 64 * t + 64)
                            for g in range(NG):
                                act.wait_ge(g_mm, NG * t + g + 3)
                                s.copy(sent[:, 4 * g:4 * g + 4, :], pf[:, 2 + g % 2, :].rearrange("p (a b) -> p a b", b=P)).then_inc(g_read, 1)
                            chunks(C_FWD, 16)

                    @block.vector
                    def _(dve):
                        v = nc.vector
                        dve.nop().then_inc(yc_done, 1)
                        dve.nop().then_inc(w_done, 1)
                        dve.nop().then_inc(fin_done, 4)
                        for n in range(3):
                            v.memset(pad[n][:, 0:1], 0.0).then_inc(hy_dv, 1)
                            v.memset(pad[n][:, L + 1:L + 2], 0.0).then_inc(hy_dv, 1)
                        v.memset(w[:, 0:1], 0.0).then_inc(hy_dv, 1)
                        dve.wait_ge(hy_dv, HV_PAD)
                        with dve.Fori(0, NB) as t:
                            st = Steps(dve, hy_dv, HV * t + 7)
                            dve.wait_ge(hv_land, 16 * t + 16)

                            def conv3(dst, src, taps, bias):
                                st(v.tensor_scalar(dst, src[:, 0:L], hv[:, taps:taps + 1], hv[:, bias:bias + 1], ALU.mult, ALU.add))
                                for k in (1, 2):
                                    st(v.scalar_tensor_tensor(dst, src[:, k:k + L], hv[:, taps + k:taps + k + 1], dst, ALU.mult, ALU.add))
                            dve.wait_ge(hy_read, 16 * t + 4 + 4)
                            dve.wait_ge(inv_out, 64 * t + 64)
                            conv3(vc, pad[0], 6, 11)
                            dve.wait_ge(hy_read, 16 * t + 8 + 4)
                            conv3(x1c, pad[1], 3, 10)
                            v.tensor_tensor(w[:, :].rearrange("p (n2 n1) -> p n1 n2", n2=R1), x1c.rearrange("p (n1 n2) -> p n1 n2", n2=R1),
                                            vc.rearrange("p (n1 n2) -> p n1 n2", n2=R1), ALU.mult).then_inc(w_done, 1)
                            pairs = sent[:, :, :].rearrange("p (g j) c -> p g j c", j=2)
                            for q in range(4):
                                dve.wait_ge(s1_mm, 4 * t + q + 1)
                                v.tensor_copy(pairs[:, 4 * q:4 * q + 4, 1, :], pf[:, 2 * (q % 2) + 1, :].rearrange("p (a b) -> p a b", b=P)).then_inc(s1_dve, 1)
                            for g in range(NG):
                                dve.wait_ge(s2_mm, NG * t + g + 1)
                                dve.wait_ge(g_mm, NG * t + g + 1)
                                if g % 2 == 0:
                                    dve.wait_ge(spec_land[0], (16 + 16 * NG) * t + 32 * (g // 2) + 48)
                                else:
                                    dve.wait_ge(spec_land[1], 16 * NG * t + 32 * (g // 2) + 32)
                                x = pf[:, g % 2, :].rearrange("p (a b) -> p a b", b=P)
                                for b in range(2):
                                    ins = v.tensor_tensor(prd[:, g % 2, b, :, :], x, spec[:, g % 2, b, :].rearrange("p (a b) -> p a b", b=P), ALU.mult)
                                ins.then_inc(prd_done, 1)
                                if g == NG - 1:
                                    conv3(x0c, pad[2], 0, 9)
                            dve.wait_ge(w_done, t + 2)
                            for q in range(4):
                                dve.wait_ge(fin_mm, 4 * t + q + 1)
                                y = flat.rearrange("p (n1 n2) -> p n2 n1", n2=R1)[:, 16 * q:16 * q + 16, :]
                                wv = w[:, CH * q:CH * q + CH].rearrange("p (n2 n1) -> p n2 n1", n1=32)
                                v.scalar_tensor_tensor(y, wv, hv[:, 12:13], pf[:, q, :].rearrange("p (a b) -> p a b", b=32),
                                                       ALU.mult, ALU.add).then_inc(fin_done, 1)
                            dve.wait_ge(fin_done, 4 * t + 8)
                            st(v.tensor_tensor(flat, flat, x0c, ALU.mult))
                            st(v.memset(pad[1][:, 0:1], 0.0))
                            dve.wait_ge(hy_read, 16 * t + 16 + 4)
                            v.tensor_tensor(sg[:, :], sg[:, :], flat, ALU.mult).then_inc(yc_done, 1)
                            assert st.n == HV, st.n

            with ExitStack() as cx:
                WM = 12 * P
                uh = sb(cx, "uh", [P, KD, CH], F32R)
                ul = sb(cx, "ul", [P, KD, CH], F32R)
                yh = sb(cx, "yh", [P, 3, NB, CH], F32R)
                yl = sb(cx, "yl", [P, 3, NB, CH], F32R)
                w = sb(cx, "w", [P, 2, WM])
                wh = sb(cx, "wh", [P, 2, WM], F32R)
                wl = sb(cx, "wl", [P, 2, WM], F32R)
                sig = sb(cx, "sig", [P, 2, CH])
                m = sb(cx, "m", [P, 2, CH])
                yraw = [ut[:, 4 * h:4 * h + 4, 0:LC] for h in range(2)]
                pg = ps(cx, "pg", [P, 3, CH])
                pr_ = ps(cx, "pr", [P, 3, CH])
                w_land = [sem(f"mg_w{n}") for n in range(2)]
                y_land = [sem("y_land0"), sem("y_land1")]
                (uh_done, ul_done, yh_done, yl_done, wh_done, wl_done, mg_mm, br_mm, sig_done, br_read, mg_dv,
                 m_out, m_free) = [sem(n) for n in (
                     "uh_done", "ul_done", "yh_done", "yl_done", "wh_done", "wl_done", "mg_mm", "br_mm", "sig_done", "br_read",
                     "mg_dv", "m_out", "m_free")]
                NU = 3 * KD

                def f32(t):
                    return t.bitcast(F32)

                def half(t, b, h):
                    return t[:, b, 2 * h:2 * h + 2, :].rearrange("p k (a c) -> p (k a) c", c=LC)
                with nc.Block() as block:
                    @block.sync
                    def _(sp_):
                        sp_.dma_start(w[:, 0, :], a["w_merge"][0]).then_inc(w_land[0], 16)
                        with sp_.Fori(0, NQ) as c:
                            for b in range(3):
                                sp_.wait_ge(wl_done, NU * c + b + 1)
                                sp_.dma_start(w[:, (b + 1) % 2, :], a["w_merge"][b + 1]).then_inc(w_land[(b + 1) % 2], 16)
                                for h in range(2):
                                    sp_.wait_ge(yl_done, 6 * c + 2 * b + h + 1)
                                    sp_.dma_start(yraw[h], yg_dram[c, b].rearrange("p (h a c) -> p h a c", h=2, c=LC)[:, h]).then_inc(y_land[h], 16)
                            for e in range(3, 6):
                                sp_.wait_ge(wl_done, NU * c + e + 1)
                                sp_.dma_start(w[:, (e + 1) % 2, :], a["w_merge"][e + 1]).then_inc(w_land[(e + 1) % 2], 16)
                            with sp_.Fori(1, KD // 2) as i:
                                for e in range(6):
                                    sp_.wait_ge(wl_done, NU * c + 6 * i + e + 1)
                                    sp_.dma_start(w[:, (e + 1) % 2, :], a["w_merge"][6 * i + e + 1]).then_inc(w_land[(e + 1) % 2], 16)

                    @block.tensor
                    def _(pe):
                        def three(bank, wcol, xh, xl, first, last):
                            (wa, wb), cols = wcol
                            pe.matmul(bank, wa[:, cols], xh, start=first, stop=False)
                            pe.matmul(bank, wa[:, cols], xl, start=False, stop=False)
                            return pe.matmul(bank, wb[:, cols], xh, start=False, stop=last)
                        pe.nop().then_inc(mg_mm, 1)
                        pe.nop().then_inc(br_mm, 1)
                        with pe.Fori(0, NQ) as c:
                            with pe.Fori(0, KD // 2) as i:
                                for e in range(6):
                                    n, b = NU * c + 6 * i + e, e % 3
                                    weights = (wh[:, e % 2, :], wl[:, e % 2, :])
                                    pe.wait_ge(wl_done, n + 2)
                                    pe.wait_ge(sig_done, n + 1)
                                    for k in range(KD):
                                        if e == 0:
                                            pe.wait_ge(ul_done, KD * c + k + 1)
                                        mm = three(pg[:, b, :], (weights, slice(k * P, (k + 1) * P)), uh[:, k, :], ul[:, k, :],
                                                   k == 0, k == KD - 1)
                                    mm.then_inc(mg_mm, 1)
                                    pe.wait_ge(br_read, n + 1)
                                    for k in range(NB):
                                        if e < 3 and k % 2 == 0:
                                            pe.wait_ge(yl_done, 6 * c + 2 * b + k // 2 + 3)
                                        mm = three(pr_[:, b, :], (weights, slice(D + k * P, D + (k + 1) * P)), yh[:, b, k, :], yl[:, b, k, :],
                                                   k == 0, k == NB - 1)
                                    mm.then_inc(br_mm, 1)

                    @block.scalar
                    def _(act):
                        act.nop().then_inc(sig_done, 3)
                        act.wait_ge(w_land[0], 16)
                        nc.scalar.copy(wh[:, 0, :], w[:, 0, :]).then_inc(wh_done, 1)

                        def gate(c, i, e):
                            n = NU * c + 6 * i + e
                            act.wait_ge(w_land[(e + 1) % 2], 16 * (NU // 2) * c + 48 * i + 16 * ((e + 1) // 2) + 16)
                            act.wait_ge(br_mm, n + 1)
                            nc.scalar.copy(wh[:, (e + 1) % 2, :], w[:, (e + 1) % 2, :]).then_inc(wh_done, 1)
                            act.wait_ge(mg_mm, n + 2)
                            act.wait_ge(br_read, n + 2)
                            nc.scalar.activation(sig[:, e % 2, :], pg[:, e % 3, :], ACT.Sigmoid).then_inc(sig_done, 1)
                        with act.Fori(0, NQ) as c:
                            act.wait_ge(mg_mm, NU * c + 1)
                            for k in range(KD):
                                nc.scalar.copy(uh[:, k, :], ut[:, k, bass.ds(c * CH + LC, CH)]).then_inc(uh_done, 1)
                            act.wait_ge(br_mm, NU * c + 1)
                            for b in range(3):
                                for h in range(2):
                                    act.wait_ge(y_land[h], 48 * c + 16 * b + 16)
                                    nc.scalar.copy(half(yh, b, h), yraw[h]).then_inc(yh_done, 1)
                                if b < 2:
                                    gate(c, 0, b)
                            for e in range(2, 6):
                                gate(c, 0, e)
                            with act.Fori(1, KD // 2) as i:
                                for e in range(6):
                                    gate(c, i, e)

                    @block.vector
                    def _(dve):
                        v = nc.vector
                        dve.nop().then_inc(br_read, 3)
                        dve.nop().then_inc(wl_done, 1)
                        dve.nop().then_inc(yl_done, 2)
                        dve.wait_ge(wh_done, 1)
                        v.tensor_tensor(wl[:, 0, :], w[:, 0, :], f32(wh[:, 0, :]), ALU.subtract).then_inc(wl_done, 1)

                        def combine(c, i, e):
                            n, b, j = NU * c + 6 * i + e, e % 3, KD * c + 2 * i + e // 3
                            dve.wait_ge(wh_done, n + 2)
                            v.tensor_tensor(wl[:, (e + 1) % 2, :], w[:, (e + 1) % 2, :], f32(wh[:, (e + 1) % 2, :]), ALU.subtract).then_inc(wl_done, 1)
                            dve.wait_ge(sig_done, n + 4)
                            dve.wait_ge(br_mm, n + 2)
                            if b == 0:
                                dve.wait_ge(m_free, j + 1)
                                v.tensor_tensor(m[:, e // 3, :], sig[:, e % 2, :], pr_[:, b, :], ALU.mult).then_inc(br_read, 1)
                                return
                            v.tensor_tensor(sig[:, e % 2, :], sig[:, e % 2, :], pr_[:, b, :], ALU.mult).then_inc(mg_dv, 1)
                            dve.wait_ge(mg_dv, 2 * j + b)
                            dve.wait_ge(br_read, n + 3)
                            v.tensor_tensor(m[:, e // 3, :], m[:, e // 3, :], sig[:, e % 2, :], ALU.add).then_inc(br_read, 1)
                        with dve.Fori(0, NQ) as c:
                            for k in range(KD):
                                dve.wait_ge(uh_done, KD * c + k + 1)
                                v.tensor_tensor(ul[:, k, :], ut[:, k, bass.ds(c * CH + LC, CH)], f32(uh[:, k, :]), ALU.subtract).then_inc(ul_done, 1)
                            for b in range(3):
                                for h in range(2):
                                    dve.wait_ge(yh_done, 6 * c + 2 * b + h + 1)
                                    v.tensor_tensor(half(yl, b, h), yraw[h], f32(half(yh, b, h)), ALU.subtract).then_inc(yl_done, 1)
                                if b < 2:
                                    combine(c, 0, b)
                            for e in range(2, 6):
                                combine(c, 0, e)
                            with dve.Fori(1, KD // 2) as i:
                                for e in range(6):
                                    combine(c, i, e)

                    @block.gpsimd
                    def _(pool):
                        pool.nop().then_inc(m_free, 2)
                        with pool.Fori(0, NQ) as c:
                            with pool.Fori(0, KD // 2) as i:
                                for h in range(2):
                                    j = 2 * i + h
                                    pool.wait_ge(br_read, NU * c + 6 * i + 3 * h + 6)
                                    pool.nop(nofuse=True)
                                    pool.dma_start(m_dram[c][:, :, bass.ds(j, 1), :].rearrange("n p o c -> p n (o c)"),
                                                   m[:, h, :].rearrange("p (n c) -> p n c", c=P)).then_inc(m_out, 16)
                                    pool.wait_ge(m_out, 16 * KD * c + 16 * j + 16)
                                    pool.nop().then_inc(m_free, 1)

        with ExitStack() as cx:
            wo = sb(cx, "wo", [P, KD, D])
            woh = sb(cx, "woh", [P, KD, D], F32R)
            wol = sb(cx, "wol", [P, KD, D], F32R)
            mt = sb(cx, "mt", [P, 2, D])
            mth = sb(cx, "mth", [P, 2, D], F32R)
            mtl = sb(cx, "mtl", [P, 2, D], F32R)
            xin = sb(cx, "xin", [P, 2, D])
            h = sb(cx, "h", [P, 2, D])
            stat = sb(cx, "stat", [P, 2, 18])
            gb = sb(cx, "gb", [P, 2, D])
            pout = ps(cx, "pout", [P, 2, 2, CH])
            wo_land = [sem(f"wo_land{n}") for n in range(4)]
            gb_land = sem("gb_land")
            mt_land = [sem("mt_land0"), sem("mt_land1")]
            x_land = [sem("x_land0"), sem("x_land1")]
            woh_done, wol_done, mth_done, mtl_done, out_mm, o_read, h_done, y_done, biased = [sem(n) for n in (
                "woh_done", "wol_done", "mth_done", "mtl_done", "out_mm", "o_read", "h_done", "y_done", "biased")]
            stored = [sem("stored0"), sem("stored1")]
            assert NV_NORM == 5
            NT = L // P

            def pipelined(eng, split, finish):
                split(0, 0, 0)
                with eng.Fori(0, NT // 2 - 1) as i:
                    split(2 * i + 1, 1, i)
                    finish(2 * i, 0, i)
                    split(2 * i + 2, 0, i + 1)
                    finish(2 * i + 1, 1, i)
                split(NT - 1, 1, NT // 2 - 1)
                finish(NT - 2, 0, NT // 2 - 1)
                finish(NT - 1, 1, NT // 2 - 1)
            with nc.Block() as block:
                @block.sync
                def _(sp_):
                    for s in range(2):
                        sp_.nop().then_inc(stored[s], 16)
                    m_tiles = m_dram.rearrange("q n p k c -> (q n) p (k c)")
                    for s in range(2):
                        sp_.dma_start(mt[:, s, :], m_tiles[s]).then_inc(mt_land[s], 16)
                        for k in range(4 * s, 4 * s + 4):
                            sp_.dma_start(wo[:, k, :], a["w_out"][:, k, :]).then_inc(wo_land[k // 2], 16)
                    for s in range(2):
                        sp_.dma_start(xin[:, s, :], a["x"].rearrange("(n p) d -> n p d", p=P)[s]).then_inc(x_land[s], 16)
                    for n, name in enumerate(("ln_g", "ln_b")):
                        sp_.dma_start(gb[:, n, :], bass.AP(tensor=a[name].tensor, offset=0, ap=[[0, P], [1, D]])).then_inc(gb_land, 16)

                    def store(n, s):
                        sp_.wait_ge(biased, n + 1)
                        sp_.dma_start(out.rearrange("(n p) d -> n p d", p=P)[n], h[:, s, :]).then_inc(stored[s], 16)
                    with sp_.Fori(1, NT // 2) as i:
                        for s in range(2):
                            n = 2 * i + s
                            sp_.wait_ge(mtl_done, n - 1)
                            sp_.dma_start(mt[:, s, :], m_tiles[n]).then_inc(mt_land[s], 16)
                            sp_.wait_ge(h_done, n - 1)
                            sp_.dma_start(xin[:, s, :], a["x"].rearrange("(n p) d -> n p d", p=P)[n]).then_inc(x_land[s], 16)
                            store(n - 2, s)
                    for s in range(2):
                        store(NT - 2 + s, s)
                    for s in range(2):
                        sp_.wait_ge(stored[s], 16 * (NT // 2) + 16)

                @block.tensor
                def _(pe):
                    pe.nop().then_inc(out_mm, 2)
                    with pe.Fori(0, NT // 2) as i:
                        for s in range(2):
                            pe.wait_ge(mtl_done, 2 * i + s + 1)
                            pe.wait_ge(o_read, 2 * i + s + 1)
                            for k in range(KD):
                                if s == 0:
                                    pe.wait_ge(wol_done, k + 1)
                                x = slice(k * P, (k + 1) * P)
                                for half in range(2):
                                    c = slice(half * CH, (half + 1) * CH)
                                    o = pout[:, s, half, :]
                                    pe.matmul(o, mth[:, s, x], woh[:, k, c], start=(k == 0), stop=False)
                                    pe.matmul(o, mth[:, s, x], wol[:, k, c], start=False, stop=False)
                                    mm = pe.matmul(o, mtl[:, s, x], woh[:, k, c], start=False, stop=(k == KD - 1))
                            mm.then_inc(out_mm, 1)

                @block.vector
                def _(dve):
                    v = nc.vector
                    dve.nop().then_inc(o_read, 2)

                    def split(n, s, i):
                        dve.wait_ge(mth_done, n + 1)
                        v.tensor_tensor(mtl[:, s, :], mt[:, s, :], mth[:, s, :].bitcast(F32), ALU.subtract).then_inc(mtl_done, 1)
                        if isinstance(n, int) and n == 0:
                            for k in range(KD):
                                dve.wait_ge(woh_done, k + 1)
                                v.tensor_tensor(wol[:, k, :], wo[:, k, :], woh[:, k, :].bitcast(F32), ALU.subtract).then_inc(wol_done, 1)

                    def finish(n, s, i):
                        st = Steps(dve, norm_dv, NV_NORM * NTILE + 5 * n)
                        x, q = h[:, s, :], stat[:, s, :]
                        dve.wait_ge(out_mm, n + 3)
                        dve.wait_ge(stored[s], 16 * i + 16)
                        v.tensor_tensor(x, pout[:, s, :, :].rearrange("p a b -> p (a b)"), gate_row[:, :], ALU.mult).then_inc(o_read, 1)
                        dve.wait_ge(o_read, n + 3)
                        dve.wait_ge(x_land[s], 16 * i + 16)
                        v.scalar_tensor_tensor(x, xin[:, s, :], ALPHA, x, ALU.mult, ALU.add).then_inc(h_done, 1)
                        dve.wait_ge(h_done, n + 1)
                        st(v.bn_stats(q[:, 0:6], x[:, 0:512]))
                        st(v.bn_stats(q[:, 6:12], x[:, 512:1024]))
                        dve.nop(nofuse=True)
                        st(v.bn_aggr(q[:, 12:14], q[:, 0:12]))
                        v.tensor_scalar(q[:, 14:15], q[:, 13:14], EPS, None, ALU.add).then_inc(var_done, 1)
                        dve.wait_ge(std_done, NTILE + n + 1)
                        st(v.reciprocal(q[:, 16:17], q[:, 15:16]))
                        dve.wait_ge(gb_land, 32)
                        st(v.tensor_scalar(x, x, q[:, 12:13], q[:, 16:17], ALU.subtract, ALU.mult))
                        v.tensor_tensor(x, x, gb[:, 0, :], ALU.mult).then_inc(y_done, 1)
                    pipelined(dve, split, finish)

                @block.scalar
                def _(act):
                    def split(n, s, i):
                        act.wait_ge(mt_land[s], 16 * i + 16)
                        act.wait_ge(out_mm, n + 1)
                        nc.scalar.copy(mth[:, s, :], mt[:, s, :]).then_inc(mth_done, 1)
                        if isinstance(n, int) and n == 0:
                            for k in range(KD):
                                act.wait_ge(wo_land[k // 2], 32)
                                nc.scalar.copy(woh[:, k, :], wo[:, k, :]).then_inc(woh_done, 1)

                    def finish(n, s, i):
                        act.wait_ge(var_done, NTILE + n + 1)
                        nc.scalar.activation(stat[:, s, 15:16], stat[:, s, 14:15], ACT.Sqrt).then_inc(std_done, 1)
                    pipelined(act, split, finish)

                @block.gpsimd
                def _(pool):
                    pool.wait_ge(gb_land, 32)
                    with pool.Fori(0, NT // 2) as i:
                        for s in range(2):
                            n = 2 * i + s
                            pool.wait_ge(y_done, n + 1)
                            nc.gpsimd.tensor_tensor(h[:, s, :], h[:, s, :], gb[:, 1, :], ALU.add).then_inc(biased, 1)


def lay_out(x, c, ctx, c_ctx, w_mod, b_mod, w_in, lru_conv_w, lru_conv_b, lru_w_a, lru_b_a, lru_w_x, lru_b_x,
            lru_lambda, na_rpb, hy_conv_w, hy_conv_b, hy_w1, hy_b1, hy_freq1, hy_w2, hy_b2, hy_freq2, hy_w3,
            hy_d_skip, w_branch_out, w_out, ln_g, ln_b):
    def tiles(v):
        return v.reshape(-1, P).T

    def twice(v):
        return np.concatenate([v, v], -1)
    o = {"x": x[0], "ctx": ctx[0]}
    o["cvec"] = np.stack([tiles(c[0]), tiles(c_ctx)], -1)
    o["w_mod"] = w_mod[0].reshape(2, KD // 2, P, 6, CH).transpose(3, 0, 2, 1, 4).reshape(12, P, KD // 2 * CH)
    o["bmod"] = np.stack([tiles(b_mod[0])] * 2, -1)
    blocks = w_in[0].reshape(KD, P, 64, P).transpose(2, 1, 0, 3).reshape(64, P, D)
    o["w_in"] = blocks[:B_G]
    o["lam"] = lru_lambda[0].reshape(2, NB, P).transpose(2, 1, 0).reshape(P, 2 * NB)
    rpb = np.zeros((HEADS, NDR, TOE), np.float32)
    rpb[:, :, GW - NKW:GW + NKW - 1] = na_rpb[0]
    o["rpb"] = rpb
    o["lru_vec"] = np.stack([*lru_conv_w[0].reshape(4, NB, P), lru_conv_b[0].reshape(NB, P),
                             *lru_b_a[0].reshape(2, NB, P), *lru_b_x[0].reshape(2, NB, P)], -1)
    gate = np.zeros((NB, P, 4, P), np.float32)
    for d in range(2):
        for n, w in enumerate((lru_w_a, lru_w_x)):
            for b in range(8):
                r = slice(64 * (b % 2), 64 * (b % 2) + 64)
                gate[b // 2, r, 2 * d + n, r] = w[0, d, b]
    o["lru_gate"] = gate
    cw = hy_conv_w[0].reshape(3, 3, NB, P)
    cb = hy_conv_b[0].reshape(3, NB, P)
    o["hy_vec"] = np.stack([cw[k, part] for part in range(3) for k in range(3)] + [cb[0], cb[1], cb[2],
                           hy_d_skip[0].reshape(NB, P)], -1)
    o["hy_w1"] = twice(hy_w1[0])
    o["hy_w2"] = twice(hy_w2[0])
    o["hy_bf"] = np.stack([twice(v[0]) for v in (hy_b1, hy_freq1, hy_b2, hy_freq2)], -1)
    o["hy_w3"] = np.concatenate([hy_w3[0][:, :512], hy_w3[0][:, 512:]], 0)
    branch = w_branch_out[0].reshape(3, NB, P, KD, P).transpose(3, 0, 2, 1, 4).reshape(KD, 3, P, NB * P)
    gates = blocks[B_G:].reshape(3, KD, P, D).transpose(1, 0, 2, 3)
    units = np.concatenate([gates, branch], -1).reshape(3 * KD, P, D + NB * P)
    o["w_merge"] = np.concatenate([units, units[:1]], 0)
    o["w_out"] = w_out[0].reshape(KD, P, D).transpose(1, 0, 2)
    o["ln_g"], o["ln_b"] = ln_g, ln_b
    return {k: np.ascontiguousarray(v) for k, v in o.items()}


def kernel(**inputs):
    import concourse.bacc as _bacc
    from concourse.bass_utils import run_bass_kernel_spmd as _run

    arrays = lay_out(**{k: np.asarray(v) for k, v in inputs.items()})
    arrays.update(shape_constants())
    nc = _bacc.Bacc("TRN2", target_bir_lowering=False, num_devices=1)
    aps = {n: nc.dram_tensor(f"in_{n}", v.shape, F32, kind="ExternalInput").ap() for n, v in arrays.items()}
    out = nc.dram_tensor("out_0", (L, D), F32, kind="ExternalOutput").ap()
    build_trunk(nc, aps, out)
    r = _run(nc, [{f"in_{n}": v for n, v in arrays.items()}], core_ids=[0])
    return r.results[0]["out_0"].reshape(1, L, D)
```
